# Optimizing a Trainium2 kernel written in Bass

```python
import math
import jax, jax.numpy as jnp
from jax import lax
import numpy as np

D_MODEL = 2048
BATCH = 1
SEQ = 256
DEPTH = 2

GRID_W = 64
CTX_LEN = 256
N_MIXERS = 2
N_ATTN = (DEPTH + N_MIXERS - 1) // N_MIXERS
N_CONV = DEPTH // N_MIXERS
DIFF_HEADS = 8
HEAD_DIM = 128
V_HEAD_DIM = 2 * HEAD_DIM
QK_WIDTH = DIFF_HEADS * 2 * HEAD_DIM
V_WIDTH = DIFF_HEADS * V_HEAD_DIM
QKV_WIDTH = 2 * QK_WIDTH + V_WIDTH
ROPE_THETA = 10000.0
Q_BLOCK = 128
CONV_W = 3
D_FF = 5632
N_MOD = 6
EPS = 1e-6

kernel_name = "hybrid_diffattn_shortconv_dit_trunk"

def rmsnorm(x, gain=None):
    xf = x.astype(jnp.float32)
    y = (xf * lax.rsqrt(jnp.mean(xf * xf, axis=-1, keepdims=True) + EPS)).astype(x.dtype)
    return y if gain is None else y * gain

def adaln(cond, w_ada, b_ada):
    mod = jax.nn.silu(cond) @ w_ada + b_ada
    return jnp.split(mod, N_MOD, axis=-1)

def modulate(h, shift, scale):
    return h * (1.0 + scale) + shift

def dwconv3(x, w):
    xp = jnp.pad(x, ((0, 0), (1, 1), (0, 0)))
    return xp[:, :-2] * w[0] + xp[:, 1:-1] * w[1] + xp[:, 2:] * w[2]

def axial_rope_tables(n_tokens):
    rows = n_tokens // GRID_W
    row = jnp.repeat(jnp.arange(rows, dtype=jnp.float32), GRID_W)
    col = jnp.tile(jnp.arange(GRID_W, dtype=jnp.float32), rows)
    half = HEAD_DIM // 2
    inv_freq = 1.0 / (ROPE_THETA ** (jnp.arange(0, half, 2, dtype=jnp.float32) / half))
    ang_r = row[:, None] * inv_freq
    ang_c = col[:, None] * inv_freq
    return (jnp.cos(ang_r), jnp.sin(ang_r), jnp.cos(ang_c), jnp.sin(ang_c))

def _rot_half(x, cos, sin):
    x1, x2 = jnp.split(x, 2, axis=-1)
    return jnp.concatenate([x1 * cos - x2 * sin, x2 * cos + x1 * sin], axis=-1)

def apply_axial_rope(x, tables):
    cr, sr, cc, sc = [t[None, :, None, None, :].astype(x.dtype) for t in tables]
    xr, xcol = jnp.split(x, 2, axis=-1)
    return jnp.concatenate([_rot_half(xr, cr, sr), _rot_half(xcol, cc, sc)], axis=-1)

def diff_attn_core(q, k, v, lam):
    s = jnp.einsum('bqhid,bkhid->bhiqk', q, k) * (HEAD_DIM ** -0.5)
    p = jax.nn.softmax(s.astype(jnp.float32), axis=-1)
    a = p[:, :, 0] - lam * p[:, :, 1]
    return jnp.einsum('bhqk,bkhe->bqhe', a.astype(v.dtype), v)

def latent_diff_attn(q, k_all, v_all, lam):
    b, t = q.shape[0], q.shape[1]
    nb = t // Q_BLOCK
    qb = q.reshape(b, nb, Q_BLOCK, DIFF_HEADS, 2, HEAD_DIM).transpose(1, 0, 2, 3, 4, 5)
    out = lax.map(lambda qblk: diff_attn_core(qblk, k_all, v_all, lam), qb)
    return out.transpose(1, 0, 2, 3, 4).reshape(b, t, DIFF_HEADS, V_HEAD_DIM)

def diff_head_out(o, subln_gain, lam_init, w_o):
    o = rmsnorm(o, subln_gain) * (1.0 - lam_init)
    return o.reshape(o.shape[0], o.shape[1], V_WIDTH) @ w_o

def split_qk(y, t):
    b = y.shape[0]
    return y.reshape(b, t, DIFF_HEADS, 2, HEAD_DIM)

def diff_attn_mixer(hl, hc, w_qkv, w_o, lq1, lk1, lq2, lk2, subln_gain, lam_init, rope_tables, need_ctx_out):
    b, t = hl.shape[0], hl.shape[1]
    lc = hc.shape[1]
    lam = (jnp.exp(jnp.sum(lq1.astype(jnp.float32) * lk1.astype(jnp.float32)))
           - jnp.exp(jnp.sum(lq2.astype(jnp.float32) * lk2.astype(jnp.float32))) + lam_init)
    yl = hl @ w_qkv
    ql = apply_axial_rope(split_qk(yl[..., :QK_WIDTH], t), rope_tables)
    kl = apply_axial_rope(split_qk(yl[..., QK_WIDTH:2 * QK_WIDTH], t), rope_tables)
    vl = yl[..., 2 * QK_WIDTH:].reshape(b, t, DIFF_HEADS, V_HEAD_DIM)
    if need_ctx_out:
        yc = hc @ w_qkv
        qc = split_qk(yc[..., :QK_WIDTH], lc)
        kv_c = yc[..., QK_WIDTH:]
    else:
        kv_c = hc @ w_qkv[:, QK_WIDTH:]
    kc = split_qk(kv_c[..., :QK_WIDTH], lc)
    vc = kv_c[..., QK_WIDTH:].reshape(b, lc, DIFF_HEADS, V_HEAD_DIM)
    k_all = jnp.concatenate([kl, kc], axis=1)
    v_all = jnp.concatenate([vl, vc], axis=1)
    out_l = diff_head_out(latent_diff_attn(ql, k_all, v_all, lam), subln_gain, lam_init, w_o)
    out_c = None
    if need_ctx_out:
        out_c = diff_head_out(diff_attn_core(qc, kc, vc, lam), subln_gain, lam_init, w_o)
    return out_l, out_c

def short_conv_mixer(h, w_in, conv_w, w_out):
    y = h @ w_in
    gb, gc, xv = jnp.split(y, 3, axis=-1)
    return (gb * dwconv3(gc * xv, conv_w)) @ w_out

def conv_ffn(h, w_up, conv_w, w_down):
    u = dwconv3(h @ w_up, conv_w)
    g, v = jnp.split(u, 2, axis=-1)
    return (jax.nn.silu(g) * v) @ w_down

def setup_inputs(seed: int = 0) -> dict:
    key = jax.random.key(seed)
    ks = jax.random.split(key, 24)
    f32 = jnp.float32
    nrm = lambda k, shape, s: jax.random.normal(k, shape, f32) * s
    d = D_MODEL
    return {
        "x": nrm(ks[0], (BATCH, SEQ, d), 1.0),
        "c": nrm(ks[1], (BATCH, d), 1.0),
        "ctx": nrm(ks[2], (BATCH, CTX_LEN, d), 1.0),
        "c_ctx": nrm(ks[3], (d,), 1.0),
        "w_ada": nrm(ks[4], (DEPTH, d, N_MOD * d), 0.5 * d ** -0.5),
        "b_ada": nrm(ks[5], (DEPTH, N_MOD * d), 0.02),
        "attn_w_qkv": nrm(ks[6], (N_ATTN, d, QKV_WIDTH), d ** -0.5),
        "attn_w_o": nrm(ks[7], (N_ATTN, V_WIDTH, d), V_WIDTH ** -0.5),
        "attn_lambda_q1": nrm(ks[8], (N_ATTN, HEAD_DIM), 0.1),
        "attn_lambda_k1": nrm(ks[9], (N_ATTN, HEAD_DIM), 0.1),
        "attn_lambda_q2": nrm(ks[10], (N_ATTN, HEAD_DIM), 0.1),
        "attn_lambda_k2": nrm(ks[11], (N_ATTN, HEAD_DIM), 0.1),
        "attn_subln_gain": 1.0 + nrm(ks[12], (N_ATTN, V_HEAD_DIM), 0.02),
        "sconv_w_in": nrm(ks[13], (N_CONV, d, 3 * d), d ** -0.5),
        "sconv_conv": nrm(ks[14], (N_CONV, CONV_W, d), CONV_W ** -0.5),
        "sconv_w_out": nrm(ks[15], (N_CONV, d, d), d ** -0.5),
        "ffn_w_up": nrm(ks[16], (DEPTH, d, 2 * D_FF), d ** -0.5),
        "ffn_conv": nrm(ks[17], (DEPTH, CONV_W, 2 * D_FF), CONV_W ** -0.5),
        "ffn_w_down": nrm(ks[18], (DEPTH, D_FF, d), D_FF ** -0.5),
        "final_gain": 1.0 + nrm(ks[19], (d,), 0.02),
    }

def reference(x, c, ctx, c_ctx, w_ada, b_ada, attn_w_qkv, attn_w_o, attn_lambda_q1, attn_lambda_k1,
              attn_lambda_q2, attn_lambda_k2, attn_subln_gain, sconv_w_in, sconv_conv, sconv_w_out,
              ffn_w_up, ffn_conv, ffn_w_down, final_gain):
    n_tokens = x.shape[1]
    rope_tables = axial_rope_tables(n_tokens)
    last_attn = max(i for i in range(DEPTH) if i % N_MIXERS == 0)
    xl, xc = x, ctx
    for i in range(DEPTH):
        ctx_update = i < last_attn
        ctx_read = i <= last_attn and i % N_MIXERS == 0
        sh1, sc1, g1, sh2, sc2, g2 = [m[:, None, :] for m in adaln(c, w_ada[i], b_ada[i])]
        hl = modulate(rmsnorm(xl), sh1, sc1)
        if ctx_update or ctx_read:
            csh1, csc1, cg1, csh2, csc2, cg2 = adaln(c_ctx, w_ada[i], b_ada[i])
            hc = modulate(rmsnorm(xc), csh1, csc1)
        if i % N_MIXERS == 0:
            a = i // N_MIXERS
            lam_init = 0.8 - 0.6 * math.exp(-0.3 * i)
            yl, yc = diff_attn_mixer(hl, hc, attn_w_qkv[a], attn_w_o[a], attn_lambda_q1[a], attn_lambda_k1[a],
                                     attn_lambda_q2[a], attn_lambda_k2[a], attn_subln_gain[a], lam_init,
                                     rope_tables, ctx_update)
        else:
            j = i // N_MIXERS
            yl = short_conv_mixer(hl, sconv_w_in[j], sconv_conv[j], sconv_w_out[j])
            if ctx_update:
                yc = short_conv_mixer(hc, sconv_w_in[j], sconv_conv[j], sconv_w_out[j])
        xl = xl + g1 * yl
        xl = xl + g2 * conv_ffn(modulate(rmsnorm(xl), sh2, sc2), ffn_w_up[i], ffn_conv[i], ffn_w_down[i])
        if ctx_update:
            xc = xc + cg1 * yc
            xc = xc + cg2 * conv_ffn(modulate(rmsnorm(xc), csh2, csc2), ffn_w_up[i], ffn_conv[i], ffn_w_down[i])
    return rmsnorm(xl, final_gain)


_drawn_inputs = setup_inputs


def setup_inputs(seed=0):
    import zlib

    import numpy as np

    out = dict(_drawn_inputs(seed))
    spreads = {}
    factors = {'attn_lambda_q1': 5.025,
     'attn_lambda_k1': 6.644,
     'attn_lambda_q2': 5.146,
     'attn_lambda_k2': 4.212,
     'attn_subln_gain': 8.0,
     'final_gain': 2.919}
    for name, (base, spread) in spreads.items():
        noise = np.random.default_rng([zlib.crc32(name.encode()), seed]).standard_normal(out[name].shape)
        drawn = base * np.exp(spread * noise) if base else spread * noise
        out[name] = __import__('jax').numpy.asarray(drawn.astype(out[name].dtype))
    for name, factor in factors.items():
        out[name] = (out[name] * factor).astype(out[name].dtype)
    return out
```

```python
import concourse.bass as bass
from concourse import mybir
from contextlib import ExitStack
import math

F32 = mybir.dt.float32
F32R = mybir.dt.float32r
ACT = mybir.ActivationFunctionType
ALU = mybir.AluOpType
AX_X = mybir.AxisListType.X

P = 128
D = 2048
T = 256
KT = D // P
HEADS = 8
QK = 2048
D_FF = 5632
FT = D_FF // P
GRID_W = 64
HEAD_DIM = 128
SCALE = HEAD_DIM ** -0.5
EPS = 1e-6
LAM_INIT = 0.8 - 0.6 * math.exp(-0.3 * 0)
SLAB = 256
RING = 4
KU = 4
ADA_COLS = 512
ADA_SLABS = 6 * D // ADA_COLS
ADA_FIRST = 2 * D // ADA_COLS

PHASES = {"k": (8, 4), "v": (8, 4), "q": (8, 4), "o": (8, 4), "up0": (44, 4), "dn0": (8, 12),
          "sin": (24, 4), "so": (8, 4), "up1": (44, 4), "dn1": (8, 12)}
UNITS, SLABS = {}, {}
_u = _s = 0
for _name, (_slabs, _units) in PHASES.items():
    UNITS[_name], SLABS[_name] = _u, _s
    _u += _slabs * _units
    _s += _slabs

B0, B1, COND, FGAIN, SUBLN, LAMB = 0, 96, 192, 224, 240, 242
CONV = (246, 246 + 3 * 88 + 3 * 16)
SCONV = 246 + 3 * 88
VECS = 246 + 3 * 88 + 3 * 16 + 3 * 88
SH1, SC1, G1, SH2, SC2, G2 = (16 * n for n in range(6))

ADA_AT = {"k": 0, "v": 4, "q": 8, "up0": 12, "dn0": 23, "sin": 31, "up1": 39}


def down_tiles(k):
    return (4 * k, 4) if k < 8 else (32 + 3 * (k - 8), 3)


def program(nc, x, c, ctx_in, c_ctx, w_ada, b_ada, w_qkv, w_o, lq1, lk1, lq2, lk2, subln, w_in, conv_in,
            w_out, w_up, conv_ffn, w_down, final_gain, ident_in, rope_cos_in, rope_sin_in, out):
    tiles = lambda w: w.rearrange("(t p) n -> p t n", p=P)
    qkv_w, o_w, in_w, out_w = tiles(w_qkv[0]), tiles(w_o[0]), tiles(w_in[0]), tiles(w_out[0])
    up_w, dn_w = [tiles(w_up[l]) for l in range(2)], [tiles(w_down[l]) for l in range(2)]
    ada_w = [tiles(w_ada[l]) for l in range(2)]
    x_rows = x[0].rearrange("(t p) n -> p t n", p=P)
    ctx_rows = ctx_in[0].rearrange("(t p) n -> p t n", p=P)
    out_rows = out[0].rearrange("(t p) n -> p t n", p=P)

    with ExitStack() as scope:
        KB = 1024
        start = (nc.sbuf_base + 63) // 64 * 64
        at_x = start
        at_u = at_x + 32 * KB
        at_res = at_u + 96 * KB
        at_raw = at_res + 16 * KB
        at_hi = at_raw + 16 * KB
        at_lo = at_hi + 16 * KB
        at_ada = at_lo + 16 * KB
        at_small = at_ada + 10 * KB
        small = [at_small]

        def at(name, shape, dt, offset):
            return nc.alloc_sbuf_tensor_at(name, shape, dt, offset=offset)

        def little(name, shape, dt=F32):
            n = 4
            for k in shape[1:]:
                n *= k
            n = (n + 31) // 32 * 32
            t = at(name, shape, dt, small[0])
            small[0] += n
            return t

        xs = at("xs", [P, KT, 2 * T], F32R, at_x)
        res = at("res", [P, KT, T], F32, at_res)
        raw = at("raw", [P, RING, KU, SLAB], F32, at_raw)
        w_hi = at("w_hi", [P, RING, KU, SLAB], F32R, at_hi)
        w_lo = at("w_lo", [P, RING, KU, SLAB], F32R, at_lo)
        ada_ring = at("ada_ring", [P, 2, 2, ADA_COLS], F32, at_ada)
        ada_sum = at("ada_sum", [P, ADA_COLS], F32, at_ada + 8 * KB)
        x_tok = at("x_tok", [P, 2, D], F32, at_u)
        ctx_tok = at("ctx_tok", [P, 2, D], F32, at_u + 16 * KB)
        xn_l = at("xn_l", [P, KT, T], F32, at_res)
        xn_c = at("xn_c", [P, KT, T], F32, at_u + 32 * KB)
        start_ring = at("start_ring", [P, 4, 2, ADA_COLS], F32, at_u + 48 * KB)
        vec_rows = at("vec_rows", [P, 8, P], F32, at_hi)
        mod_rows = at("mod_rows", [2, 2, ADA_COLS], F32, at_hi + 4 * KB)
        squares = at("squares", [P, D], F32, at_lo)
        k_t = at("k_t", [P, 2 * HEADS, 2 * T], F32, at_u)
        v_rows = at("v_rows", [P, 4, D], F32, at_u + 32 * KB)
        cs = at("cs", [P, KT, 2 * T], F32R, at_u + 64 * KB)
        attn = at_u + 64 * KB
        probs = at("probs", [P, 4, 512], F32, attn)
        a_t = at("a_t", [P, 2, 512], F32, attn + 8 * KB)
        q_head = at("q_head", [P, 2, T], F32, attn + 12 * KB)
        o_square = at("o_square", [P, T], F32, attn + 14 * KB)
        q_t = at("q_t", [P, 2 * HEADS, T], F32, attn + 16 * KB)
        o_rows = at("o_rows", [P, 2, D], F32, at_res)
        o_feat = at("o_feat", [P, 2, 2, T], F32, attn)
        y_qk = at("y_qk", [P, 2, T], F32, at_res)
        rot = at("rot", [P, 2, T], F32, at_res + 2 * KB)
        rope_cos = at("rope_cos", [P, T], F32, at_res + 4 * KB)
        rope_sin = at("rope_sin", [P, T], F32, at_res + 5 * KB)
        act = at("act", [P, FT, 2 * T], F32R, at_u)
        z = at("z", [P, KT, 2 * T], F32R, at_u)
        y = at("y", [P, 2, T], F32, at_u + 88 * KB)
        part_a = at("part_a", [P, 2, T], F32, at_u + 90 * KB)
        part_b = at("part_b", [P, 2, T], F32, at_u + 92 * KB)
        part_c = at("part_c", [P, 2, T], F32, at_u + 94 * KB)
        out_tok = at("out_tok", [P, 2, D], F32, at_u)
        ident = little("ident", [P, P])
        ones = little("ones", [P, P])
        vec = little("vec", [P, VECS])
        cond = little("cond", [P, 2, KT])
        ctx_mod = little("ctx_mod", [P, 32])
        row_sum = little("row_sum", [P, 4])
        row_var = little("row_var", [P, 4])
        row_inv = little("row_inv", [P, 4])
        row_rstd = little("row_rstd", [P, 4])
        lam_prod = little("lam_prod", [P, 2])
        lam_exp = little("lam_exp", [P, 2])
        neg_lam = little("neg_lam", [P, 1])
        gain_o = little("gain_o", [P, 2])
        s_max = little("s_max", [P, 4])
        s_neg = little("s_neg", [P, 4])
        s_sum = little("s_sum", [P, 4])
        s_inv = little("s_inv", [P, 4])
        s_lam = little("s_lam", [P, 2])
        o_sum = little("o_sum", [P, 2, HEADS])
        o_inv = little("o_inv", [P, 2, HEADS])
        o_rstd = little("o_rstd", [P, 2, HEADS])
        assert small[0] <= nc.sbuf_usable_end, (small[0], nc.sbuf_usable_end)

        ps = scope.enter_context(nc.psum_tensor("ps", [P, 8, 512], F32))

        sem = lambda name: scope.enter_context(nc.semaphore(name))
        vecs_loaded, ident_loaded, x_loaded, ctx_loaded = sem("vecs_loaded"), sem("ident_loaded"), sem("x_loaded"), sem("ctx_loaded")
        rope_loaded = sem("rope_loaded")
        start_full = [sem(f"start_full{n}") for n in range(4)]
        start_used = sem("start_used")
        ones_made, vecs_turned, vecs_made, plus_one = sem("ones_made"), sem("vecs_turned"), sem("vecs_made"), sem("plus_one")
        cond_made, lam_multiplied, lam_summed, lam_exped, lam_part, lam_made = (
            sem("cond_made"), sem("lam_multiplied"), sem("lam_summed"), sem("lam_exped"), sem("lam_part"), sem("lam_made"))
        rows_squared, rows_var, rows_inv, rows_rstd, rows_normed = (
            sem("rows_squared"), sem("rows_var"), sem("rows_inv"), sem("rows_rstd"), sem("rows_normed"))
        xn_turned, xn_kept = sem("xn_turned"), sem("xn_kept")
        mod_copied, mod_turned, mod_made, h_made, h_hi = (
            sem("mod_copied"), sem("mod_turned"), sem("mod_made"), sem("h_made"), sem("h_hi"))
        raw_full = [sem(f"raw_full{n}") for n in range(RING)]
        hi_made, lo_made, w_used = sem("hi_made"), sem("lo_made"), sem("w_used")
        ada_full = [sem("ada_full0"), sem("ada_full1")]
        ada_step, ada_reduced, ada_added = sem("ada_step"), sem("ada_reduced"), sem("ada_added")
        a_copied, acc_read = sem("a_copied"), sem("acc_read")
        xs_ready = sem("xs_ready")
        rot_made, rope_part, rope_done = sem("rot_made"), sem("rope_part"), sem("rope_done")
        taps_mid, taps_first, taps_done = sem("taps_mid"), sem("taps_first"), sem("taps_done")
        silu_made, gated, act_hi_made, act_made = sem("silu_made"), sem("gated"), sem("act_hi_made"), sem("act_made")
        gx_made, z_mul, z_hi_made, z_made = sem("gx_made"), sem("z_mul"), sem("z_hi_made"), sem("z_made")
        res_made, sq_made, sq_used = sem("res_made"), sem("sq_made"), sem("sq_used")
        var_made, inv_made, rstd_made, xm_made, xh_made, xh_hi = (
            sem("var_made"), sem("inv_made"), sem("rstd_made"), sem("xm_made"), sem("xh_made"), sem("xh_hi"))
        qh_made, scores_made, max_made, neg_made, exp_done = (
            sem("qh_made"), sem("scores_made"), sem("max_made"), sem("neg_made"), sem("exp_done"))
        sum_inv, lam_scaled, p1_scaled, a_made = sem("sum_inv"), sem("lam_scaled"), sem("p1_scaled"), sem("a_made")
        at_made, at_copied, o_made, o_copied, o_squared = (
            sem("at_made"), sem("at_copied"), sem("o_made"), sem("o_copied"), sem("o_squared"))
        o_var, o_inverted, o_root, o_normed, o_turned, o_gained, o_hi = (
            sem("o_var"), sem("o_inverted"), sem("o_root"), sem("o_normed"), sem("o_turned"), sem("o_gained"), sem("o_hi"))
        xt_turned, xt_kept, xt_loaded = sem("xt_turned"), sem("xt_kept"), sem("xt_loaded")
        fin_turned, fin_kept, fin_stored = sem("fin_turned"), sem("fin_kept"), sem("fin_stored")

        block = scope.enter_context(nc.Block())

        def wait(eng, s, n):
            if isinstance(n, int) and n <= 0:
                return
            eng.wait_ge(s, n)

        def loop(eng, n, body):
            body(0)
            if n > 1:
                with eng.Fori(1, n) as i:
                    body(i)

        @block.sync
        def _(sp):
            def first_modulation(g, back=0):
                for half, first in ((0, SC1 * P), (1, SH1 * P)):
                    for q in range(8):
                        n = 16 * g + (8 * half + q - 16 * back)
                        wait(sp, start_used, n - 3)
                        sp.dma_start(start_ring[:, q % 4, :, :],
                                     ada_w[0][:, 2 * q:2 * q + 2, bass.ds(g * ADA_COLS + (first - back * ADA_COLS), ADA_COLS)]
                                     ).then_inc(start_full[q % 4], 16)

            first_modulation(0)
            with sp.Fori(2, 5) as g:
                first_modulation(g, 1)

            def load(quad, slot, w, tile, n_tiles, col):
                wait(sp, lo_made, 4 * quad + slot - 3)
                sp.dma_start(raw[:, slot, 0:n_tiles, :], w[:, tile:tile + n_tiles, bass.ds(col, SLAB)]
                             ).then_inc(raw_full[slot], 16)

            def k_slab(s):
                for k in range(4):
                    load(s + UNITS["k"] // 4, k, qkv_w, 4 * k, 4, s * SLAB + QK)
            loop(sp, 8, k_slab)

            def plain(phase, w, base):
                with sp.Fori(0, 8) as s:
                    for k in range(4):
                        load(s + UNITS[phase] // 4, k, w, 4 * k, 4, s * SLAB + base)

            def up(phase, w):
                with sp.Fori(0, FT // 2) as j:
                    for h in range(2):
                        for k in range(4):
                            load(2 * j + (UNITS[phase] // 4 + h), k, w, 4 * k, 4, j * SLAB + h * D_FF)

            def down(phase, w):
                with sp.Fori(0, 8) as s:
                    for k in range(12):
                        tile, n = down_tiles(k)
                        load(3 * s + (UNITS[phase] // 4 + k // 4), k % 4, w, tile, n, s * SLAB)

            plain("v", qkv_w, 2 * QK)
            plain("q", qkv_w, 0)
            plain("o", o_w, 0)
            up("up0", up_w[0])
            down("dn0", dn_w[0])
            with sp.Fori(1, 9) as n:
                for h, first in ((0, D), (1, 2 * D), (2, 0)):
                    for k in range(4):
                        load(3 * n + (UNITS["sin"] // 4 + h - 3), k, in_w, 4 * k, 4, n * SLAB + (first - SLAB))
            plain("so", out_w, 0)
            up("up1", up_w[1])
            down("dn1", dn_w[1])
            for n in range(4):
                sp.wait_ge(fin_kept, 2 * (n + 1))
                sp.dma_start(out_rows[:, :, 512 * n:512 * (n + 1)], out_tok[:, :, 512 * n:512 * (n + 1)]
                             ).then_inc(fin_stored, 16)
            sp.wait_ge(fin_stored, 64)

        @block.gpsimd
        def _(pool):
            nc.gpsimd.memset(ones[:, :], 1.0).then_inc(ones_made, 1)
            pool.wait_ge(xs_ready, 8)
            pool.dma_start(rope_cos[:, :], rope_cos_in).then_inc(rope_loaded, 16)
            pool.dma_start(rope_sin[:, :], rope_sin_in).then_inc(rope_loaded, 16)

            def ada_slab(j, layer, col):
                for q in range(8):
                    wait(pool, ada_step, 16 * j + (2 * q - 2))
                    pool.dma_start(ada_ring[:, q % 2, :, :],
                                   ada_w[layer][:, 2 * q:2 * q + 2, bass.ds(col, ADA_COLS)]
                                   ).then_inc(ada_full[q % 2], 16)

            loop(pool, 12, lambda j: ada_slab(j, 0, j * ADA_COLS + ADA_FIRST * ADA_COLS))
            pool.wait_ge(scores_made, 4 * HEADS)
            pool.dma_start(x_tok[:, :, :], x_rows).then_inc(xt_loaded, 16)
            with pool.Fori(12, 16) as j:
                ada_slab(j, 0, j * ADA_COLS + ADA_FIRST * ADA_COLS)
            with pool.Fori(16, 40) as j:
                ada_slab(j, 1, j * ADA_COLS + (-16 * ADA_COLS))

        @block.scalar
        def _(se):
            se.dma_start(ident[:, :], ident_in).then_inc(ident_loaded, 16)
            rows = lambda v: v.rearrange("(t p) -> t p", p=P)
            r = vec_rows
            loads = [(r[0:96, 0, :], rows(b_ada[0])), (r[96:112, 0, :], rows(c[0])), (r[112:128, 0, :], rows(c_ctx)),
                     (r[0:96, 1, :], rows(b_ada[1])), (r[96:112, 1, :], rows(final_gain)),
                     (r[112:114, 1, :], rows(subln[0])), (r[114:115, 1, :], lq1), (r[115:116, 1, :], lk1),
                     (r[116:117, 1, :], lq2), (r[117:118, 1, :], lk2)]
            for n in range(3):
                loads += [(r[0:88, 2 + n, :], rows(conv_ffn[0, n])), (r[88:104, 2 + n, :], rows(conv_in[0, n])),
                          (r[0:88, 5 + n, :], rows(conv_ffn[1, n]))]
            for dst, src in loads:
                se.dma_start(dst, src).then_inc(vecs_loaded, 16)
            assert len(loads) == 19
            se.dma_start(x_tok[:, :, :], x_rows).then_inc(x_loaded, 16)
            se.dma_start(ctx_tok[:, :, :], ctx_rows).then_inc(ctx_loaded, 16)

            se.wait_ge(vecs_made, 1)
            nc.scalar.activation(cond[:, :, :], vec[:, COND:COND + 32].rearrange("p (c k) -> p c k", c=2), ACT.Silu).then_inc(cond_made, 1)
            se.wait_ge(lam_summed, 1)
            nc.scalar.activation(lam_exp[:, :], ps[:, 6, 0:2], ACT.Exp).then_inc(lam_exped, 1)
            for n, (loaded, tok) in enumerate(((x_loaded, x_tok), (ctx_loaded, ctx_tok))):
                se.wait_ge(loaded, 16)
                for t in range(2):
                    wait(se, rows_squared, 2 * n + t)
                    nc.scalar.activation(squares[:, :], tok[:, t, :], ACT.Square,
                                         accum_out=row_sum[:, 2 * n + t:2 * n + t + 1]).then_inc(rows_squared, 1)
            se.wait_ge(rows_inv, 1)
            nc.scalar.activation(row_rstd[:, :], row_inv[:, :], ACT.Sqrt).then_inc(rows_rstd, 1)

            def first_modulation(g):
                for b in range(2):
                    n = 2 * g + b
                    wait(se, start_used, 8 * n + 8)
                    wait(se, mod_turned, n - 1)
                    nc.scalar.activation(mod_rows[:, b, :], ps[0:2, 2 + b, :], ACT.Copy).then_inc(mod_copied, 1)
                se.wait_ge(mod_made, 2 * g + 2)
                if isinstance(g, int):
                    se.wait_ge(xn_kept, 16)
                for m, (xn, dst) in enumerate(((xn_l, xs), (xn_c, cs))):
                    table = ctx_mod if m else vec
                    for k in range(4):
                        last = nc.scalar.activation(
                            xn[:, bass.ds(4 * g + k, 1), :], xn[:, bass.ds(4 * g + k, 1), :], ACT.Identity,
                            scale=table[:, bass.ds(4 * g + (SC1 + k), 1)], bias=table[:, bass.ds(4 * g + (SH1 + k), 1)])
                    last.then_inc(h_made, 1)
                    se.wait_ge(h_made, 2 * g + (m + 1))
                    nc.scalar.activation(dst[:, bass.ds(4 * g, 4), 0:T], xn[:, bass.ds(4 * g, 4), :], ACT.Copy).then_inc(h_hi, 1)
            loop(se, 4, first_modulation)

            def hi(quad, slot, n_tiles=KU):
                se.wait_ge(raw_full[slot], 16 * quad + 16)
                wait(se, w_used, 4 * quad + slot - 3)
                nc.scalar.activation(w_hi[:, slot, 0:n_tiles, :], raw[:, slot, 0:n_tiles, :], ACT.Copy).then_inc(hi_made, 1)

            def copy_a(phase, s, bank, dst, per_slab=4):
                se.wait_ge(w_used, per_slab * s + (UNITS[phase] + per_slab))
                nc.scalar.activation(dst, ps[:, bank:bank + 2, 0:T], ACT.Copy).then_inc(a_copied, 1)

            def rotate(n):
                se.wait_ge(acc_read, n + 1)
                for d in range(4):
                    last = nc.scalar.activation(rot[32 * d:32 * d + 32, :, :], y_qk[32 * (d ^ 1):32 * (d ^ 1) + 32, :, :], ACT.Copy)
                last.then_inc(rot_made, 1)

            def k_point(k, s):
                if k == 2:
                    se.wait_ge(w_used, 4 * s + (UNITS["k"] + 4))
                    wait(se, rope_done, s)
                    nc.scalar.activation(y_qk[:, :, :], ps[:, 0:2, 0:T], ACT.Copy)
                    nc.scalar.activation(k_t[:, bass.ds(2 * s, 2), T:2 * T], ps[:, 2:4, 0:T], ACT.Copy).then_inc(a_copied, 1)
                if k == 3:
                    rotate(s + SLABS["k"])

            def v_point(k, s):
                if k == 2:
                    se.wait_ge(w_used, 4 * s + (UNITS["v"] + 4))
                    nc.scalar.activation(v_rows[:, 0:2, bass.ds(s * SLAB, SLAB)], ps[:, 0:2, 0:SLAB], ACT.Copy).then_inc(a_copied, 1)

            def q_point(k, s, h):
                if k == 2:
                    se.wait_ge(rope_done, s + 8)
                    copy_a("q", s, 2 * h, y_qk[:, :, :])
                if k == 3:
                    rotate(s + SLABS["q"])

            def res_point(k, phase, s, h, n_res, per_slab=4):
                if k == 2:
                    wait(se, res_made, s + n_res)
                    copy_a(phase, s, 2 * h, y[:, :, :], per_slab)
                if k == 3:
                    se.wait_ge(res_made, s + (n_res + 1))
                    wait(se, sq_used, s + n_res)
                    nc.scalar.activation(part_c[:, :, :], res[:, bass.ds(2 * s, 2), :], ACT.Square).then_inc(sq_made, 1)

            def norm_tail(n_norm, table, gain_only=False):
                se.wait_ge(inv_made, n_norm + 1)
                nc.scalar.activation(part_c[:, 1, :], part_c[:, 0, :], ACT.Sqrt).then_inc(rstd_made, 1)

                def two(i):
                    for b, part in ((0, part_a), (1, part_b)):
                        n = 2 * i + b
                        se.wait_ge(xm_made, n + (8 * n_norm + 1))
                        for m in range(2):
                            if gain_only:
                                last = nc.scalar.activation(part[:, m, :], part[:, m, :], ACT.Copy,
                                                            scale=vec[:, bass.ds(2 * n + (FGAIN + m), 1)])
                            else:
                                last = nc.scalar.activation(part[:, m, :], part[:, m, :], ACT.Identity,
                                                            scale=vec[:, bass.ds(2 * n + (table + 16 + m), 1)],
                                                            bias=vec[:, bass.ds(2 * n + (table + m), 1)])
                        last.then_inc(xh_made, 1)
                        if not gain_only:
                            se.wait_ge(xh_made, n + (8 * n_norm + 1))
                            nc.scalar.activation(xs[:, bass.ds(2 * n, 2), 0:T], part[:, :, :], ACT.Copy).then_inc(xh_hi, 1)
                with se.Fori(0, 4) as i:
                    two(i)

            def up_copy(phase, j, which, h):
                wait(se, taps_done, 2 * j + (TAPS[phase] + which))
                copy_a(phase, 2 * j + which, 2 * h, y[:, :, :])

            def up_mid(phase, j, which, part):
                se.wait_ge(acc_read, 2 * j + (SLABS[phase] + which + 1))
                for m in range(2):
                    last = nc.scalar.activation(part[:, m, :], y[:, m, :], ACT.Copy,
                                                scale=vec[:, bass.ds(2 * j + tap_column(phase, which, m, 1), 1)])
                last.then_inc(taps_mid, 1)

            def up_silu(phase, j):
                se.wait_ge(taps_done, 2 * j + (TAPS[phase] + 1))
                nc.scalar.activation(part_a[:, :, :], part_a[:, :, :], ACT.Silu).then_inc(silu_made, 1)

            def up_hi(phase, j):
                se.wait_ge(gated, j + (PAIRS[phase] + 1))
                nc.scalar.activation(act[:, bass.ds(2 * j, 2), 0:T], part_a[:, :, :], ACT.Copy).then_inc(act_hi_made, 1)

            def g_point(k, phase, j, h):
                if k == 2:
                    up_copy(phase, j, 0, h)
                if k == 3:
                    wait(se, act_made, j + PAIRS[phase])
                    up_mid(phase, j, 0, part_a)

            def v_up_point(k, phase, j, h):
                if k == 0:
                    up_silu(phase, j)
                if k == 2:
                    up_copy(phase, j, 1, h)
                if k == 3:
                    up_mid(phase, j, 1, part_b)

            first = lambda i, h: isinstance(i, int) and h == 0

            def k_pair(i):
                for h in range(2):
                    for k in range(4):
                        hi(2 * i + h, k)
                        if not first(i, h):
                            k_point(k, 2 * i + (h - 1))
            loop(se, 4, k_pair)

            def v_pair(i):
                for h in range(2):
                    for k in range(4):
                        hi(2 * i + (UNITS["v"] // 4 + h), k)
                        if first(i, h):
                            k_point(k, 7)
                        else:
                            v_point(k, 2 * i + (h - 1))
            loop(se, 4, v_pair)

            def q_pair(i):
                for h in range(2):
                    for k in range(4):
                        hi(2 * i + (UNITS["q"] // 4 + h), k)
                        if first(i, h):
                            v_point(k, 7)
                        else:
                            q_point(k, 2 * i + (h - 1), 1 - h)
            loop(se, 4, q_pair)

            def attention():
                def take_q(h):
                    wait(se, scores_made, 4 * h)
                    nc.scalar.activation(q_head[:, :, :], q_t[:, bass.ds(2 * h, 2), :], ACT.Copy).then_inc(qh_made, 1)

                def square_o(h):
                    for t in range(2):
                        se.wait_ge(o_copied, 2 * h + (t + 1))
                        wait(se, o_squared, 2 * h + t)
                        nc.scalar.activation(o_square[:, :], o_rows[:, t, bass.ds(T * h, T)], ACT.Square,
                                             accum_out=o_sum[:, t, bass.ds(h, 1)]).then_inc(o_squared, 1)

                def head(h, at_start, at_end):
                    se.wait_ge(neg_made, h + 1)
                    for n in range(4):
                        if n % 2 == 0:
                            wait(se, at_made, 2 * h + (n // 2 - 1))
                        nc.scalar.activation(probs[:, n, :], ps[:, n, :], ACT.Exp, scale=SCALE, bias=s_neg[:, n:n + 1],
                                             accum_out=s_sum[:, n:n + 1]).then_inc(exp_done, 1)
                    if not at_end:
                        take_q(h + 1)
                    if not at_start:
                        square_o(h + (-1))
                    for t in range(2):
                        se.wait_ge(at_made, 2 * h + (t + 1))
                        wait(se, o_made, 2 * h + (t - 1))
                        nc.scalar.activation(a_t[:, t, :], ps[:, 4 + t, :], ACT.Copy).then_inc(at_copied, 1)

                se.wait_ge(rope_done, 16)
                take_q(0)
                head(0, True, False)
                with se.Fori(1, HEADS - 1) as h:
                    head(h, False, False)
                head(HEADS - 1, False, True)
                square_o(HEADS - 1)
                se.wait_ge(o_inverted, 1)
                nc.scalar.activation(o_rstd[:, :, :], o_inv[:, :, :], ACT.Sqrt).then_inc(o_root, 1)

                def gain(i):
                    for b in range(2):
                        h = 2 * i + b
                        se.wait_ge(o_turned, h + 1)
                        wait(se, xs_ready, h + (8 - 1))
                        for m in range(2):
                            last = nc.scalar.activation(o_feat[:, b, m, :], ps[:, b, T * m:T * m + T], ACT.Copy, scale=gain_o[:, m:m + 1])
                        last.then_inc(o_gained, 1)
                        se.wait_ge(o_gained, h + 1)
                        nc.scalar.activation(xs[:, bass.ds(2 * h, 2), 0:T], o_feat[:, b, :, :], ACT.Copy).then_inc(o_hi, 1)
                loop(se, 4, gain)

                def keep_x(i):
                    for b in range(2):
                        n = 2 * i + b
                        se.wait_ge(xt_turned, n + 1)
                        nc.scalar.activation(res[:, bass.ds(2 * n, 2), :], ps[:, 4 + b, :].rearrange("p (k t) -> p k t", k=2), ACT.Copy).then_inc(xt_kept, 1)
                loop(se, 4, keep_x)

            def o_pair(i):
                for h in range(2):
                    for k in range(4):
                        hi(2 * i + (UNITS["o"] // 4 + h), k)
                        if first(i, h):
                            q_point(k, 7, 1)
                            if k == 3:
                                attention()
                        else:
                            res_point(k, "o", 2 * i + (h - 1), 1 - h, RES["o"])
            loop(se, 4, o_pair)

            def up(phase, tail):
                def four(i):
                    for p in range(2):
                        for h in range(2):
                            for k in range(4):
                                hi(4 * i + (UNITS[phase] // 4 + 2 * p + h), k)
                                if first(i, p + h):
                                    tail(k)
                                elif h == 0:
                                    v_up_point(k, phase, 2 * i + (p - 1), 1)
                                else:
                                    g_point(k, phase, 2 * i + p, 0)
                                    if k == 1 and not first(i, p):
                                        up_hi(phase, 2 * i + (p - 1))
                loop(se, FT // 4, four)

            def down(phase, up_phase):
                def pair(i):
                    for h in range(2):
                        for k in range(12):
                            hi(6 * i + (UNITS[phase] // 4 + 3 * h + k // 4), k % 4, down_tiles(k)[1])
                            if first(i, h):
                                v_up_point(k, up_phase, FT // 2 - 1, 1)
                                if k == 5:
                                    up_hi(up_phase, FT // 2 - 1)
                            else:
                                res_point(k, phase, 2 * i + (h - 1), 1 - h, RES[phase], 12)
                loop(se, 4, pair)

            def o_tail(k):
                res_point(k, "o", 7, 1, RES["o"])
                if k == 3:
                    se.wait_ge(ada_added, 12)
                    norm_tail(0, B0 + SH2)
            up("up0", o_tail)
            down("dn0", "up0")

            def sin_point(k, j, h, which):
                if which == 0:
                    if k == 2:
                        wait(se, gx_made, j)
                        copy_a("sin", 3 * j, 2 * h, part_a[:, :, :])
                elif which == 1:
                    if k == 2:
                        wait(se, taps_done, j + TAPS["sin"])
                        copy_a("sin", 3 * j + 1, 2 * h, y[:, :, :])
                    if k == 3:
                        se.wait_ge(gx_made, j + 1)
                        wait(se, z_mul, j)
                        for m in range(2):
                            last = nc.scalar.activation(part_b[:, m, :], y[:, m, :], ACT.Copy,
                                                        scale=vec[:, bass.ds(2 * j + (SCONV + 16 + m), 1)])
                        last.then_inc(taps_mid, 1)
                else:
                    if k == 2:
                        wait(se, z_made, j)
                        copy_a("sin", 3 * j + 2, 2 * h, part_c[:, :, :])
                    if k == 3:
                        se.wait_ge(z_mul, j + 1)
                        nc.scalar.activation(z[:, bass.ds(2 * j, 2), 0:T], part_c[:, :, :], ACT.Copy).then_inc(z_hi_made, 1)

            def sin_six(i):
                for n in range(6):
                    for k in range(4):
                        hi(6 * i + (UNITS["sin"] // 4 + n), k)
                        if first(i, n):
                            res_point(k, "dn0", 7, 1, RES["dn0"], 12)
                            if k == 3:
                                se.wait_ge(ada_added, 24)
                                norm_tail(1, B1 + SH1)
                        elif n % 3 == 0:
                            sin_point(k, 2 * i + (n // 3 - 1), (n - 1) % 2, 2)
                        else:
                            sin_point(k, 2 * i + n // 3, (n - 1) % 2, n % 3 - 1)
            loop(se, 4, sin_six)

            def so_pair(i):
                for h in range(2):
                    for k in range(4):
                        hi(2 * i + (UNITS["so"] // 4 + h), k)
                        if first(i, h):
                            sin_point(k, 7, 1, 2)
                        else:
                            res_point(k, "so", 2 * i + (h - 1), 1 - h, RES["so"])
            loop(se, 4, so_pair)

            def so_tail(k):
                res_point(k, "so", 7, 1, RES["so"])
                if k == 3:
                    norm_tail(2, B1 + SH2)
            up("up1", so_tail)
            down("dn1", "up1")
            for k in range(4):
                res_point(k, "dn1", 7, 1, RES["dn1"], 12)
            norm_tail(3, 0, gain_only=True)

        @block.vector
        def _(ve):
            ve.wait_ge(vecs_turned, 1)
            spans = [(0, 0, 96, B0), (0, 96, 32, COND), (1, 0, 96, B1), (1, 96, 16 + 2 + 4, FGAIN)]
            for n in range(3):
                spans += [(2 + n, 0, 88, CONV[0] + 88 * n), (2 + n, 88, 16, SCONV + 16 * n), (5 + n, 0, 88, CONV[1] + 88 * n)]
            for tile, first_col, n, dst in spans:
                last = nc.vector.tensor_copy(vec[:, dst:dst + n],
                                             ps[:, tile // 4, 128 * (tile % 4) + first_col:128 * (tile % 4) + first_col + n])
            last.then_inc(vecs_made, 1)
            ve.wait_ge(vecs_made, 1)
            for base in (B0, B1):
                for scale in (SC1, SC2):
                    v = vec[:, base + scale:base + scale + 16]
                    last = nc.vector.tensor_scalar(v, v, 1.0, None, ALU.add)
            last.then_inc(plus_one, 1)
            lam4 = vec[:, LAMB:LAMB + 4].rearrange("p (n two) -> p two n", two=2)
            nc.vector.tensor_tensor(lam_prod[:, :], lam4[:, 0, :], lam4[:, 1, :], ALU.mult).then_inc(lam_multiplied, 1)
            nc.vector.tensor_scalar(gain_o[:, :], vec[:, SUBLN:SUBLN + 2], 1.0 - LAM_INIT, None, ALU.mult)
            ve.wait_ge(plus_one, 1)
            nc.vector.tensor_copy(ctx_mod[:, :], vec[:, 0:32]).then_inc(plus_one, 1)
            ve.wait_ge(lam_exped, 1)
            nc.vector.tensor_tensor(neg_lam[:, :], lam_exp[:, 1:2], lam_exp[:, 0:1], ALU.subtract).then_inc(lam_part, 1)
            ve.wait_ge(lam_part, 1)
            nc.vector.tensor_scalar(neg_lam[:, :], neg_lam[:, :], LAM_INIT, None, ALU.subtract).then_inc(lam_made, 1)

            ve.wait_ge(rows_squared, 4)
            nc.vector.tensor_scalar(row_var[:, :], row_sum[:, :], 1.0 / D, EPS, ALU.mult, ALU.add).then_inc(rows_var, 1)
            ve.wait_ge(rows_var, 1)
            nc.vector.reciprocal(row_inv[:, :], row_var[:, :]).then_inc(rows_inv, 1)
            ve.wait_ge(rows_rstd, 1)
            for n, tok in enumerate((x_tok, ctx_tok)):
                for t in range(2):
                    nc.vector.tensor_scalar(tok[:, t, :], tok[:, t, :], row_rstd[:, 2 * n + t:2 * n + t + 1], None, ALU.mult
                                            ).then_inc(rows_normed, 1)
            for n, xn in enumerate((xn_l, xn_c)):
                def keep(i):
                    for b in range(2):
                        ve.wait_ge(xn_turned, 2 * i + (8 * n + b + 1))
                        nc.vector.tensor_copy(xn[:, bass.ds(4 * i + 2 * b, 2), :],
                                              ps[:, b, :].rearrange("p (k t) -> p k t", k=2)).then_inc(xn_kept, 1)
                loop(ve, 4, keep)

            ve.wait_ge(plus_one, 2)

            def first_modulation(g):
                for b in range(2):
                    col = (SC1, SH1)[b]
                    ve.wait_ge(mod_turned, 2 * g + (b + 1))
                    both = ps[:, 4 + b, 0:8].rearrange("p (k c) -> p c k", c=2)
                    for m, table in enumerate((vec, ctx_mod)):
                        v = table[:, bass.ds(4 * g + col, 4)]
                        last = nc.vector.tensor_tensor(v, v, both[:, m, :], ALU.add)
                    last.then_inc(mod_made, 1)
                for m, (xn, dst) in enumerate(((xn_l, xs), (xn_c, cs))):
                    ve.wait_ge(h_hi, 2 * g + (m + 1))
                    nc.vector.tensor_tensor(dst[:, bass.ds(4 * g, 4), T:2 * T], xn[:, bass.ds(4 * g, 4), :],
                                            dst[:, bass.ds(4 * g, 4), 0:T], ALU.subtract).then_inc(xs_ready, 1)
            loop(ve, 4, first_modulation)

            def lo(quad, slot, n_tiles=KU):
                ve.wait_ge(hi_made, 4 * quad + (slot + 1))
                nc.vector.tensor_tensor(w_lo[:, slot, 0:n_tiles, :], raw[:, slot, 0:n_tiles, :],
                                        w_hi[:, slot, 0:n_tiles, :], ALU.subtract).then_inc(lo_made, 1)

            def ada_chunk(j, q):
                ve.wait_ge(ada_full[q % 2], 64 * j + 16 * (q // 2 + 1))
                for b in range(2):
                    t = 2 * q + b
                    w, scalar = ada_ring[:, q % 2, b, :], cond[:, 0, t:t + 1]
                    if t == 0:
                        wait(ve, ada_reduced, j)
                        nc.vector.tensor_scalar(ada_sum[:, :], w, scalar, None, ALU.mult).then_inc(ada_step, 1)
                    else:
                        ve.wait_ge(ada_step, 16 * j + t)
                        nc.vector.scalar_tensor_tensor(out=ada_sum[:, :], in0=w, scalar=scalar, in1=ada_sum[:, :],
                                                       op0=ALU.mult, op1=ALU.add).then_inc(ada_step, 1)

            def ada_add(j):
                ve.wait_ge(ada_reduced, j + 1)
                v = vec[:, bass.ds(4 * j + 4 * ADA_FIRST, 4)]
                nc.vector.tensor_tensor(v, v, ps[:, 6, 0:4], ALU.add).then_inc(ada_added, 1)

            def ada_in_pair(phase, i, h, k):
                j = i + ADA_AT[phase]
                if h == 0:
                    ada_chunk(j, 2 * k)
                    ada_chunk(j, 2 * k + 1)
                elif k == 3:
                    ada_add(j)

            def ada_in_24(phase, i, n):
                j = 2 * i + ADA_AT[phase]
                if n < 8:
                    ada_chunk(j, n)
                if n == 11:
                    ada_add(j)
                if 11 <= n < 19:
                    ada_chunk(j + 1, n - 11)
                if n == 23:
                    ada_add(j + 1)

            def add_b(n, bank, dst):
                ve.wait_ge(a_copied, n + 1)
                nc.vector.tensor_tensor(dst, dst, ps[:, bank:bank + 2, T:2 * T], ALU.add).then_inc(acc_read, 1)

            two = lambda t: t[:, :].unsqueeze(1).broadcast_to([P, 2, T])

            def rope(r, dst, n_slabs):
                if isinstance(r, int) and r == 0:
                    ve.wait_ge(rope_loaded, 32)
                ve.wait_ge(acc_read, n_slabs + 1)
                nc.vector.tensor_tensor(dst, y_qk[:, :, :], two(rope_cos), ALU.mult)
                ve.wait_ge(rot_made, r + 1)
                nc.vector.tensor_tensor(rot[:, :, :], rot[:, :, :], two(rope_sin), ALU.mult).then_inc(rope_part, 1)
                ve.wait_ge(rope_part, r + 1)
                nc.vector.tensor_tensor(dst, dst, rot[:, :, :], ALU.add).then_inc(rope_done, 1)

            def k_point(k, s):
                if k == 2:
                    ve.wait_ge(a_copied, s + 1)
                    nc.vector.tensor_tensor(y_qk[:, :, :], y_qk[:, :, :], ps[:, 0:2, T:2 * T], ALU.add)
                    kc = k_t[:, bass.ds(2 * s, 2), T:2 * T]
                    nc.vector.tensor_tensor(kc, kc, ps[:, 2:4, T:2 * T], ALU.add).then_inc(acc_read, 1)
                if k == 3:
                    rope(s, k_t[:, bass.ds(2 * s, 2), 0:T], s)

            def v_point(k, s):
                if k == 2:
                    ve.wait_ge(a_copied, s + (SLABS["v"] + 1))
                    nc.vector.tensor_copy(v_rows[:, 2:4, bass.ds(s * SLAB, SLAB)], ps[:, 2:4, 0:SLAB]).then_inc(acc_read, 1)

            def q_point(k, s, h):
                if k == 2:
                    add_b(s + SLABS["q"], 2 * h, y_qk[:, :, :])
                if k == 3:
                    rope(s + 8, q_t[:, bass.ds(2 * s, 2), :], s + SLABS["q"])

            def res_point(k, phase, s, h, gate):
                if k == 2:
                    n = s + SLABS[phase]
                    add_b(n, 2 * h, y[:, :, :])
                    ve.wait_ge(acc_read, n + 1)
                    for m in range(2):
                        r_ = res[:, bass.ds(2 * s + m, 1), :]
                        last = nc.vector.scalar_tensor_tensor(out=r_, in0=y[:, m:m + 1, :], scalar=vec[:, bass.ds(2 * s + (gate + m), 1)],
                                                              in1=r_, op0=ALU.mult, op1=ALU.add)
                    last.then_inc(res_made, 1)

            def norm_tail(n_norm, final=False):
                ve.wait_ge(sq_used, 8 * (n_norm + 1))
                nc.vector.tensor_scalar(part_c[:, 1, :], ps[:, 7, 0:T], 1.0 / D, EPS, ALU.mult, ALU.add).then_inc(var_made, 1)
                ve.wait_ge(var_made, n_norm + 1)
                nc.vector.reciprocal(part_c[:, 0, :], part_c[:, 1, :]).then_inc(inv_made, 1)
                ve.wait_ge(rstd_made, n_norm + 1)
                parts = (part_a, part_b)
                rstd = part_c[:, 1:2, :].broadcast_to([P, 2, T])

                def scaled(n, b):
                    nc.vector.tensor_tensor(parts[b][:, :, :], res[:, bass.ds(2 * n, 2), :], rstd, ALU.mult).then_inc(xm_made, 1)

                def low(n, b):
                    ve.wait_ge(xh_hi, n + (8 * n_norm + 1))
                    nc.vector.tensor_tensor(xs[:, bass.ds(2 * n, 2), T:2 * T], parts[b][:, :, :], xs[:, bass.ds(2 * n, 2), 0:T],
                                            ALU.subtract).then_inc(xs_ready, 1)
                if not final:
                    scaled(0, 0)
                    scaled(1, 1)
                    with ve.Fori(0, 3) as i:
                        for b in range(2):
                            low(2 * i + b, b)
                            ve.wait_ge(xs_ready, 2 * i + (8 * n_norm + 16 + b + 1))
                            scaled(2 * i + (b + 2), b)
                    low(6, 0)
                    low(7, 1)
                else:
                    def last_two(i):
                        for b in range(2):
                            n = 2 * i + b
                            wait(ve, fin_turned, n - 1)
                            scaled(n, b)
                        for b in range(2):
                            n = 2 * i + b
                            ve.wait_ge(fin_turned, n + 1)
                            nc.vector.tensor_copy(out_tok[:, :, bass.ds(2 * P * n, 2 * P)],
                                                  ps[:, b, :].rearrange("p (t f) -> p t f", t=2)).then_inc(fin_kept, 1)
                    loop(ve, 4, last_two)

            def taps(phase, j, which, part):
                n = j + TAPS[phase] if phase == "sin" else 2 * j + (TAPS[phase] + which)
                ve.wait_ge(taps_mid, n + 1)
                for m in range(2):
                    last = nc.vector.scalar_tensor_tensor(out=part[:, m, 1:T], in0=y[:, m, 0:T - 1],
                                                          scalar=vec[:, bass.ds(2 * j + tap_column(phase, which, m, 0), 1)],
                                                          in1=part[:, m, 1:T], op0=ALU.mult, op1=ALU.add)
                last.then_inc(taps_first, 1)
                ve.wait_ge(taps_first, n + 1)
                for m in range(2):
                    last = nc.vector.scalar_tensor_tensor(out=part[:, m, 0:T - 1], in0=y[:, m, 1:T],
                                                          scalar=vec[:, bass.ds(2 * j + tap_column(phase, which, m, 2), 1)],
                                                          in1=part[:, m, 0:T - 1], op0=ALU.mult, op1=ALU.add)
                last.then_inc(taps_done, 1)

            def g_point(k, phase, j, h):
                if k == 2:
                    add_b(2 * j + SLABS[phase], 2 * h, y[:, :, :])
                if k == 3:
                    taps(phase, j, 0, part_a)

            def v_up_point(k, phase, j, h):
                if k == 2:
                    add_b(2 * j + (SLABS[phase] + 1), 2 * h, y[:, :, :])
                if k == 3:
                    taps(phase, j, 1, part_b)

            def gate_pair(phase, j):
                n = j + PAIRS[phase]
                ve.wait_ge(silu_made, n + 1)
                ve.wait_ge(taps_done, 2 * j + (TAPS[phase] + 2))
                nc.vector.tensor_tensor(part_a[:, :, :], part_a[:, :, :], part_b[:, :, :], ALU.mult).then_inc(gated, 1)

            def low_pair(phase, j):
                ve.wait_ge(act_hi_made, j + (PAIRS[phase] + 1))
                nc.vector.tensor_tensor(act[:, bass.ds(2 * j, 2), T:2 * T], part_a[:, :, :], act[:, bass.ds(2 * j, 2), 0:T],
                                        ALU.subtract).then_inc(act_made, 1)

            first = lambda i, h: isinstance(i, int) and h == 0

            def k_pair(i):
                for h in range(2):
                    for k in range(4):
                        lo(2 * i + h, k)
                        ada_in_pair("k", i, h, k)
                        if not first(i, h):
                            k_point(k, 2 * i + (h - 1))
            loop(ve, 4, k_pair)

            def v_pair(i):
                for h in range(2):
                    for k in range(4):
                        lo(2 * i + (UNITS["v"] // 4 + h), k)
                        ada_in_pair("v", i, h, k)
                        if first(i, h):
                            k_point(k, 7)
                        else:
                            v_point(k, 2 * i + (h - 1))
            loop(ve, 4, v_pair)

            def q_pair(i):
                for h in range(2):
                    for k in range(4):
                        lo(2 * i + (UNITS["q"] // 4 + h), k)
                        ada_in_pair("q", i, h, k)
                        if first(i, h):
                            v_point(k, 7)
                        else:
                            q_point(k, 2 * i + (h - 1), 1 - h)
            loop(ve, 4, q_pair)

            def attention():
                def keep_o(h):
                    for t in range(2):
                        ve.wait_ge(o_made, 2 * h + (t + 1))
                        nc.vector.tensor_copy(o_rows[:, t, bass.ds(T * h, T)], ps[:, 6 + t, 0:T]).then_inc(o_copied, 1)

                def head(h, at_start):
                    ve.wait_ge(scores_made, 4 * h + 4)
                    nc.vector.reduce_max(s_max[:, :], ps[:, 0:4, :], AX_X).then_inc(max_made, 1)
                    ve.wait_ge(max_made, h + 1)
                    nc.vector.tensor_scalar(s_neg[:, :], s_max[:, :], -SCALE, None, ALU.mult).then_inc(neg_made, 1)
                    if not at_start:
                        keep_o(h + (-1))
                    ve.wait_ge(exp_done, 4 * h + 4)
                    nc.vector.reciprocal(s_inv[:, :], s_sum[:, :]).then_inc(sum_inv, 1)
                    ve.wait_ge(sum_inv, h + 1)
                    nc.vector.tensor_scalar(s_lam[:, :], s_inv[:, :].rearrange("p (t i) -> p i t", i=2)[:, 1, :], neg_lam[:, 0:1], None, ALU.mult
                                            ).then_inc(lam_scaled, 1)
                    ve.wait_ge(lam_scaled, h + 1)
                    for t in range(2):
                        last = nc.vector.tensor_scalar(probs[:, 2 * t + 1, :], probs[:, 2 * t + 1, :], s_lam[:, t:t + 1], None, ALU.mult)
                    last.then_inc(p1_scaled, 1)
                    ve.wait_ge(p1_scaled, h + 1)
                    for t in range(2):
                        nc.vector.scalar_tensor_tensor(out=probs[:, 2 * t, :], in0=probs[:, 2 * t, :], scalar=s_inv[:, 2 * t:2 * t + 1],
                                                       in1=probs[:, 2 * t + 1, :], op0=ALU.mult, op1=ALU.add).then_inc(a_made, 1)

                ve.wait_ge(lam_made, 1)
                head(0, True)
                with ve.Fori(1, HEADS) as h:
                    head(h, False)
                keep_o(HEADS - 1)
                ve.wait_ge(o_squared, 2 * HEADS)
                nc.vector.tensor_scalar(o_sum[:, :, :], o_sum[:, :, :], 1.0 / T, EPS, ALU.mult, ALU.add).then_inc(o_var, 1)
                ve.wait_ge(o_var, 1)
                nc.vector.reciprocal(o_inv[:, :, :], o_sum[:, :, :]).then_inc(o_inverted, 1)
                ve.wait_ge(o_root, 1)
                ve.wait_ge(o_copied, 2 * HEADS)

                def scaled(h):
                    for t in range(2):
                        o = o_rows[:, t, bass.ds(T * h, T)]
                        last = nc.vector.tensor_scalar(o, o, o_rstd[:, t, bass.ds(h, 1)], None, ALU.mult)
                    last.then_inc(o_normed, 1)

                def low(h, b):
                    ve.wait_ge(o_hi, h + 1)
                    nc.vector.tensor_tensor(xs[:, bass.ds(2 * h, 2), T:2 * T], o_feat[:, b, :, :], xs[:, bass.ds(2 * h, 2), 0:T],
                                            ALU.subtract).then_inc(xs_ready, 1)
                scaled(0)
                scaled(1)
                with ve.Fori(0, 3) as i:
                    for b in range(2):
                        low(2 * i + b, b)
                        scaled(2 * i + (b + 2))
                low(6, 0)
                low(7, 1)

            def o_pair(i):
                for h in range(2):
                    for k in range(4):
                        lo(2 * i + (UNITS["o"] // 4 + h), k)
                        if first(i, h):
                            q_point(k, 7, 1)
                            if k == 3:
                                attention()
                                ve.wait_ge(xt_kept, 8)
                        else:
                            res_point(k, "o", 2 * i + (h - 1), 1 - h, B0 + G1)
            loop(ve, 4, o_pair)

            def up(phase, tail, ada):
                def four(i):
                    for p in range(2):
                        for h in range(2):
                            for k in range(4):
                                lo(4 * i + (UNITS[phase] // 4 + 2 * p + h), k)
                                if first(i, p + h):
                                    tail(k)
                                elif h == 0:
                                    v_up_point(k, phase, 2 * i + (p - 1), 1)
                                else:
                                    if not first(i, p):
                                        if k == 0:
                                            gate_pair(phase, 2 * i + (p - 1))
                                        if k == 1:
                                            low_pair(phase, 2 * i + (p - 1))
                                    g_point(k, phase, 2 * i + p, 0)
                                n = 8 * p + 4 * h + k
                                if ada(i):
                                    j = i + ADA_AT[phase]
                                    if n < 8:
                                        ada_chunk(j, n)
                                    if n == 13:
                                        ada_add(j)
                loop(ve, FT // 4, four)

            def down(phase, up_phase, gate, ada):
                def pair(i):
                    for h in range(2):
                        for k in range(12):
                            lo(6 * i + (UNITS[phase] // 4 + 3 * h + k // 4), k % 4, down_tiles(k)[1])
                            if ada:
                                ada_in_24(phase, i, 12 * h + k)
                            if first(i, h):
                                v_up_point(k, up_phase, FT // 2 - 1, 1)
                                if k == 4:
                                    gate_pair(up_phase, FT // 2 - 1)
                                if k == 5:
                                    low_pair(up_phase, FT // 2 - 1)
                            else:
                                res_point(k, phase, 2 * i + (h - 1), 1 - h, gate)
                loop(ve, 4, pair)

            def o_tail(k):
                res_point(k, "o", 7, 1, B0 + G1)
                if k == 3:
                    norm_tail(0)
            up("up0", o_tail, lambda i: True)
            down("dn0", "up0", B0 + G2, True)

            def sin_point(k, j, h, which):
                n = 3 * j + (SLABS["sin"] + which)
                if which == 0 and k == 2:
                    add_b(n, 2 * h, part_a[:, :, :])
                if which == 1:
                    if k == 2:
                        add_b(n, 2 * h, y[:, :, :])
                        ve.wait_ge(acc_read, n + 1)
                        nc.vector.tensor_tensor(y[:, :, :], y[:, :, :], part_a[:, :, :], ALU.mult).then_inc(gx_made, 1)
                    if k == 3:
                        taps("sin", j, 0, part_b)
                if which == 2:
                    if k == 2:
                        add_b(n, 2 * h, part_c[:, :, :])
                        ve.wait_ge(acc_read, n + 1)
                        ve.wait_ge(taps_done, j + (TAPS["sin"] + 1))
                        nc.vector.tensor_tensor(part_c[:, :, :], part_c[:, :, :], part_b[:, :, :], ALU.mult).then_inc(z_mul, 1)
                    if k == 3:
                        ve.wait_ge(z_hi_made, j + 1)
                        nc.vector.tensor_tensor(z[:, bass.ds(2 * j, 2), T:2 * T], part_c[:, :, :], z[:, bass.ds(2 * j, 2), 0:T],
                                                ALU.subtract).then_inc(z_made, 1)

            def sin_six(i):
                for n in range(6):
                    for k in range(4):
                        lo(6 * i + (UNITS["sin"] // 4 + n), k)
                        if first(i, n):
                            res_point(k, "dn0", 7, 1, B0 + G2)
                            if k == 3:
                                norm_tail(1)
                        elif n % 3 == 0:
                            sin_point(k, 2 * i + (n // 3 - 1), (n - 1) % 2, 2)
                        else:
                            sin_point(k, 2 * i + n // 3, (n - 1) % 2, n % 3 - 1)
                        ada_in_24("sin", i, 4 * n + k)
            loop(ve, 4, sin_six)

            def so_pair(i):
                for h in range(2):
                    for k in range(4):
                        lo(2 * i + (UNITS["so"] // 4 + h), k)
                        if first(i, h):
                            sin_point(k, 7, 1, 2)
                        else:
                            res_point(k, "so", 2 * i + (h - 1), 1 - h, B1 + G1)
            loop(ve, 4, so_pair)

            def so_tail(k):
                res_point(k, "so", 7, 1, B1 + G1)
                if k == 3:
                    norm_tail(2)
            up("up1", so_tail, lambda i: isinstance(i, int))
            down("dn1", "up1", B1 + G2, False)
            for k in range(4):
                res_point(k, "dn1", 7, 1, B1 + G2)
            norm_tail(3, final=True)

        @block.tensor
        def _(pe):
            mm = nc.tensor.matmul
            pe.wait_ge(ident_loaded, 16)
            pe.wait_ge(vecs_loaded, 16 * 19)
            for tile, n in enumerate((128, 118, 104, 104, 104, 88, 88, 88)):
                last = nc.tensor.transpose(ps[:, tile // 4, 128 * (tile % 4):128 * (tile % 4) + n], vec_rows[0:n, tile, :], ident[0:n, 0:n])
            last.then_inc(vecs_turned, 1)
            pe.wait_ge(ones_made, 1)
            pe.wait_ge(lam_multiplied, 1)
            mm(ps[:, 6, 0:2], ones[:, :], lam_prod[:, :], start=True, stop=True).then_inc(lam_summed, 1)

            pe.wait_ge(cond_made, 1)

            def mod_products(g, b):
                wait(pe, mod_copied, 2 * g + (b - 1))
                for q in range(8):
                    pe.wait_ge(start_full[q % 4], 64 * g + 16 * (2 * b + q // 4 + 1))
                    for t in range(2):
                        last = mm(ps[0:2, 2 + b, :], cond[:, :, 2 * q + t], start_ring[:, q % 4, t, :],
                                  start=(q == 0 and t == 0), stop=(q == 7 and t == 1))
                    last.then_inc(start_used, 1)

            def mod_turn(n, b):
                pe.wait_ge(mod_copied, n + 1)
                wait(pe, mod_made, n - 1)
                for t in range(4):
                    last = nc.tensor.transpose(ps[:, 4 + b, 2 * t:2 * t + 2], mod_rows[:, b, P * t:P * t + P], ident[0:2, 0:2])
                last.then_inc(mod_turned, 1)

            def first_modulation(g):
                mod_products(g, 0)
                if g > 0:
                    mod_turn(2 * g - 1, 1)
                mod_products(g, 1)
                mod_turn(2 * g, 0)
            first_modulation(0)
            pe.wait_ge(vecs_made, 1)
            for n, tok in enumerate((x_tok, ctx_tok)):
                pe.wait_ge(rows_normed, 2 * n + 2)

                for i in range(8):
                    wait(pe, xn_kept, 8 * n + i - 1)
                    for k in range(2):
                        for t in range(2):
                            last = nc.tensor.transpose(ps[:, i % 2, T * k + P * t:T * k + P * t + P],
                                                       tok[:, t, P * (2 * i + k):P * (2 * i + k) + P], ident[:, :])
                    last.then_inc(xn_turned, 1)
            for g in range(1, 4):
                first_modulation(g)
            mod_turn(7, 1)

            def unit(quad, slot, bank, src, tile, n_tiles, is_first, is_last):
                pe.wait_ge(lo_made, 4 * quad + (slot + 1))
                for t in range(n_tiles):
                    for m in range(2):
                        cols = slice(P * m, P * m + P)
                        mm(ps[:, bank + m, :], w_hi[:, slot, t, cols], src[:, tile + t, :],
                           start=(is_first and t == 0), stop=False)
                        last = mm(ps[:, bank + m, 0:T], w_lo[:, slot, t, cols], src[:, tile + t, 0:T],
                                  start=False, stop=(is_last and t == n_tiles - 1))
                last.then_inc(w_used, 1)

            def ada_reduce(j):
                pe.wait_ge(ada_step, 16 * j + 16)
                wait(pe, ada_added, j)
                for t in range(4):
                    last = mm(ps[:, 6, t:t + 1], ada_sum[:, P * t:P * t + P], ones[:, 0:1], start=True, stop=True)
                last.then_inc(ada_reduced, 1)

            def sum_squares(n, is_first, is_last):
                pe.wait_ge(sq_made, n + 1)
                for m in range(2):
                    last = mm(ps[:, 7, 0:T], ones[:, :], part_c[:, m, :], start=(is_first and m == 0), stop=(is_last and m == 1))
                last.then_inc(sq_used, 1)

            first = lambda i, h: isinstance(i, int) and h == 0

            def k_pair(i):
                for h in range(2):
                    for k in range(4):
                        if first(i, h):
                            pe.wait_ge(xs_ready, 2 * (k + 1))
                        if k == 0:
                            wait(pe, acc_read, 2 * i + h)
                        pe.wait_ge(lo_made, 8 * i + (4 * h + k + 1))
                        for t in range(4):
                            for m in range(2):
                                cols = slice(P * m, P * m + P)
                                for n, src in enumerate((xs, cs)):
                                    mm(ps[:, 2 * n + m, :], w_hi[:, k, t, cols], src[:, 4 * k + t, :], start=(k == 0 and t == 0), stop=False)
                                for n, src in enumerate((xs, cs)):
                                    last = mm(ps[:, 2 * n + m, 0:T], w_lo[:, k, t, cols], src[:, 4 * k + t, 0:T], start=False, stop=(k == 3 and t == 3))
                        last.then_inc(w_used, 1)
                        if h == 1 and k == 0:
                            ada_reduce(i + ADA_AT["k"])
            loop(pe, 4, k_pair)

            def v_pair(i):
                for h in range(2):
                    for k in range(4):
                        if k == 0:
                            pe.wait_ge(acc_read, 2 * i + (SLABS["v"] + h))
                        pe.wait_ge(lo_made, 8 * i + (UNITS["v"] + 4 * h + k + 1))
                        for t in range(4):
                            for n in range(4):
                                src, tok = (xs, cs)[n // 2], P * (n % 2)
                                x_hi, x_lo = src[:, 4 * k + t, tok:tok + P], src[:, 4 * k + t, T + tok:T + tok + P]
                                mm(ps[:, n, 0:SLAB], x_hi, w_hi[:, k, t, :], start=(k == 0 and t == 0), stop=False)
                                mm(ps[:, n, 0:SLAB], x_hi, w_lo[:, k, t, :], start=False, stop=False)
                                last = mm(ps[:, n, 0:SLAB], x_lo, w_hi[:, k, t, :], start=False, stop=(k == 3 and t == 3))
                        last.then_inc(w_used, 1)
                        if h == 1 and k == 0:
                            ada_reduce(i + ADA_AT["v"])
            loop(pe, 4, v_pair)

            def q_pair(i):
                for h in range(2):
                    if first(i, h):
                        pe.wait_ge(acc_read, SLABS["q"])
                    elif not first(i, h - 1):
                        pe.wait_ge(acc_read, 2 * i + (SLABS["q"] + h - 1))
                    for k in range(4):
                        unit(2 * i + (UNITS["q"] // 4 + h), k, 2 * h, xs, 4 * k, 4, k == 0, k == 3)
                        if h == 1 and k == 0:
                            ada_reduce(i + ADA_AT["q"])
            loop(pe, 4, q_pair)

            def attention():
                def scores(h):
                    pe.wait_ge(qh_made, h + 1)
                    for n in range(4):
                        wait(pe, exp_done, 4 * h + (n - 3))
                        mm(ps[:, n, :], q_head[:, n % 2, P * (n // 2):P * (n // 2) + P],
                           k_t[:, bass.ds(2 * h + n % 2, 1), :], start=True, stop=True).then_inc(scores_made, 1)

                def weigh(h):
                    for t in range(2):
                        pe.wait_ge(a_made, 2 * h + (t + 1))
                        wait(pe, at_copied, 2 * h + (t - 1))
                        for k in range(4):
                            last = nc.tensor.transpose(ps[:, 4 + t, P * k:P * k + P], probs[:, 2 * t, P * k:P * k + P], ident[:, :])
                        last.then_inc(at_made, 1)
                    for t in range(2):
                        pe.wait_ge(at_copied, 2 * h + (t + 1))
                        wait(pe, o_copied, 2 * h + (t - 1))
                        for k in range(4):
                            last = mm(ps[:, 6 + t, 0:T], a_t[:, t, P * k:P * k + P],
                                      v_rows[:, k, bass.ds(T * h, T)], start=(k == 0), stop=(k == 3))
                        last.then_inc(o_made, 1)

                pe.wait_ge(rope_done, 16)
                pe.wait_ge(acc_read, SLABS["o"])
                scores(0)
                scores(1)
                weigh(0)
                with pe.Fori(1, HEADS - 1) as h:
                    scores(h + 1)
                    weigh(h)
                weigh(HEADS - 1)

                for h in range(HEADS):
                    pe.wait_ge(o_normed, h + 1)
                    wait(pe, o_gained, h - 1)
                    for m in range(2):
                        for t in range(2):
                            last = nc.tensor.transpose(ps[:, h % 2, T * m + P * t:T * m + P * t + P],
                                                       o_rows[:, t, T * h + P * m:T * h + P * m + P], ident[:, :])
                    last.then_inc(o_turned, 1)
                pe.wait_ge(xt_loaded, 16)
                for n in range(8):
                    wait(pe, xt_kept, n - 1)
                    for k in range(2):
                        for t in range(2):
                            last = nc.tensor.transpose(ps[:, 4 + n % 2, T * k + P * t:T * k + P * t + P],
                                                       x_tok[:, t, P * (2 * n + k):P * (2 * n + k) + P], ident[:, :])
                    last.then_inc(xt_turned, 1)
            attention()

            def narrow(phase, i, src, n_ready=None, squares_at=None, ready=None):
                for h in range(2):
                    if not first(i, h) and not first(i, h - 1):
                        pe.wait_ge(acc_read, 2 * i + (SLABS[phase] + h - 1))
                    if first(i, h - 1):
                        pe.wait_ge(acc_read, SLABS[phase])
                    for k in range(4):
                        if first(i, h) and ready:
                            ready(k)
                        unit(2 * i + (UNITS[phase] // 4 + h), k, 2 * h, src, 4 * k, 4, k == 0, k == 3)
                    if not first(i, h):
                        sum_squares(2 * i + (RES[phase] + h - 1), first(i, h - 1), False)

            def all_heads(k):
                pe.wait_ge(xs_ready, 8 + 2 * (k + 1))
                if k == 0:
                    pe.wait_ge(o_gained, 8)
            loop(pe, 4, lambda i: narrow("o", i, xs, ready=all_heads))

            def up(phase, n_ready, res_phase, ada):
                sum_squares(RES[res_phase] + 7, False, True)

                def four(i):
                    for p in range(2):
                        for h in range(2):
                            g = 2 * p + h
                            if first(i, g) or first(i, g - 1):
                                pe.wait_ge(acc_read, SLABS[phase])
                            else:
                                pe.wait_ge(acc_read, 4 * i + (SLABS[phase] + g - 1))
                            for k in range(4):
                                if first(i, g):
                                    pe.wait_ge(xs_ready, n_ready + 2 * (k + 1))
                                unit(4 * i + (UNITS[phase] // 4 + g), k, 2 * h, xs, 4 * k, 4, k == 0, k == 3)
                                if ada(i) and 4 * g + k == 9:
                                    ada_reduce(i + ADA_AT[phase])
                loop(pe, FT // 4, four)

            def down(phase, ada):
                def pair(i):
                    for h in range(2):
                        if first(i, h) or first(i, h - 1):
                            pe.wait_ge(acc_read, SLABS[phase] + h - 1)
                        else:
                            pe.wait_ge(acc_read, 2 * i + (SLABS[phase] + h - 1))
                        for k in range(12):
                            tile, n = down_tiles(k)
                            if first(i, h) and k in (0, 11):
                                pe.wait_ge(act_made, PAIRS_END[phase] - (1 if k == 0 else 0))
                            unit(6 * i + (UNITS[phase] // 4 + 3 * h + k // 4), k % 4, 2 * h, act, tile, n, k == 0, k == 11)
                            if k == 4 and not first(i, h):
                                sum_squares(2 * i + (RES[phase] + h - 1), first(i, h - 1), False)
                            if ada and 12 * h + k == 8:
                                ada_reduce(2 * i + ADA_AT[phase])
                            if ada and 12 * h + k == 20:
                                ada_reduce(2 * i + (ADA_AT[phase] + 1))
                loop(pe, 4, pair)

            up("up0", 16, "o", lambda i: True)
            down("dn0", True)
            sum_squares(RES["dn0"] + 7, False, True)

            def sin_six(i):
                for n in range(6):
                    if first(i, n) or first(i, n - 1):
                        pe.wait_ge(acc_read, SLABS["sin"])
                    else:
                        pe.wait_ge(acc_read, 6 * i + (SLABS["sin"] + n - 1))
                    for k in range(4):
                        if first(i, n):
                            pe.wait_ge(xs_ready, 24 + 2 * (k + 1))
                        unit(6 * i + (UNITS["sin"] // 4 + n), k, 2 * (n % 2), xs, 4 * k, 4, k == 0, k == 3)
                        if 4 * n + k == 8:
                            ada_reduce(2 * i + ADA_AT["sin"])
                        if 4 * n + k == 20:
                            ada_reduce(2 * i + (ADA_AT["sin"] + 1))
            loop(pe, 4, sin_six)

            def z_ready(k):
                pe.wait_ge(z_made, 8 if k == 3 else 7)
                if k == 0:
                    pe.wait_ge(acc_read, SLABS["so"] - 1)
            loop(pe, 4, lambda i: narrow("so", i, z, ready=z_ready))

            up("up1", 32, "so", lambda i: isinstance(i, int))
            down("dn1", False)
            sum_squares(RES["dn1"] + 7, False, True)

            for n in range(8):
                pe.wait_ge(xh_made, 24 + n + 1)
                wait(pe, fin_kept, n - 1)
                part = (part_a, part_b)[n % 2]
                for t in range(2):
                    for m in range(2):
                        last = nc.tensor.transpose(ps[:, n % 2, T * t + P * m:T * t + P * m + P], part[:, m, P * t:P * t + P], ident[:, :])
                last.then_inc(fin_turned, 1)


RES = {"o": 0, "dn0": 8, "so": 16, "dn1": 24}
TAPS = {"up0": 0, "sin": 44, "up1": 52}
PAIRS = {"up0": 0, "up1": 22}
PAIRS_END = {"dn0": 22, "dn1": 44}


def tap_column(phase, which, m, tap):
    if phase == "sin":
        return SCONV + KT * tap + m
    return CONV[0 if phase == "up0" else 1] + 2 * FT * tap + FT * which + m


_INS = ["x", "c", "ctx", "c_ctx", "w_ada", "b_ada", "attn_w_qkv", "attn_w_o", "attn_lambda_q1", "attn_lambda_k1",
        "attn_lambda_q2", "attn_lambda_k2", "attn_subln_gain", "sconv_w_in", "sconv_conv", "sconv_w_out",
        "ffn_w_up", "ffn_conv", "ffn_w_down", "final_gain"]


def _rope_tables(np):
    half = HEAD_DIM // 2
    inv = (1.0 / (np.float32(10000.0) ** (np.arange(0, half, 2, dtype=np.float32) / np.float32(half)))).astype(np.float32)
    row = np.repeat(np.arange(T // GRID_W, dtype=np.float32), GRID_W)
    col = np.tile(np.arange(GRID_W, dtype=np.float32), T // GRID_W)
    ang_r, ang_c = inv[:, None] * row[None, :], inv[:, None] * col[None, :]
    ang = np.concatenate([ang_r, ang_r, ang_c, ang_c], axis=0)
    sign = np.repeat(np.array([-1, 1, -1, 1], np.float32), 32)[:, None]
    return np.cos(ang).astype(np.float32), (sign * np.sin(ang)).astype(np.float32)


def kernel(**inputs):
    import numpy as _np
    import concourse.bacc as _bacc
    from concourse import mybir as _mybir
    from concourse.bass_utils import run_bass_kernel_spmd as _run

    nc = _bacc.Bacc("TRN2", target_bir_lowering=False, num_devices=1)
    arrays, args = {}, []

    def give(name, a):
        arrays[f"in_{name}_dram"] = a
        args.append(nc.dram_tensor(f"in_{name}_dram", a.shape, _mybir.dt.from_np(a.dtype), kind="ExternalInput").ap())

    for name in _INS:
        give(name, _np.ascontiguousarray(inputs[name]))
    cos, sin = _rope_tables(_np)
    give("ident", _np.eye(P, dtype=_np.float32))
    give("rope_cos", cos)
    give("rope_sin", sin)
    o = nc.dram_tensor("out_0_dram", (1, T, D), _mybir.dt.float32, kind="ExternalOutput").ap()
    program(nc, *args, o)
    r = _run(nc, [arrays], core_ids=[0])
    return r.results[0]["out_0_dram"]
```

```python
import concourse.bass as bass
from concourse import mybir
from contextlib import ExitStack
import math

F32 = mybir.dt.float32
F32R = mybir.dt.float32r
ACT = mybir.ActivationFunctionType
ALU = mybir.AluOpType
AX_X = mybir.AxisListType.X

P = 128
D = 2048
T = 256
KT = D // P
HEADS = 8
QK = 2048
D_FF = 5632
FT = D_FF // P
GRID_W = 64
HEAD_DIM = 128
SCALE = HEAD_DIM ** -0.5
EPS = 1e-6
LAM_INIT = 0.8 - 0.6 * math.exp(-0.3 * 0)
SLAB = 256
RING = 4
KU = 4
ADA_COLS = 512
ADA_SLABS = 6 * D // ADA_COLS
ADA_FIRST = 2 * D // ADA_COLS
ADA_SLOTS, ADA_SLOTS_KV = 2, 4

PHASES = {"k": (8, 4), "v": (8, 4), "q": (8, 4), "o": (8, 4), "up0": (44, 4), "dn0": (8, 12),
          "sin": (24, 4), "so": (8, 4), "up1": (44, 4), "dn1": (8, 12)}
UNITS, SLABS = {}, {}
_u = _s = 0
for _name, (_slabs, _units) in PHASES.items():
    UNITS[_name], SLABS[_name] = _u, _s
    _u += _slabs * _units
    _s += _slabs

B0, B1, COND, FGAIN, SUBLN, LAMB = 0, 96, 192, 224, 240, 242
CONV = (246, 246 + 3 * 88 + 3 * 16)
SCONV = 246 + 3 * 88
VECS = 246 + 3 * 88 + 3 * 16 + 3 * 88
SH1, SC1, G1, SH2, SC2, G2 = (16 * n for n in range(6))

ADA_AT = {"k": 0, "v": 8, "up0": 16, "dn0": 20, "sin": 28, "up1": 36}


def down_tiles(k):
    return (4 * k, 4) if k < 8 else (32 + 3 * (k - 8), 3)


def program(nc, x, c, ctx_in, c_ctx, w_ada, b_ada, w_qkv, w_o, lq1, lk1, lq2, lk2, subln, w_in, conv_in,
            w_out, w_up, conv_ffn, w_down, final_gain, ident_in, rope_cos_in, rope_sin_in, out):
    tiles = lambda w: w.rearrange("(t p) n -> p t n", p=P)
    qkv_w, o_w, in_w, out_w = tiles(w_qkv[0]), tiles(w_o[0]), tiles(w_in[0]), tiles(w_out[0])
    up_w, dn_w = [tiles(w_up[l]) for l in range(2)], [tiles(w_down[l]) for l in range(2)]
    ada_w = [tiles(w_ada[l]) for l in range(2)]
    x_rows = x[0].rearrange("(t p) n -> p t n", p=P)
    ctx_rows = ctx_in[0].rearrange("(t p) n -> p t n", p=P)
    out_rows = out[0].rearrange("(t p) n -> p t n", p=P)

    with ExitStack() as scope:
        KB = 1024
        start = (nc.sbuf_base + 63) // 64 * 64
        at_x = start
        at_u = at_x + 32 * KB
        at_res = at_u + 96 * KB
        at_raw = at_res + 16 * KB
        at_hi = at_raw + 16 * KB
        at_lo = at_hi + 16 * KB
        at_ada = at_lo + 16 * KB
        at_small = at_ada + 10 * KB
        small = [at_small]

        def at(name, shape, dt, offset):
            return nc.alloc_sbuf_tensor_at(name, shape, dt, offset=offset)

        def little(name, shape, dt=F32):
            n = 4
            for k in shape[1:]:
                n *= k
            n = (n + 31) // 32 * 32
            t = at(name, shape, dt, small[0])
            small[0] += n
            return t

        xs = at("xs", [P, KT, 2 * T], F32R, at_x)
        res = at("res", [P, KT, T], F32, at_res)
        raw = at("raw", [P, RING, KU, SLAB], F32, at_raw)
        w_hi = at("w_hi", [P, RING, KU, SLAB], F32R, at_hi)
        w_lo = at("w_lo", [P, RING, KU, SLAB], F32R, at_lo)
        ada_ring = at("ada_ring", [P, 2, 2, ADA_COLS], F32, at_ada)
        ada_sum = at("ada_sum", [P, ADA_COLS], F32, at_ada + 8 * KB)
        ada_sum_b = at("ada_sum_b", [P, ADA_COLS], F32, at_res + 6 * KB)
        ada_ring_kv = at("ada_ring_kv", [P, 2, 2, ADA_COLS], F32, at_res + 8 * KB)
        ada_slot = lambda n: ada_ring[:, n, :, :] if n < ADA_SLOTS else ada_ring_kv[:, n - ADA_SLOTS, :, :]
        x_tok = at("x_tok", [P, 2, D], F32, at_u)
        ctx_tok = at("ctx_tok", [P, 2, D], F32, at_u + 16 * KB)
        xn_l = at("xn_l", [P, KT, T], F32, at_res)
        xn_c = at("xn_c", [P, KT, T], F32, at_u + 32 * KB)
        start_ring = at("start_ring", [P, 4, 2, ADA_COLS], F32, at_u + 48 * KB)
        vec_rows = at("vec_rows", [P, 8, P], F32, at_hi)
        mod_rows = at("mod_rows", [2, 2, ADA_COLS], F32, at_hi + 4 * KB)
        squares = at("squares", [P, D], F32, at_lo)
        k_t = at("k_t", [P, 2 * HEADS, 2 * T], F32, at_u)
        v_rows = at("v_rows", [P, 4, D], F32, at_u + 32 * KB)
        cs = at("cs", [P, KT, 2 * T], F32R, at_u + 64 * KB)
        attn = at_u + 64 * KB
        probs = at("probs", [P, 4, 512], F32, attn)
        a_t = at("a_t", [P, 2, 512], F32, attn + 8 * KB)
        q_head = at("q_head", [P, 2, T], F32, attn + 12 * KB)
        o_square = at("o_square", [P, T], F32, attn + 14 * KB)
        q_t = at("q_t", [P, 2 * HEADS, T], F32, attn + 16 * KB)
        o_rows = at("o_rows", [P, 2, D], F32, at_res)
        o_feat = at("o_feat", [P, 2, 2, T], F32, attn)
        y_qk = at("y_qk", [P, 2, T], F32, at_res)
        rot = at("rot", [P, 2, T], F32, at_res + 2 * KB)
        rope_cos = at("rope_cos", [P, T], F32, at_res + 4 * KB)
        rope_sin = at("rope_sin", [P, T], F32, at_res + 5 * KB)
        act = at("act", [P, FT, 2 * T], F32R, at_u)
        z = at("z", [P, KT, 2 * T], F32R, at_u)
        y = at("y", [P, 2, T], F32, at_u + 88 * KB)
        part_a = at("part_a", [P, 2, T], F32, at_u + 90 * KB)
        part_b = at("part_b", [P, 2, T], F32, at_u + 92 * KB)
        part_c = at("part_c", [P, 2, T], F32, at_u + 94 * KB)
        out_tok = at("out_tok", [P, 2, D], F32, at_x)
        ident = little("ident", [P, P])
        ones = little("ones", [P, P])
        vec = little("vec", [P, VECS])
        cond = little("cond", [P, 2, KT])
        ctx_mod = little("ctx_mod", [P, 32])
        row_sum = little("row_sum", [P, 4])
        row_var = little("row_var", [P, 4])
        row_inv = little("row_inv", [P, 4])
        row_rstd = little("row_rstd", [P, 4])
        lam_prod = little("lam_prod", [P, 2])
        lam_exp = little("lam_exp", [P, 2])
        neg_lam = little("neg_lam", [P, 1])
        gain_o = little("gain_o", [P, 2])
        s_max = little("s_max", [P, 4])
        s_neg = little("s_neg", [P, 4])
        s_sum = little("s_sum", [P, 4])
        s_inv = little("s_inv", [P, 4])
        s_lam = little("s_lam", [P, 2])
        o_sum = little("o_sum", [P, 2, HEADS])
        o_inv = little("o_inv", [P, 2, HEADS])
        o_rstd = little("o_rstd", [P, 2, HEADS])
        assert small[0] <= nc.sbuf_usable_end, (small[0], nc.sbuf_usable_end)

        ps = scope.enter_context(nc.psum_tensor("ps", [P, 8, 512], F32))

        sem = lambda name: scope.enter_context(nc.semaphore(name))
        vecs_loaded, ident_loaded, x_loaded, ctx_loaded = sem("vecs_loaded"), sem("ident_loaded"), sem("x_loaded"), sem("ctx_loaded")
        rope_loaded = sem("rope_loaded")
        start_full = [sem(f"start_full{n}") for n in range(4)]
        start_used = sem("start_used")
        ones_made, vecs_turned, vecs_made, plus_one = sem("ones_made"), sem("vecs_turned"), sem("vecs_made"), sem("plus_one")
        cond_made, lam_multiplied, lam_summed, lam_exped, lam_part, lam_made = (
            sem("cond_made"), sem("lam_multiplied"), sem("lam_summed"), sem("lam_exped"), sem("lam_part"), sem("lam_made"))
        rows_squared, rows_var, rows_inv, rows_rstd, rows_normed = (
            sem("rows_squared"), sem("rows_var"), sem("rows_inv"), sem("rows_rstd"), sem("rows_normed"))
        xn_turned, xn_kept = sem("xn_turned"), sem("xn_kept")
        mod_copied, mod_turned, mod_made, h_made, h_hi = (
            sem("mod_copied"), sem("mod_turned"), sem("mod_made"), sem("h_made"), sem("h_hi"))
        raw_full = [sem(f"raw_full{n}") for n in range(RING)]
        hi_made, lo_made, w_used = sem("hi_made"), sem("lo_made"), sem("w_used")
        ada_full = [sem(f"ada_full{n}") for n in range(ADA_SLOTS_KV)]
        ada_step, ada_reduced, ada_added = sem("ada_step"), sem("ada_reduced"), sem("ada_added")
        a_copied, acc_read = sem("a_copied"), sem("acc_read")
        ctx_copied, ctx_read = sem("ctx_copied"), sem("ctx_read")
        xs_ready = sem("xs_ready")
        rot_made, rope_part, rope_done = sem("rot_made"), sem("rope_part"), sem("rope_done")
        taps_mid, taps_first, taps_done = sem("taps_mid"), sem("taps_first"), sem("taps_done")
        silu_made, gated, act_hi_made, act_made = sem("silu_made"), sem("gated"), sem("act_hi_made"), sem("act_made")
        gx_made, z_mul, z_hi_made, z_made = sem("gx_made"), sem("z_mul"), sem("z_hi_made"), sem("z_made")
        res_made, sq_made, sq_added, sq_used = sem("res_made"), sem("sq_made"), sem("sq_added"), sem("sq_used")
        var_made, inv_made, rstd_made, xm_made, xh_made, xh_hi = (
            sem("var_made"), sem("inv_made"), sem("rstd_made"), sem("xm_made"), sem("xh_made"), sem("xh_hi"))
        qh_made, scores_made, max_made, neg_made, exp_done = (
            sem("qh_made"), sem("scores_made"), sem("max_made"), sem("neg_made"), sem("exp_done"))
        sum_inv, lam_scaled, p1_scaled, a_made = sem("sum_inv"), sem("lam_scaled"), sem("p1_scaled"), sem("a_made")
        at_made, at_copied, o_made, o_copied, o_squared = (
            sem("at_made"), sem("at_copied"), sem("o_made"), sem("o_copied"), sem("o_squared"))
        o_var, o_inverted, o_root, o_normed, o_turned, o_gained, o_hi = (
            sem("o_var"), sem("o_inverted"), sem("o_root"), sem("o_normed"), sem("o_turned"), sem("o_gained"), sem("o_hi"))
        xt_turned, xt_kept, xt_loaded = sem("xt_turned"), sem("xt_kept"), sem("xt_loaded")
        fin_gained, fin_turned, fin_kept, fin_stored = sem("fin_gained"), sem("fin_turned"), sem("fin_kept"), sem("fin_stored")
        fin_scaled = [sem("fin_scaled0"), sem("fin_scaled1")]

        block = scope.enter_context(nc.Block())

        def wait(eng, s, n):
            if isinstance(n, int) and n <= 0:
                return
            eng.wait_ge(s, n)

        def loop(eng, n, body):
            body(0)
            if n > 1:
                with eng.Fori(1, n) as i:
                    body(i)

        def up_loop(eng, body):
            body(0, True)
            with eng.Fori(1, 4) as i:
                body(i, True)
            with eng.Fori(4, FT // 4) as i:
                body(i, False)

        @block.sync
        def _(sp):
            def first_modulation(g, back=0):
                for half, first in ((0, SC1 * P), (1, SH1 * P)):
                    for q in range(8):
                        n = 16 * g + (8 * half + q - 16 * back)
                        wait(sp, start_used, n - 3)
                        sp.dma_start(start_ring[:, q % 4, :, :],
                                     ada_w[0][:, 2 * q:2 * q + 2, bass.ds(g * ADA_COLS + (first - back * ADA_COLS), ADA_COLS)]
                                     ).then_inc(start_full[q % 4], 16)

            first_modulation(0)
            with sp.Fori(2, 5) as g:
                first_modulation(g, 1)

            def load(quad, slot, w, tile, n_tiles, col):
                wait(sp, lo_made, 4 * quad + slot - 3)
                sp.dma_start(raw[:, slot, 0:n_tiles, :], w[:, tile:tile + n_tiles, bass.ds(col, SLAB)]
                             ).then_inc(raw_full[slot], 16)

            def k_slab(s):
                for k in range(4):
                    load(s + UNITS["k"] // 4, k, qkv_w, 4 * k, 4, s * SLAB + QK)
            loop(sp, 8, k_slab)

            def plain(phase, w, base):
                with sp.Fori(0, 8) as s:
                    for k in range(4):
                        load(s + UNITS[phase] // 4, k, w, 4 * k, 4, s * SLAB + base)

            def up(phase, w):
                with sp.Fori(0, FT // 2) as j:
                    for h in range(2):
                        for k in range(4):
                            load(2 * j + (UNITS[phase] // 4 + h), k, w, 4 * k, 4, j * SLAB + h * D_FF)

            def down(phase, w):
                with sp.Fori(0, 8) as s:
                    for k in range(12):
                        tile, n = down_tiles(k)
                        load(3 * s + (UNITS[phase] // 4 + k // 4), k % 4, w, tile, n, s * SLAB)

            plain("v", qkv_w, 2 * QK)
            plain("q", qkv_w, 0)
            plain("o", o_w, 0)
            up("up0", up_w[0])
            down("dn0", dn_w[0])
            with sp.Fori(1, 9) as n:
                for h, first in ((0, D), (1, 2 * D), (2, 0)):
                    for k in range(4):
                        load(3 * n + (UNITS["sin"] // 4 + h - 3), k, in_w, 4 * k, 4, n * SLAB + (first - SLAB))
            plain("so", out_w, 0)
            up("up1", up_w[1])
            down("dn1", dn_w[1])
            for t in range(2):
                sp.wait_ge(fin_scaled[t], 1)
                sp.dma_start(out_rows[:, t, :], out_tok[:, t, :]).then_inc(fin_stored, 16)
            sp.wait_ge(fin_stored, 32)

        @block.gpsimd
        def _(pool):
            nc.gpsimd.memset(ones[:, :], 1.0).then_inc(ones_made, 1)

            def ada_slab(j, layer, col, slots=ADA_SLOTS):
                for q in range(8):
                    if isinstance(j, int) and q == 2:
                        pool.wait_ge(xs_ready, 8)
                    wait(pool, ada_step, 16 * j + (2 * q + 2 - 2 * slots))
                    pool.dma_start(ada_slot(q % slots),
                                   ada_w[layer][:, 2 * q:2 * q + 2, bass.ds(col, ADA_COLS)]
                                   ).then_inc(ada_full[q % slots], 16)
                    if isinstance(j, int) and q == 3:
                        pool.dma_start(rope_cos[:, :], rope_cos_in).then_inc(rope_loaded, 16)
                        pool.dma_start(rope_sin[:, :], rope_sin_in).then_inc(rope_loaded, 16)

            loop(pool, 16, lambda j: ada_slab(j, 0, j * ADA_COLS + ADA_FIRST * ADA_COLS, ADA_SLOTS_KV))
            pool.wait_ge(scores_made, 4 * HEADS)
            pool.dma_start(x_tok[:, :, :], x_rows).then_inc(xt_loaded, 16)
            with pool.Fori(16, 40) as j:
                ada_slab(j, 1, j * ADA_COLS + (-16 * ADA_COLS))

        @block.scalar
        def _(se):
            se.dma_start(ident[:, :], ident_in).then_inc(ident_loaded, 16)
            rows = lambda v: v.rearrange("(t p) -> t p", p=P)
            r = vec_rows
            loads = [(r[0:96, 0, :], rows(b_ada[0])), (r[96:112, 0, :], rows(c[0])), (r[112:128, 0, :], rows(c_ctx)),
                     (r[0:96, 1, :], rows(b_ada[1])), (r[96:112, 1, :], rows(final_gain)),
                     (r[112:114, 1, :], rows(subln[0])), (r[114:115, 1, :], lq1), (r[115:116, 1, :], lk1),
                     (r[116:117, 1, :], lq2), (r[117:118, 1, :], lk2)]
            for n in range(3):
                loads += [(r[0:88, 2 + n, :], rows(conv_ffn[0, n])), (r[88:104, 2 + n, :], rows(conv_in[0, n])),
                          (r[0:88, 5 + n, :], rows(conv_ffn[1, n]))]
            for dst, src in loads:
                se.dma_start(dst, src).then_inc(vecs_loaded, 16)
            assert len(loads) == 19
            se.dma_start(x_tok[:, :, :], x_rows).then_inc(x_loaded, 16)
            se.dma_start(ctx_tok[:, :, :], ctx_rows).then_inc(ctx_loaded, 16)

            se.wait_ge(vecs_made, 1)
            nc.scalar.activation(cond[:, :, :], vec[:, COND:COND + 32].rearrange("p (c k) -> p c k", c=2), ACT.Silu).then_inc(cond_made, 1)
            se.wait_ge(lam_summed, 1)
            nc.scalar.activation(lam_exp[:, :], ps[:, 6, 0:2], ACT.Exp).then_inc(lam_exped, 1)
            for n, (loaded, tok) in enumerate(((x_loaded, x_tok), (ctx_loaded, ctx_tok))):
                se.wait_ge(loaded, 16)
                for t in range(2):
                    wait(se, rows_squared, 2 * n + t)
                    nc.scalar.activation(squares[:, :], tok[:, t, :], ACT.Square,
                                         accum_out=row_sum[:, 2 * n + t:2 * n + t + 1]).then_inc(rows_squared, 1)
            se.wait_ge(rows_inv, 1)
            nc.scalar.activation(row_rstd[:, :], row_inv[:, :], ACT.Sqrt).then_inc(rows_rstd, 1)

            def first_modulation(g):
                for b in range(2):
                    n = 2 * g + b
                    wait(se, start_used, 8 * n + 8)
                    wait(se, mod_turned, n - 1)
                    nc.scalar.activation(mod_rows[:, b, :], ps[0:2, 2 + b, :], ACT.Copy).then_inc(mod_copied, 1)
                se.wait_ge(mod_made, 2 * g + 2)
                if isinstance(g, int):
                    se.wait_ge(xn_kept, 16)
                for m, (xn, dst) in enumerate(((xn_l, xs), (xn_c, cs))):
                    table = ctx_mod if m else vec
                    for k in range(4):
                        last = nc.scalar.activation(
                            xn[:, bass.ds(4 * g + k, 1), :], xn[:, bass.ds(4 * g + k, 1), :], ACT.Identity,
                            scale=table[:, bass.ds(4 * g + (SC1 + k), 1)], bias=table[:, bass.ds(4 * g + (SH1 + k), 1)])
                    last.then_inc(h_made, 1)
                    se.wait_ge(h_made, 2 * g + (m + 1))
                    nc.scalar.activation(dst[:, bass.ds(4 * g, 4), 0:T], xn[:, bass.ds(4 * g, 4), :], ACT.Copy).then_inc(h_hi, 1)
            loop(se, 4, first_modulation)

            def hi(quad, slot, n_tiles=KU):
                se.wait_ge(raw_full[slot], 16 * quad + 16)
                wait(se, w_used, 4 * quad + slot - 3)
                nc.scalar.activation(w_hi[:, slot, 0:n_tiles, :], raw[:, slot, 0:n_tiles, :], ACT.Copy).then_inc(hi_made, 1)

            def copy_a(phase, s, bank, dst, per_slab=4):
                se.wait_ge(w_used, per_slab * s + (UNITS[phase] + per_slab))
                nc.scalar.activation(dst, ps[:, bank:bank + 2, 0:T], ACT.Copy).then_inc(a_copied, 1)

            def rotate(n):
                se.wait_ge(acc_read, n + 1)
                for d in range(4):
                    last = nc.scalar.activation(rot[32 * d:32 * d + 32, :, :], y_qk[32 * (d ^ 1):32 * (d ^ 1) + 32, :, :], ACT.Copy)
                last.then_inc(rot_made, 1)

            def k_point(k, s, h):
                if k == 2:
                    se.wait_ge(w_used, 4 * s + (UNITS["k"] + 4))
                    nc.scalar.activation(k_t[:, bass.ds(2 * s, 2), T:2 * T], ps[:, 2:4, 0:T], ACT.Copy).then_inc(ctx_copied, 1)
                    wait(se, rope_done, s)
                    copy_a("k", s, 4 * h, y_qk[:, :, :])
                if k == 3:
                    rotate(s + SLABS["k"])

            def v_point(k, s, h):
                if k == 2:
                    copy_a("v", s, 4 * h, v_rows[:, 0:2, bass.ds(s * SLAB, SLAB)])

            def q_point(k, s, h):
                if k == 2:
                    se.wait_ge(rope_done, s + 8)
                    copy_a("q", s, 2 * h, y_qk[:, :, :])
                if k == 3:
                    rotate(s + SLABS["q"])

            def res_point(k, phase, s, h, n_res, per_slab=4):
                if k == 2:
                    wait(se, res_made, s + n_res)
                    copy_a(phase, s, 2 * h, y[:, :, :], per_slab)
                if k == 3:
                    se.wait_ge(res_made, s + (n_res + 1))
                    wait(se, sq_added, s + n_res)
                    nc.scalar.activation(part_c[:, :, :], res[:, bass.ds(2 * s, 2), :], ACT.Square).then_inc(sq_made, 1)
                    if phase == "dn1":
                        gained(s)

            def gained(s):
                wait(se, fin_turned, s)
                for m in range(2):
                    last = nc.scalar.activation(part_a[:, m, :], res[:, bass.ds(2 * s + m, 1), :], ACT.Copy,
                                                scale=vec[:, bass.ds(2 * s + (FGAIN + m), 1)])
                last.then_inc(fin_gained, 1)

            def keep_rows(s, h):
                se.wait_ge(fin_turned, s + 1)
                nc.scalar.activation(out_tok[:, :, bass.ds(2 * P * s, 2 * P)],
                                     ps[:, 4 + h, :].rearrange("p (t f) -> p t f", t=2), ACT.Copy).then_inc(fin_kept, 1)

            def norm_tail(n_norm, table):
                se.wait_ge(inv_made, n_norm + 1)
                nc.scalar.activation(part_c[:, 1, :], part_c[:, 0, :], ACT.Sqrt).then_inc(rstd_made, 1)

                def two(i):
                    for b, part in ((0, part_a), (1, part_b)):
                        n = 2 * i + b
                        se.wait_ge(xm_made, n + (8 * n_norm + 1))
                        for m in range(2):
                            last = nc.scalar.activation(part[:, m, :], part[:, m, :], ACT.Identity,
                                                        scale=vec[:, bass.ds(2 * n + (table + 16 + m), 1)],
                                                        bias=vec[:, bass.ds(2 * n + (table + m), 1)])
                        last.then_inc(xh_made, 1)
                        se.wait_ge(xh_made, n + (8 * n_norm + 1))
                        nc.scalar.activation(xs[:, bass.ds(2 * n, 2), 0:T], part[:, :, :], ACT.Copy).then_inc(xh_hi, 1)
                with se.Fori(0, 4) as i:
                    two(i)

            def up_copy(phase, j, which, h):
                wait(se, taps_done, 2 * j + (TAPS[phase] + which))
                copy_a(phase, 2 * j + which, 2 * h, y[:, :, :])

            def up_mid(phase, j, which, part):
                se.wait_ge(acc_read, 2 * j + (SLABS[phase] + which + 1))
                for m in range(2):
                    last = nc.scalar.activation(part[:, m, :], y[:, m, :], ACT.Copy,
                                                scale=vec[:, bass.ds(2 * j + tap_column(phase, which, m, 1), 1)])
                last.then_inc(taps_mid, 1)

            def up_silu(phase, j):
                se.wait_ge(taps_done, 2 * j + (TAPS[phase] + 1))
                nc.scalar.activation(part_a[:, :, :], part_a[:, :, :], ACT.Silu).then_inc(silu_made, 1)

            def up_hi(phase, j):
                se.wait_ge(gated, j + (PAIRS[phase] + 1))
                nc.scalar.activation(act[:, bass.ds(2 * j, 2), 0:T], part_a[:, :, :], ACT.Copy).then_inc(act_hi_made, 1)

            def g_point(k, phase, j, h):
                if k == 2:
                    up_copy(phase, j, 0, h)
                if k == 3:
                    wait(se, act_made, j + PAIRS[phase])
                    up_mid(phase, j, 0, part_a)

            def v_up_point(k, phase, j, h):
                if k == 0:
                    up_silu(phase, j)
                if k == 2:
                    up_copy(phase, j, 1, h)
                if k == 3:
                    up_mid(phase, j, 1, part_b)

            first = lambda i, h: isinstance(i, int) and h == 0

            def k_pair(i):
                for h in range(2):
                    for k in range(4):
                        hi(2 * i + h, k)
                        if not first(i, h):
                            k_point(k, 2 * i + (h - 1), 1 - h)
            loop(se, 4, k_pair)

            def v_pair(i):
                for h in range(2):
                    for k in range(4):
                        hi(2 * i + (UNITS["v"] // 4 + h), k)
                        if first(i, h):
                            k_point(k, 7, 1)
                        else:
                            v_point(k, 2 * i + (h - 1), 1 - h)
            loop(se, 4, v_pair)

            def q_pair(i):
                for h in range(2):
                    for k in range(4):
                        hi(2 * i + (UNITS["q"] // 4 + h), k)
                        if first(i, h):
                            v_point(k, 7, 1)
                        else:
                            q_point(k, 2 * i + (h - 1), 1 - h)
            loop(se, 4, q_pair)

            def attention():
                def take_q(h):
                    wait(se, scores_made, 4 * h)
                    nc.scalar.activation(q_head[:, :, :], q_t[:, bass.ds(2 * h, 2), :], ACT.Copy).then_inc(qh_made, 1)

                def square_o(h):
                    for t in range(2):
                        se.wait_ge(o_copied, 2 * h + (t + 1))
                        wait(se, o_squared, 2 * h + t)
                        nc.scalar.activation(o_square[:, :], o_rows[:, t, bass.ds(T * h, T)], ACT.Square,
                                             accum_out=o_sum[:, t, bass.ds(h, 1)]).then_inc(o_squared, 1)

                def head(h, at_start, at_end):
                    se.wait_ge(neg_made, h + 1)
                    for n in range(4):
                        if n % 2 == 0:
                            wait(se, at_made, 2 * h + (n // 2 - 1))
                        nc.scalar.activation(probs[:, n, :], ps[:, n, :], ACT.Exp, scale=SCALE, bias=s_neg[:, n:n + 1],
                                             accum_out=s_sum[:, n:n + 1]).then_inc(exp_done, 1)
                    if not at_end:
                        take_q(h + 1)
                    if not at_start:
                        square_o(h + (-1))
                    for t in range(2):
                        se.wait_ge(at_made, 2 * h + (t + 1))
                        wait(se, o_made, 2 * h + (t - 1))
                        nc.scalar.activation(a_t[:, t, :], ps[:, 4 + t, :], ACT.Copy).then_inc(at_copied, 1)

                se.wait_ge(rope_done, 16)
                take_q(0)
                head(0, True, False)
                with se.Fori(1, HEADS - 1) as h:
                    head(h, False, False)
                head(HEADS - 1, False, True)
                square_o(HEADS - 1)
                se.wait_ge(o_inverted, 1)
                nc.scalar.activation(o_rstd[:, :, :], o_inv[:, :, :], ACT.Sqrt).then_inc(o_root, 1)

                def gain(i):
                    for b in range(2):
                        h = 2 * i + b
                        se.wait_ge(o_turned, h + 1)
                        wait(se, xs_ready, h + (8 - 1))
                        for m in range(2):
                            last = nc.scalar.activation(o_feat[:, b, m, :], ps[:, b, T * m:T * m + T], ACT.Copy, scale=gain_o[:, m:m + 1])
                        last.then_inc(o_gained, 1)
                        se.wait_ge(o_gained, h + 1)
                        nc.scalar.activation(xs[:, bass.ds(2 * h, 2), 0:T], o_feat[:, b, :, :], ACT.Copy).then_inc(o_hi, 1)
                loop(se, 4, gain)

                def keep_x(i):
                    for b in range(2):
                        n = 2 * i + b
                        se.wait_ge(xt_turned, n + 1)
                        nc.scalar.activation(res[:, bass.ds(2 * n, 2), :], ps[:, 4 + b, :].rearrange("p (k t) -> p k t", k=2), ACT.Copy).then_inc(xt_kept, 1)
                loop(se, 4, keep_x)

            def o_pair(i):
                for h in range(2):
                    for k in range(4):
                        hi(2 * i + (UNITS["o"] // 4 + h), k)
                        if first(i, h):
                            q_point(k, 7, 1)
                            if k == 3:
                                attention()
                        else:
                            res_point(k, "o", 2 * i + (h - 1), 1 - h, RES["o"])
            loop(se, 4, o_pair)

            def up(phase, tail):
                def four(i, ada):
                    for p in range(2):
                        for h in range(2):
                            for k in range(4):
                                hi(4 * i + (UNITS[phase] // 4 + 2 * p + h), k)
                                if first(i, p + h):
                                    tail(k)
                                elif h == 0:
                                    v_up_point(k, phase, 2 * i + (p - 1), 1)
                                else:
                                    g_point(k, phase, 2 * i + p, 0)
                                    if k == 1 and not first(i, p):
                                        up_hi(phase, 2 * i + (p - 1))
                up_loop(se, four)

            def down(phase, up_phase):
                def pair(i):
                    for h in range(2):
                        for k in range(12):
                            hi(6 * i + (UNITS[phase] // 4 + 3 * h + k // 4), k % 4, down_tiles(k)[1])
                            if first(i, h):
                                v_up_point(k, up_phase, FT // 2 - 1, 1)
                                if k == 5:
                                    up_hi(up_phase, FT // 2 - 1)
                            else:
                                res_point(k, phase, 2 * i + (h - 1), 1 - h, RES[phase], 12)
                                if phase == "dn1" and k == 8:
                                    keep_rows(2 * i + (h - 1), 1 - h)
                loop(se, 4, pair)

            def o_tail(k):
                res_point(k, "o", 7, 1, RES["o"])
                if k == 3:
                    se.wait_ge(ada_added, 12)
                    norm_tail(0, B0 + SH2)
            up("up0", o_tail)
            down("dn0", "up0")

            def sin_point(k, j, h, which):
                if which == 0:
                    if k == 2:
                        wait(se, gx_made, j)
                        copy_a("sin", 3 * j, 2 * h, part_a[:, :, :])
                elif which == 1:
                    if k == 2:
                        wait(se, taps_done, j + TAPS["sin"])
                        copy_a("sin", 3 * j + 1, 2 * h, y[:, :, :])
                    if k == 3:
                        se.wait_ge(gx_made, j + 1)
                        wait(se, z_mul, j)
                        for m in range(2):
                            last = nc.scalar.activation(part_b[:, m, :], y[:, m, :], ACT.Copy,
                                                        scale=vec[:, bass.ds(2 * j + (SCONV + 16 + m), 1)])
                        last.then_inc(taps_mid, 1)
                else:
                    if k == 2:
                        wait(se, z_made, j)
                        copy_a("sin", 3 * j + 2, 2 * h, part_c[:, :, :])
                    if k == 3:
                        se.wait_ge(z_mul, j + 1)
                        nc.scalar.activation(z[:, bass.ds(2 * j, 2), 0:T], part_c[:, :, :], ACT.Copy).then_inc(z_hi_made, 1)

            def sin_six(i):
                for n in range(6):
                    for k in range(4):
                        hi(6 * i + (UNITS["sin"] // 4 + n), k)
                        if first(i, n):
                            res_point(k, "dn0", 7, 1, RES["dn0"], 12)
                            if k == 3:
                                se.wait_ge(ada_added, 24)
                                norm_tail(1, B1 + SH1)
                        elif n % 3 == 0:
                            sin_point(k, 2 * i + (n // 3 - 1), (n - 1) % 2, 2)
                        else:
                            sin_point(k, 2 * i + n // 3, (n - 1) % 2, n % 3 - 1)
            loop(se, 4, sin_six)

            def so_pair(i):
                for h in range(2):
                    for k in range(4):
                        hi(2 * i + (UNITS["so"] // 4 + h), k)
                        if first(i, h):
                            sin_point(k, 7, 1, 2)
                        else:
                            res_point(k, "so", 2 * i + (h - 1), 1 - h, RES["so"])
            loop(se, 4, so_pair)

            def so_tail(k):
                res_point(k, "so", 7, 1, RES["so"])
                if k == 3:
                    norm_tail(2, B1 + SH2)
            up("up1", so_tail)
            down("dn1", "up1")
            for k in range(4):
                res_point(k, "dn1", 7, 1, RES["dn1"], 12)
            keep_rows(7, 1)
            se.wait_ge(rows_inv, 2)
            nc.scalar.activation(row_rstd[:, 0:2], row_inv[:, 0:2], ACT.Sqrt).then_inc(rows_rstd, 1)
            se.wait_ge(fin_kept, 8)
            se.wait_ge(rows_rstd, 2)
            nc.scalar.activation(out_tok[:, 1, :], out_tok[:, 1, :], ACT.Copy, scale=row_rstd[:, 1:2]).then_inc(fin_scaled[1], 1)

        @block.vector
        def _(ve):
            ve.wait_ge(vecs_turned, 1)
            spans = [(0, 0, 96, B0), (0, 96, 32, COND), (1, 0, 96, B1), (1, 96, 16 + 2 + 4, FGAIN)]
            for n in range(3):
                spans += [(2 + n, 0, 88, CONV[0] + 88 * n), (2 + n, 88, 16, SCONV + 16 * n), (5 + n, 0, 88, CONV[1] + 88 * n)]
            for tile, first_col, n, dst in spans:
                last = nc.vector.tensor_copy(vec[:, dst:dst + n],
                                             ps[:, tile // 4, 128 * (tile % 4) + first_col:128 * (tile % 4) + first_col + n])
            last.then_inc(vecs_made, 1)
            ve.wait_ge(vecs_made, 1)
            for base in (B0, B1):
                for scale in (SC1, SC2):
                    v = vec[:, base + scale:base + scale + 16]
                    last = nc.vector.tensor_scalar(v, v, 1.0, None, ALU.add)
            last.then_inc(plus_one, 1)
            lam4 = vec[:, LAMB:LAMB + 4].rearrange("p (n two) -> p two n", two=2)
            nc.vector.tensor_tensor(lam_prod[:, :], lam4[:, 0, :], lam4[:, 1, :], ALU.mult).then_inc(lam_multiplied, 1)
            nc.vector.tensor_scalar(gain_o[:, :], vec[:, SUBLN:SUBLN + 2], 1.0 - LAM_INIT, None, ALU.mult)
            ve.wait_ge(plus_one, 1)
            nc.vector.tensor_copy(ctx_mod[:, :], vec[:, 0:32]).then_inc(plus_one, 1)
            ve.wait_ge(lam_exped, 1)
            nc.vector.tensor_tensor(neg_lam[:, :], lam_exp[:, 1:2], lam_exp[:, 0:1], ALU.subtract).then_inc(lam_part, 1)
            ve.wait_ge(lam_part, 1)
            nc.vector.tensor_scalar(neg_lam[:, :], neg_lam[:, :], LAM_INIT, None, ALU.subtract).then_inc(lam_made, 1)

            ve.wait_ge(rows_squared, 4)
            nc.vector.tensor_scalar(row_var[:, :], row_sum[:, :], 1.0 / D, EPS, ALU.mult, ALU.add).then_inc(rows_var, 1)
            ve.wait_ge(rows_var, 1)
            nc.vector.reciprocal(row_inv[:, :], row_var[:, :]).then_inc(rows_inv, 1)
            ve.wait_ge(rows_rstd, 1)
            for n, tok in enumerate((x_tok, ctx_tok)):
                for t in range(2):
                    nc.vector.tensor_scalar(tok[:, t, :], tok[:, t, :], row_rstd[:, 2 * n + t:2 * n + t + 1], None, ALU.mult
                                            ).then_inc(rows_normed, 1)
            for n, xn in enumerate((xn_l, xn_c)):
                def keep(i):
                    for b in range(2):
                        ve.wait_ge(xn_turned, 2 * i + (8 * n + b + 1))
                        nc.vector.tensor_copy(xn[:, bass.ds(4 * i + 2 * b, 2), :],
                                              ps[:, b, :].rearrange("p (k t) -> p k t", k=2)).then_inc(xn_kept, 1)
                loop(ve, 4, keep)

            ve.wait_ge(plus_one, 2)

            def first_modulation(g):
                for b in range(2):
                    col = (SC1, SH1)[b]
                    ve.wait_ge(mod_turned, 2 * g + (b + 1))
                    both = ps[:, 4 + b, 0:8].rearrange("p (k c) -> p c k", c=2)
                    for m, table in enumerate((vec, ctx_mod)):
                        v = table[:, bass.ds(4 * g + col, 4)]
                        last = nc.vector.tensor_tensor(v, v, both[:, m, :], ALU.add)
                    last.then_inc(mod_made, 1)
                for m, (xn, dst) in enumerate(((xn_l, xs), (xn_c, cs))):
                    ve.wait_ge(h_hi, 2 * g + (m + 1))
                    nc.vector.tensor_tensor(dst[:, bass.ds(4 * g, 4), T:2 * T], xn[:, bass.ds(4 * g, 4), :],
                                            dst[:, bass.ds(4 * g, 4), 0:T], ALU.subtract).then_inc(xs_ready, 1)
            loop(ve, 4, first_modulation)

            def lo(quad, slot, n_tiles=KU):
                ve.wait_ge(hi_made, 4 * quad + (slot + 1))
                nc.vector.tensor_tensor(w_lo[:, slot, 0:n_tiles, :], raw[:, slot, 0:n_tiles, :],
                                        w_hi[:, slot, 0:n_tiles, :], ALU.subtract).then_inc(lo_made, 1)

            def ada_chunk(j, q, sums=ada_sum, buffers=1):
                if buffers == 2:
                    slot = q % ADA_SLOTS_KV
                    ve.wait_ge(ada_full[slot], 32 * j + 16 * (q // ADA_SLOTS_KV + 1))
                else:
                    slot = q % ADA_SLOTS
                    ve.wait_ge(ada_full[slot], 64 * j + 16 * (q // ADA_SLOTS + 1 - 32))
                for b in range(2):
                    t = 2 * q + b
                    w, scalar = ada_slot(slot)[:, b, :], cond[:, 0, t:t + 1]
                    if t == 0:
                        wait(ve, ada_reduced, j + (1 - buffers))
                        nc.vector.tensor_scalar(sums[:, :], w, scalar, None, ALU.mult).then_inc(ada_step, 1)
                    else:
                        ve.wait_ge(ada_step, 16 * j + t)
                        nc.vector.scalar_tensor_tensor(out=sums[:, :], in0=w, scalar=scalar, in1=sums[:, :],
                                                       op0=ALU.mult, op1=ALU.add).then_inc(ada_step, 1)

            def ada_add(j):
                ve.wait_ge(ada_reduced, j + 1)
                v = vec[:, bass.ds(4 * j + 4 * ADA_FIRST, 4)]
                nc.vector.tensor_tensor(v, v, ps[:, 6, 0:4], ALU.add).then_inc(ada_added, 1)

            def ada_in_pair(phase, i, h, k):
                j = 2 * i + ADA_AT[phase]
                sums = (ada_sum, ada_sum_b)[h]
                ada_chunk(j + h, 2 * k, sums, 2)
                ada_chunk(j + h, 2 * k + 1, sums, 2)
                if h == 0 and k == 3 and not (isinstance(i, int) and phase == "k"):
                    ada_add(j + (-1))
                if h == 1 and k == 3:
                    ada_add(j)

            def ada_in_24(phase, i, n):
                j = 2 * i + ADA_AT[phase]
                if n < 8:
                    ada_chunk(j, n)
                if n == 11:
                    ada_add(j)
                if 11 <= n < 19:
                    ada_chunk(j + 1, n - 11)
                if n == 23:
                    ada_add(j + 1)

            def add_b(n, bank, dst):
                ve.wait_ge(a_copied, n + 1)
                nc.vector.tensor_tensor(dst, dst, ps[:, bank:bank + 2, T:2 * T], ALU.add).then_inc(acc_read, 1)

            two = lambda t: t[:, :].unsqueeze(1).broadcast_to([P, 2, T])

            def rope(r, dst, n_slabs):
                if isinstance(r, int) and r == 0:
                    ve.wait_ge(rope_loaded, 32)
                ve.wait_ge(acc_read, n_slabs + 1)
                nc.vector.tensor_tensor(dst, y_qk[:, :, :], two(rope_cos), ALU.mult)
                ve.wait_ge(rot_made, r + 1)
                nc.vector.tensor_tensor(rot[:, :, :], rot[:, :, :], two(rope_sin), ALU.mult).then_inc(rope_part, 1)
                ve.wait_ge(rope_part, r + 1)
                nc.vector.tensor_tensor(dst, dst, rot[:, :, :], ALU.add).then_inc(rope_done, 1)

            def k_point(k, s, h):
                if k == 2:
                    kc = k_t[:, bass.ds(2 * s, 2), T:2 * T]
                    ve.wait_ge(ctx_copied, s + 1)
                    nc.vector.tensor_tensor(kc, kc, ps[:, 2:4, T:2 * T], ALU.add).then_inc(ctx_read, 1)
                    add_b(s, 4 * h, y_qk[:, :, :])
                if k == 3:
                    rope(s, k_t[:, bass.ds(2 * s, 2), 0:T], s)

            def v_point(k, s, h):
                if k == 2:
                    ve.wait_ge(a_copied, s + (SLABS["v"] + 1))
                    nc.vector.tensor_copy(v_rows[:, 2:4, bass.ds(s * SLAB, SLAB)], ps[:, 2:4, 0:SLAB]).then_inc(acc_read, 1)

            def q_point(k, s, h):
                if k == 2:
                    add_b(s + SLABS["q"], 2 * h, y_qk[:, :, :])
                if k == 3:
                    rope(s + 8, q_t[:, bass.ds(2 * s, 2), :], s + SLABS["q"])

            def res_point(k, phase, s, h, gate):
                if k == 2:
                    n = s + SLABS[phase]
                    add_b(n, 2 * h, y[:, :, :])
                    ve.wait_ge(acc_read, n + 1)
                    for m in range(2):
                        r_ = res[:, bass.ds(2 * s + m, 1), :]
                        last = nc.vector.scalar_tensor_tensor(out=r_, in0=y[:, m:m + 1, :], scalar=vec[:, bass.ds(2 * s + (gate + m), 1)],
                                                              in1=r_, op0=ALU.mult, op1=ALU.add)
                    last.then_inc(res_made, 1)
                if k == 3:
                    n = s + RES[phase]
                    ve.wait_ge(sq_made, n + 1)
                    if isinstance(s, int) and s == 0:
                        nc.vector.tensor_copy(part_b[:, :, :], part_c[:, :, :]).then_inc(sq_added, 1)
                    else:
                        ve.wait_ge(sq_added, n)
                        nc.vector.tensor_tensor(part_b[:, :, :], part_b[:, :, :], part_c[:, :, :], ALU.add).then_inc(sq_added, 1)

            def norm_tail(n_norm):
                ve.wait_ge(sq_used, n_norm + 1)
                nc.vector.tensor_scalar(part_c[:, 1, :], ps[:, 7, 0:T], 1.0 / D, EPS, ALU.mult, ALU.add).then_inc(var_made, 1)
                ve.wait_ge(var_made, n_norm + 1)
                nc.vector.reciprocal(part_c[:, 0, :], part_c[:, 1, :]).then_inc(inv_made, 1)
                ve.wait_ge(rstd_made, n_norm + 1)
                parts = (part_a, part_b)
                rstd = part_c[:, 1:2, :].broadcast_to([P, 2, T])

                def scaled(n, b):
                    nc.vector.tensor_tensor(parts[b][:, :, :], res[:, bass.ds(2 * n, 2), :], rstd, ALU.mult).then_inc(xm_made, 1)

                def low(n, b):
                    ve.wait_ge(xh_hi, n + (8 * n_norm + 1))
                    nc.vector.tensor_tensor(xs[:, bass.ds(2 * n, 2), T:2 * T], parts[b][:, :, :], xs[:, bass.ds(2 * n, 2), 0:T],
                                            ALU.subtract).then_inc(xs_ready, 1)
                scaled(0, 0)
                scaled(1, 1)
                with ve.Fori(0, 3) as i:
                    for b in range(2):
                        low(2 * i + b, b)
                        ve.wait_ge(xs_ready, 2 * i + (8 * n_norm + 16 + b + 1))
                        scaled(2 * i + (b + 2), b)
                low(6, 0)
                low(7, 1)

            def taps(phase, j, which, part):
                n = j + TAPS[phase] if phase == "sin" else 2 * j + (TAPS[phase] + which)
                ve.wait_ge(taps_mid, n + 1)
                for m in range(2):
                    last = nc.vector.scalar_tensor_tensor(out=part[:, m, 1:T], in0=y[:, m, 0:T - 1],
                                                          scalar=vec[:, bass.ds(2 * j + tap_column(phase, which, m, 0), 1)],
                                                          in1=part[:, m, 1:T], op0=ALU.mult, op1=ALU.add)
                last.then_inc(taps_first, 1)
                ve.wait_ge(taps_first, n + 1)
                for m in range(2):
                    last = nc.vector.scalar_tensor_tensor(out=part[:, m, 0:T - 1], in0=y[:, m, 1:T],
                                                          scalar=vec[:, bass.ds(2 * j + tap_column(phase, which, m, 2), 1)],
                                                          in1=part[:, m, 0:T - 1], op0=ALU.mult, op1=ALU.add)
                last.then_inc(taps_done, 1)

            def g_point(k, phase, j, h):
                if k == 2:
                    add_b(2 * j + SLABS[phase], 2 * h, y[:, :, :])
                if k == 3:
                    taps(phase, j, 0, part_a)

            def v_up_point(k, phase, j, h):
                if k == 2:
                    add_b(2 * j + (SLABS[phase] + 1), 2 * h, y[:, :, :])
                if k == 3:
                    taps(phase, j, 1, part_b)

            def gate_pair(phase, j):
                n = j + PAIRS[phase]
                ve.wait_ge(silu_made, n + 1)
                ve.wait_ge(taps_done, 2 * j + (TAPS[phase] + 2))
                nc.vector.tensor_tensor(part_a[:, :, :], part_a[:, :, :], part_b[:, :, :], ALU.mult).then_inc(gated, 1)

            def low_pair(phase, j):
                ve.wait_ge(act_hi_made, j + (PAIRS[phase] + 1))
                nc.vector.tensor_tensor(act[:, bass.ds(2 * j, 2), T:2 * T], part_a[:, :, :], act[:, bass.ds(2 * j, 2), 0:T],
                                        ALU.subtract).then_inc(act_made, 1)

            first = lambda i, h: isinstance(i, int) and h == 0

            def k_pair(i):
                for h in range(2):
                    for k in range(4):
                        lo(2 * i + h, k)
                        if not first(i, h):
                            k_point(k, 2 * i + (h - 1), 1 - h)
                        ada_in_pair("k", i, h, k)
            loop(ve, 4, k_pair)

            def v_pair(i):
                for h in range(2):
                    for k in range(4):
                        lo(2 * i + (UNITS["v"] // 4 + h), k)
                        if first(i, h):
                            k_point(k, 7, 1)
                        else:
                            v_point(k, 2 * i + (h - 1), 1 - h)
                        ada_in_pair("v", i, h, k)
            loop(ve, 4, v_pair)

            def q_pair(i):
                for h in range(2):
                    for k in range(4):
                        lo(2 * i + (UNITS["q"] // 4 + h), k)
                        if first(i, h):
                            v_point(k, 7, 1)
                            if k == 3:
                                ada_add(ADA_AT["up0"] - 1)
                        else:
                            q_point(k, 2 * i + (h - 1), 1 - h)
            loop(ve, 4, q_pair)

            def attention():
                def keep_o(h):
                    for t in range(2):
                        ve.wait_ge(o_made, 2 * h + (t + 1))
                        nc.vector.tensor_copy(o_rows[:, t, bass.ds(T * h, T)], ps[:, 6 + t, 0:T]).then_inc(o_copied, 1)

                def head(h, at_start):
                    ve.wait_ge(scores_made, 4 * h + 4)
                    nc.vector.reduce_max(s_max[:, :], ps[:, 0:4, :], AX_X).then_inc(max_made, 1)
                    ve.wait_ge(max_made, h + 1)
                    nc.vector.tensor_scalar(s_neg[:, :], s_max[:, :], -SCALE, None, ALU.mult).then_inc(neg_made, 1)
                    if not at_start:
                        keep_o(h + (-1))
                    ve.wait_ge(exp_done, 4 * h + 4)
                    nc.vector.reciprocal(s_inv[:, :], s_sum[:, :]).then_inc(sum_inv, 1)
                    ve.wait_ge(sum_inv, h + 1)
                    nc.vector.tensor_scalar(s_lam[:, :], s_inv[:, :].rearrange("p (t i) -> p i t", i=2)[:, 1, :], neg_lam[:, 0:1], None, ALU.mult
                                            ).then_inc(lam_scaled, 1)
                    ve.wait_ge(lam_scaled, h + 1)
                    for t in range(2):
                        last = nc.vector.tensor_scalar(probs[:, 2 * t + 1, :], probs[:, 2 * t + 1, :], s_lam[:, t:t + 1], None, ALU.mult)
                    last.then_inc(p1_scaled, 1)
                    ve.wait_ge(p1_scaled, h + 1)
                    for t in range(2):
                        nc.vector.scalar_tensor_tensor(out=probs[:, 2 * t, :], in0=probs[:, 2 * t, :], scalar=s_inv[:, 2 * t:2 * t + 1],
                                                       in1=probs[:, 2 * t + 1, :], op0=ALU.mult, op1=ALU.add).then_inc(a_made, 1)

                ve.wait_ge(lam_made, 1)
                head(0, True)
                with ve.Fori(1, HEADS) as h:
                    head(h, False)
                keep_o(HEADS - 1)
                ve.wait_ge(o_squared, 2 * HEADS)
                nc.vector.tensor_scalar(o_sum[:, :, :], o_sum[:, :, :], 1.0 / T, EPS, ALU.mult, ALU.add).then_inc(o_var, 1)
                ve.wait_ge(o_var, 1)
                nc.vector.reciprocal(o_inv[:, :, :], o_sum[:, :, :]).then_inc(o_inverted, 1)
                ve.wait_ge(o_root, 1)
                ve.wait_ge(o_copied, 2 * HEADS)

                def scaled(h):
                    for t in range(2):
                        o = o_rows[:, t, bass.ds(T * h, T)]
                        last = nc.vector.tensor_scalar(o, o, o_rstd[:, t, bass.ds(h, 1)], None, ALU.mult)
                    last.then_inc(o_normed, 1)

                def low(h, b):
                    ve.wait_ge(o_hi, h + 1)
                    nc.vector.tensor_tensor(xs[:, bass.ds(2 * h, 2), T:2 * T], o_feat[:, b, :, :], xs[:, bass.ds(2 * h, 2), 0:T],
                                            ALU.subtract).then_inc(xs_ready, 1)
                scaled(0)
                scaled(1)
                with ve.Fori(0, 3) as i:
                    for b in range(2):
                        low(2 * i + b, b)
                        scaled(2 * i + (b + 2))
                low(6, 0)
                low(7, 1)

            def o_pair(i):
                for h in range(2):
                    for k in range(4):
                        lo(2 * i + (UNITS["o"] // 4 + h), k)
                        if first(i, h):
                            q_point(k, 7, 1)
                            if k == 3:
                                attention()
                                ve.wait_ge(xt_kept, 8)
                        else:
                            res_point(k, "o", 2 * i + (h - 1), 1 - h, B0 + G1)
            loop(ve, 4, o_pair)

            def up(phase, tail):
                def four(i, ada):
                    for p in range(2):
                        for h in range(2):
                            for k in range(4):
                                lo(4 * i + (UNITS[phase] // 4 + 2 * p + h), k)
                                if first(i, p + h):
                                    tail(k)
                                elif h == 0:
                                    v_up_point(k, phase, 2 * i + (p - 1), 1)
                                else:
                                    if not first(i, p):
                                        if k == 0:
                                            gate_pair(phase, 2 * i + (p - 1))
                                        if k == 1:
                                            low_pair(phase, 2 * i + (p - 1))
                                    g_point(k, phase, 2 * i + p, 0)
                                n = 8 * p + 4 * h + k
                                if ada:
                                    j = i + ADA_AT[phase]
                                    if n < 8:
                                        ada_chunk(j, n)
                                    if n == 13:
                                        ada_add(j)
                up_loop(ve, four)

            def down(phase, up_phase, gate, ada):
                def pair(i):
                    for h in range(2):
                        for k in range(12):
                            lo(6 * i + (UNITS[phase] // 4 + 3 * h + k // 4), k % 4, down_tiles(k)[1])
                            if ada:
                                ada_in_24(phase, i, 12 * h + k)
                            if first(i, h):
                                v_up_point(k, up_phase, FT // 2 - 1, 1)
                                if k == 4:
                                    gate_pair(up_phase, FT // 2 - 1)
                                if k == 5:
                                    low_pair(up_phase, FT // 2 - 1)
                            else:
                                res_point(k, phase, 2 * i + (h - 1), 1 - h, gate)
                loop(ve, 4, pair)

            def o_tail(k):
                res_point(k, "o", 7, 1, B0 + G1)
                if k == 3:
                    norm_tail(0)
            up("up0", o_tail)
            down("dn0", "up0", B0 + G2, True)

            def sin_point(k, j, h, which):
                n = 3 * j + (SLABS["sin"] + which)
                if which == 0 and k == 2:
                    add_b(n, 2 * h, part_a[:, :, :])
                if which == 1:
                    if k == 2:
                        add_b(n, 2 * h, y[:, :, :])
                        ve.wait_ge(acc_read, n + 1)
                        nc.vector.tensor_tensor(y[:, :, :], y[:, :, :], part_a[:, :, :], ALU.mult).then_inc(gx_made, 1)
                    if k == 3:
                        taps("sin", j, 0, part_b)
                if which == 2:
                    if k == 2:
                        add_b(n, 2 * h, part_c[:, :, :])
                        ve.wait_ge(acc_read, n + 1)
                        ve.wait_ge(taps_done, j + (TAPS["sin"] + 1))
                        nc.vector.tensor_tensor(part_c[:, :, :], part_c[:, :, :], part_b[:, :, :], ALU.mult).then_inc(z_mul, 1)
                    if k == 3:
                        ve.wait_ge(z_hi_made, j + 1)
                        nc.vector.tensor_tensor(z[:, bass.ds(2 * j, 2), T:2 * T], part_c[:, :, :], z[:, bass.ds(2 * j, 2), 0:T],
                                                ALU.subtract).then_inc(z_made, 1)

            def sin_six(i):
                for n in range(6):
                    for k in range(4):
                        lo(6 * i + (UNITS["sin"] // 4 + n), k)
                        if first(i, n):
                            res_point(k, "dn0", 7, 1, B0 + G2)
                            if k == 3:
                                norm_tail(1)
                        elif n % 3 == 0:
                            sin_point(k, 2 * i + (n // 3 - 1), (n - 1) % 2, 2)
                        else:
                            sin_point(k, 2 * i + n // 3, (n - 1) % 2, n % 3 - 1)
                        ada_in_24("sin", i, 4 * n + k)
            loop(ve, 4, sin_six)

            def so_pair(i):
                for h in range(2):
                    for k in range(4):
                        lo(2 * i + (UNITS["so"] // 4 + h), k)
                        if first(i, h):
                            sin_point(k, 7, 1, 2)
                        else:
                            res_point(k, "so", 2 * i + (h - 1), 1 - h, B1 + G1)
            loop(ve, 4, so_pair)

            def so_tail(k):
                res_point(k, "so", 7, 1, B1 + G1)
                if k == 3:
                    norm_tail(2)
            up("up1", so_tail)
            down("dn1", "up1", B1 + G2, False)
            for k in range(4):
                res_point(k, "dn1", 7, 1, B1 + G2)
            ve.wait_ge(sq_used, 4)
            for t in range(2):
                last = nc.vector.tensor_scalar(row_var[:, t:t + 1], ps[:, 6 + t, 0:1], 1.0 / D, EPS, ALU.mult, ALU.add)
            last.then_inc(rows_var, 1)
            ve.wait_ge(rows_var, 2)
            nc.vector.reciprocal(row_inv[:, 0:2], row_var[:, 0:2]).then_inc(rows_inv, 1)
            ve.wait_ge(fin_kept, 8)
            ve.wait_ge(rows_rstd, 2)
            nc.vector.tensor_scalar(out_tok[:, 0, :], out_tok[:, 0, :], row_rstd[:, 0:1], None, ALU.mult).then_inc(fin_scaled[0], 1)

        @block.tensor
        def _(pe):
            mm = nc.tensor.matmul
            pe.wait_ge(ident_loaded, 16)
            pe.wait_ge(vecs_loaded, 16 * 19)
            for tile, n in enumerate((128, 118, 104, 104, 104, 88, 88, 88)):
                last = nc.tensor.transpose(ps[:, tile // 4, 128 * (tile % 4):128 * (tile % 4) + n], vec_rows[0:n, tile, :], ident[0:n, 0:n])
            last.then_inc(vecs_turned, 1)
            pe.wait_ge(ones_made, 1)
            pe.wait_ge(lam_multiplied, 1)
            mm(ps[:, 6, 0:2], ones[:, :], lam_prod[:, :], start=True, stop=True).then_inc(lam_summed, 1)

            pe.wait_ge(cond_made, 1)

            def mod_products(g, b):
                wait(pe, mod_copied, 2 * g + (b - 1))
                for q in range(8):
                    pe.wait_ge(start_full[q % 4], 64 * g + 16 * (2 * b + q // 4 + 1))
                    for t in range(2):
                        last = mm(ps[0:2, 2 + b, :], cond[:, :, 2 * q + t], start_ring[:, q % 4, t, :],
                                  start=(q == 0 and t == 0), stop=(q == 7 and t == 1))
                    last.then_inc(start_used, 1)

            def mod_turn(n, b):
                pe.wait_ge(mod_copied, n + 1)
                wait(pe, mod_made, n - 1)
                for t in range(4):
                    last = nc.tensor.transpose(ps[:, 4 + b, 2 * t:2 * t + 2], mod_rows[:, b, P * t:P * t + P], ident[0:2, 0:2])
                last.then_inc(mod_turned, 1)

            def first_modulation(g):
                mod_products(g, 0)
                if g > 0:
                    mod_turn(2 * g - 1, 1)
                mod_products(g, 1)
                mod_turn(2 * g, 0)
            first_modulation(0)
            pe.wait_ge(vecs_made, 1)
            for n, tok in enumerate((x_tok, ctx_tok)):
                pe.wait_ge(rows_normed, 2 * n + 2)

                for i in range(8):
                    wait(pe, xn_kept, 8 * n + i - 1)
                    for k in range(2):
                        for t in range(2):
                            last = nc.tensor.transpose(ps[:, i % 2, T * k + P * t:T * k + P * t + P],
                                                       tok[:, t, P * (2 * i + k):P * (2 * i + k) + P], ident[:, :])
                    last.then_inc(xn_turned, 1)
            for g in range(1, 4):
                first_modulation(g)
            mod_turn(7, 1)

            def unit(quad, slot, bank, src, tile, n_tiles, is_first, is_last):
                pe.wait_ge(lo_made, 4 * quad + (slot + 1))
                for t in range(n_tiles):
                    for m in range(2):
                        cols = slice(P * m, P * m + P)
                        mm(ps[:, bank + m, :], w_hi[:, slot, t, cols], src[:, tile + t, :],
                           start=(is_first and t == 0), stop=False)
                        last = mm(ps[:, bank + m, 0:T], w_lo[:, slot, t, cols], src[:, tile + t, 0:T],
                                  start=False, stop=(is_last and t == n_tiles - 1))
                last.then_inc(w_used, 1)

            def ada_reduce(j, sums=ada_sum):
                pe.wait_ge(ada_step, 16 * j + 16)
                wait(pe, ada_added, j)
                for t in range(4):
                    last = mm(ps[:, 6, t:t + 1], sums[:, P * t:P * t + P], ones[:, 0:1], start=True, stop=True)
                last.then_inc(ada_reduced, 1)

            def ada_in_pair(phase, i, h, k):
                if h == 0 and k == 0 and not (isinstance(i, int) and phase == "k"):
                    ada_reduce(2 * i + (ADA_AT[phase] - 1), ada_sum_b)
                if h == 1 and k == 0:
                    ada_reduce(2 * i + ADA_AT[phase], ada_sum)

            def sum_squares(n_norm):
                pe.wait_ge(sq_added, 8 * (n_norm + 1))
                for m in range(2):
                    last = mm(ps[:, 7, 0:T], ones[:, :], part_b[:, m, :], start=(m == 0), stop=(m == 1))
                last.then_inc(sq_used, 1)

            first = lambda i, h: isinstance(i, int) and h == 0

            def k_pair(i):
                for h in range(2):
                    wait(pe, acc_read, 2 * i + (h - 1))
                    for k in range(4):
                        if first(i, h):
                            pe.wait_ge(xs_ready, 2 * (k + 1))
                        pe.wait_ge(lo_made, 8 * i + (4 * h + k + 1))
                        for src, bank in ((xs, 4 * h), (cs, 2)):
                            if src is cs and k == 0:
                                wait(pe, ctx_read, 2 * i + h)
                            for t in range(4):
                                for m in range(2):
                                    cols = slice(P * m, P * m + P)
                                    mm(ps[:, bank + m, :], w_hi[:, k, t, cols], src[:, 4 * k + t, :], start=(k == 0 and t == 0), stop=False)
                                    last = mm(ps[:, bank + m, 0:T], w_lo[:, k, t, cols], src[:, 4 * k + t, 0:T], start=False, stop=(k == 3 and t == 3))
                        last.then_inc(w_used, 1)
                        ada_in_pair("k", i, h, k)
            loop(pe, 4, k_pair)

            def v_pair(i):
                for h in range(2):
                    if first(i, h):
                        pe.wait_ge(acc_read, SLABS["v"] - 1)
                        pe.wait_ge(ctx_read, SLABS["v"])
                    for k in range(4):
                        pe.wait_ge(lo_made, 8 * i + (UNITS["v"] + 4 * h + k + 1))
                        for src, bank in ((xs, 4 * h), (cs, 2)):
                            if src is cs and k == 0 and not first(i, h):
                                pe.wait_ge(acc_read, 2 * i + (SLABS["v"] + h))
                            for t in range(4):
                                for n in range(2):
                                    x_hi = src[:, 4 * k + t, P * n:P * n + P]
                                    x_lo = src[:, 4 * k + t, T + P * n:T + P * n + P]
                                    mm(ps[:, bank + n, 0:SLAB], x_hi, w_hi[:, k, t, :], start=(k == 0 and t == 0), stop=False)
                                    mm(ps[:, bank + n, 0:SLAB], x_hi, w_lo[:, k, t, :], start=False, stop=False)
                                    last = mm(ps[:, bank + n, 0:SLAB], x_lo, w_hi[:, k, t, :], start=False, stop=(k == 3 and t == 3))
                        last.then_inc(w_used, 1)
                        ada_in_pair("v", i, h, k)
            loop(pe, 4, v_pair)

            def q_pair(i):
                for h in range(2):
                    if first(i, h):
                        pe.wait_ge(acc_read, SLABS["q"] - 1)
                    elif first(i, h - 1):
                        pe.wait_ge(acc_read, SLABS["q"])
                    else:
                        pe.wait_ge(acc_read, 2 * i + (SLABS["q"] + h - 1))
                    for k in range(4):
                        unit(2 * i + (UNITS["q"] // 4 + h), k, 2 * h, xs, 4 * k, 4, k == 0, k == 3)
                        if first(i, h) and k == 0:
                            ada_reduce(ADA_AT["up0"] - 1, ada_sum_b)
            loop(pe, 4, q_pair)

            def attention():
                def scores(h):
                    pe.wait_ge(qh_made, h + 1)
                    for n in range(4):
                        wait(pe, exp_done, 4 * h + (n - 3))
                        mm(ps[:, n, :], q_head[:, n % 2, P * (n // 2):P * (n // 2) + P],
                           k_t[:, bass.ds(2 * h + n % 2, 1), :], start=True, stop=True).then_inc(scores_made, 1)

                def weigh(h):
                    for t in range(2):
                        pe.wait_ge(a_made, 2 * h + (t + 1))
                        wait(pe, at_copied, 2 * h + (t - 1))
                        for k in range(4):
                            last = nc.tensor.transpose(ps[:, 4 + t, P * k:P * k + P], probs[:, 2 * t, P * k:P * k + P], ident[:, :])
                        last.then_inc(at_made, 1)
                    for t in range(2):
                        pe.wait_ge(at_copied, 2 * h + (t + 1))
                        wait(pe, o_copied, 2 * h + (t - 1))
                        for k in range(4):
                            last = mm(ps[:, 6 + t, 0:T], a_t[:, t, P * k:P * k + P],
                                      v_rows[:, k, bass.ds(T * h, T)], start=(k == 0), stop=(k == 3))
                        last.then_inc(o_made, 1)

                pe.wait_ge(rope_done, 16)
                pe.wait_ge(acc_read, SLABS["o"])
                scores(0)
                scores(1)
                weigh(0)
                with pe.Fori(1, HEADS - 1) as h:
                    scores(h + 1)
                    weigh(h)
                weigh(HEADS - 1)

                for h in range(HEADS):
                    pe.wait_ge(o_normed, h + 1)
                    wait(pe, o_gained, h - 1)
                    for m in range(2):
                        for t in range(2):
                            last = nc.tensor.transpose(ps[:, h % 2, T * m + P * t:T * m + P * t + P],
                                                       o_rows[:, t, T * h + P * m:T * h + P * m + P], ident[:, :])
                    last.then_inc(o_turned, 1)
                pe.wait_ge(xt_loaded, 16)
                for n in range(8):
                    wait(pe, xt_kept, n - 1)
                    for k in range(2):
                        for t in range(2):
                            last = nc.tensor.transpose(ps[:, 4 + n % 2, T * k + P * t:T * k + P * t + P],
                                                       x_tok[:, t, P * (2 * n + k):P * (2 * n + k) + P], ident[:, :])
                    last.then_inc(xt_turned, 1)
            attention()

            def narrow(phase, i, src, n_ready=None, squares_at=None, ready=None):
                for h in range(2):
                    if not first(i, h) and not first(i, h - 1):
                        pe.wait_ge(acc_read, 2 * i + (SLABS[phase] + h - 1))
                    if first(i, h - 1):
                        pe.wait_ge(acc_read, SLABS[phase])
                    for k in range(4):
                        if first(i, h) and ready:
                            ready(k)
                        unit(2 * i + (UNITS[phase] // 4 + h), k, 2 * h, src, 4 * k, 4, k == 0, k == 3)
            def all_heads(k):
                pe.wait_ge(xs_ready, 8 + 2 * (k + 1))
                if k == 0:
                    pe.wait_ge(o_gained, 8)
            loop(pe, 4, lambda i: narrow("o", i, xs, ready=all_heads))

            def up(phase, n_ready, n_norm):
                sum_squares(n_norm)

                def four(i, ada):
                    for p in range(2):
                        for h in range(2):
                            g = 2 * p + h
                            if first(i, g) or first(i, g - 1):
                                pe.wait_ge(acc_read, SLABS[phase])
                            else:
                                pe.wait_ge(acc_read, 4 * i + (SLABS[phase] + g - 1))
                            for k in range(4):
                                if first(i, g):
                                    pe.wait_ge(xs_ready, n_ready + 2 * (k + 1))
                                unit(4 * i + (UNITS[phase] // 4 + g), k, 2 * h, xs, 4 * k, 4, k == 0, k == 3)
                                if ada and 4 * g + k == 9:
                                    ada_reduce(i + ADA_AT[phase])
                up_loop(pe, four)

            def turn_rows(s, h):
                pe.wait_ge(fin_gained, s + 1)
                wait(pe, fin_kept, s - 1)
                for t in range(2):
                    for m in range(2):
                        last = nc.tensor.transpose(ps[:, 4 + h, T * t + P * m:T * t + P * m + P], part_a[:, m, P * t:P * t + P], ident[:, :])
                last.then_inc(fin_turned, 1)

            def down(phase, ada):
                def pair(i):
                    for h in range(2):
                        if first(i, h) or first(i, h - 1):
                            pe.wait_ge(acc_read, SLABS[phase] + h - 1)
                        else:
                            pe.wait_ge(acc_read, 2 * i + (SLABS[phase] + h - 1))
                        for k in range(12):
                            tile, n = down_tiles(k)
                            if first(i, h) and k in (0, 11):
                                pe.wait_ge(act_made, PAIRS_END[phase] - (1 if k == 0 else 0))
                            unit(6 * i + (UNITS[phase] // 4 + 3 * h + k // 4), k % 4, 2 * h, act, tile, n, k == 0, k == 11)
                            if phase == "dn1" and k == 4 and not first(i, h):
                                turn_rows(2 * i + (h - 1), 1 - h)
                            if ada and 12 * h + k == 8:
                                ada_reduce(2 * i + ADA_AT[phase])
                            if ada and 12 * h + k == 20:
                                ada_reduce(2 * i + (ADA_AT[phase] + 1))
                loop(pe, 4, pair)

            up("up0", 16, 0)
            down("dn0", True)
            sum_squares(1)

            def sin_six(i):
                for n in range(6):
                    if first(i, n) or first(i, n - 1):
                        pe.wait_ge(acc_read, SLABS["sin"])
                    else:
                        pe.wait_ge(acc_read, 6 * i + (SLABS["sin"] + n - 1))
                    for k in range(4):
                        if first(i, n):
                            pe.wait_ge(xs_ready, 24 + 2 * (k + 1))
                        unit(6 * i + (UNITS["sin"] // 4 + n), k, 2 * (n % 2), xs, 4 * k, 4, k == 0, k == 3)
                        if 4 * n + k == 8:
                            ada_reduce(2 * i + ADA_AT["sin"])
                        if 4 * n + k == 20:
                            ada_reduce(2 * i + (ADA_AT["sin"] + 1))
            loop(pe, 4, sin_six)

            def z_ready(k):
                pe.wait_ge(z_made, 8 if k == 3 else 7)
                if k == 0:
                    pe.wait_ge(acc_read, SLABS["so"] - 1)
            loop(pe, 4, lambda i: narrow("so", i, z, ready=z_ready))

            up("up1", 32, 2)
            down("dn1", False)
            pe.wait_ge(sq_added, 32)
            for t in range(2):
                for m in range(2):
                    last = mm(ps[:, 6 + t, 0:1], part_b[:, m, P * t:P * t + P], ones[:, 0:1], start=(m == 0), stop=(m == 1))
            last.then_inc(sq_used, 1)
            turn_rows(7, 1)


RES = {"o": 0, "dn0": 8, "so": 16, "dn1": 24}
TAPS = {"up0": 0, "sin": 44, "up1": 52}
PAIRS = {"up0": 0, "up1": 22}
PAIRS_END = {"dn0": 22, "dn1": 44}


def tap_column(phase, which, m, tap):
    if phase == "sin":
        return SCONV + KT * tap + m
    return CONV[0 if phase == "up0" else 1] + 2 * FT * tap + FT * which + m


_INS = ["x", "c", "ctx", "c_ctx", "w_ada", "b_ada", "attn_w_qkv", "attn_w_o", "attn_lambda_q1", "attn_lambda_k1",
        "attn_lambda_q2", "attn_lambda_k2", "attn_subln_gain", "sconv_w_in", "sconv_conv", "sconv_w_out",
        "ffn_w_up", "ffn_conv", "ffn_w_down", "final_gain"]


def _rope_tables(np):
    half = HEAD_DIM // 2
    inv = (1.0 / (np.float32(10000.0) ** (np.arange(0, half, 2, dtype=np.float32) / np.float32(half)))).astype(np.float32)
    row = np.repeat(np.arange(T // GRID_W, dtype=np.float32), GRID_W)
    col = np.tile(np.arange(GRID_W, dtype=np.float32), T // GRID_W)
    ang_r, ang_c = inv[:, None] * row[None, :], inv[:, None] * col[None, :]
    ang = np.concatenate([ang_r, ang_r, ang_c, ang_c], axis=0)
    sign = np.repeat(np.array([-1, 1, -1, 1], np.float32), 32)[:, None]
    return np.cos(ang).astype(np.float32), (sign * np.sin(ang)).astype(np.float32)


def kernel(**inputs):
    import numpy as _np
    import concourse.bacc as _bacc
    from concourse import mybir as _mybir
    from concourse.bass_utils import run_bass_kernel_spmd as _run

    nc = _bacc.Bacc("TRN2", target_bir_lowering=False, num_devices=1)
    arrays, args = {}, []

    def give(name, a):
        arrays[f"in_{name}_dram"] = a
        args.append(nc.dram_tensor(f"in_{name}_dram", a.shape, _mybir.dt.from_np(a.dtype), kind="ExternalInput").ap())

    for name in _INS:
        give(name, _np.ascontiguousarray(inputs[name]))
    cos, sin = _rope_tables(_np)
    give("ident", _np.eye(P, dtype=_np.float32))
    give("rope_cos", cos)
    give("rope_sin", sin)
    o = nc.dram_tensor("out_0_dram", (1, T, D), _mybir.dt.float32, kind="ExternalOutput").ap()
    program(nc, *args, o)
    r = _run(nc, [arrays], core_ids=[0])
    return r.results[0]["out_0_dram"]
```

```python
import concourse.bass as bass
from concourse import mybir
from contextlib import ExitStack
import math

F32 = mybir.dt.float32
F32R = mybir.dt.float32r
ACT = mybir.ActivationFunctionType
ALU = mybir.AluOpType
AX_X = mybir.AxisListType.X

P = 128
D = 2048
T = 256
KT = D // P
HEADS = 8
QK = 2048
D_FF = 5632
FT = D_FF // P
GRID_W = 64
HEAD_DIM = 128
SCALE = HEAD_DIM ** -0.5
EPS = 1e-6
LAM_INIT = 0.8 - 0.6 * math.exp(-0.3 * 0)
SLAB = 256
RING = 4
KU = 4
ADA_COLS = 512
ADA_SLABS = 6 * D // ADA_COLS
ADA_FIRST = 2 * D // ADA_COLS
ADA_SLOTS, ADA_SLOTS_KV = 2, 4

PHASES = {"k": (8, 4), "v": (8, 4), "q": (8, 4), "o": (8, 4), "up0": (44, 4), "dn0": (8, 12),
          "sin": (24, 4), "so": (8, 4), "up1": (44, 4), "dn1": (8, 12)}
UNITS, SLABS = {}, {}
_u = _s = 0
for _name, (_slabs, _units) in PHASES.items():
    UNITS[_name], SLABS[_name] = _u, _s
    _u += _slabs * _units
    _s += _slabs

B0, B1, COND, FGAIN, SUBLN, LAMB = 0, 96, 192, 224, 240, 242
CONV = (246, 246 + 3 * 88 + 3 * 16)
SCONV = 246 + 3 * 88
VECS = 246 + 3 * 88 + 3 * 16 + 3 * 88
SH1, SC1, G1, SH2, SC2, G2 = (16 * n for n in range(6))

ADA_AT = {"k": -1, "v": 7, "up0": 16, "dn0": 20, "sin": 28, "up1": 36}

O_FIRST = ((0, 0), (0, 1), (1, 0), (1, 1), (0, 2), (1, 2), (0, 3), (1, 3))


def down_tiles(k):
    return (4 * k, 4) if k < 8 else (32 + 3 * (k - 8), 3)


def program(nc, x, c, ctx_in, c_ctx, w_ada, b_ada, w_qkv, w_o, lq1, lk1, lq2, lk2, subln, w_in, conv_in,
            w_out, w_up, conv_ffn, w_down, final_gain, ident_in, rope_cos_in, rope_sin_in, out):
    tiles = lambda w: w.rearrange("(t p) n -> p t n", p=P)
    qkv_w, o_w, in_w, out_w = tiles(w_qkv[0]), tiles(w_o[0]), tiles(w_in[0]), tiles(w_out[0])
    up_w, dn_w = [tiles(w_up[l]) for l in range(2)], [tiles(w_down[l]) for l in range(2)]
    ada_w = [tiles(w_ada[l]) for l in range(2)]
    x_rows = x[0].rearrange("(t p) n -> p t n", p=P)
    ctx_rows = ctx_in[0].rearrange("(t p) n -> p t n", p=P)
    out_rows = out[0].rearrange("(t p) n -> p t n", p=P)

    with ExitStack() as scope:
        KB = 1024
        start = (nc.sbuf_base + 63) // 64 * 64
        at_x = start
        at_u = at_x + 32 * KB
        at_res = at_u + 96 * KB
        at_raw = at_res + 16 * KB
        at_hi = at_raw + 16 * KB
        at_lo = at_hi + 16 * KB
        at_ada = at_lo + 16 * KB
        at_small = at_ada + 10 * KB
        small = [at_small]

        def at(name, shape, dt, offset):
            return nc.alloc_sbuf_tensor_at(name, shape, dt, offset=offset)

        def little(name, shape, dt=F32):
            n = 4
            for k in shape[1:]:
                n *= k
            n = (n + 31) // 32 * 32
            t = at(name, shape, dt, small[0])
            small[0] += n
            return t

        xs = at("xs", [P, KT, 2 * T], F32R, at_x)
        res = at("res", [P, KT, T], F32, at_res)
        raw = at("raw", [P, RING, KU, SLAB], F32, at_raw)
        w_hi = at("w_hi", [P, RING, KU, SLAB], F32R, at_hi)
        w_lo = at("w_lo", [P, RING, KU, SLAB], F32R, at_lo)
        ada_ring = at("ada_ring", [P, 2, 2, ADA_COLS], F32, at_ada)
        ada_sum = at("ada_sum", [P, ADA_COLS], F32, at_ada + 8 * KB)
        ada_sum_b = at("ada_sum_b", [P, ADA_COLS], F32, at_res + 6 * KB)
        ada_ring_kv = at("ada_ring_kv", [P, 2, 2, ADA_COLS], F32, at_res + 8 * KB)
        ada_slot = lambda n: ada_ring[:, n, :, :] if n < ADA_SLOTS else ada_ring_kv[:, n - ADA_SLOTS, :, :]
        x_tok = at("x_tok", [P, 2, D], F32, at_u)
        ctx_tok = at("ctx_tok", [P, 2, D], F32, at_u + 16 * KB)
        xn_l = at("xn_l", [P, KT, T], F32, at_res)
        xn_c = at("xn_c", [P, KT, T], F32, at_u + 32 * KB)
        start_ring = at("start_ring", [P, 4, 2, ADA_COLS], F32, at_u + 48 * KB)
        vec_rows = at("vec_rows", [P, 8, P], F32, at_hi)
        mod_rows = at("mod_rows", [2, 2, ADA_COLS], F32, at_ada + 4 * KB)
        sums_ring = at("sums_ring", [P, 4, 2, ADA_COLS], F32, at_u)
        start_sum = at("start_sum", [P, 2, ADA_COLS], F32, at_ada)
        squares = at("squares", [P, D], F32, at_lo)
        k_t = at("k_t", [P, 2 * HEADS, 2 * T], F32, at_u)
        v_rows = at("v_rows", [P, 4, D], F32, at_u + 32 * KB)
        cs = at("cs", [P, KT, 2 * T], F32R, at_u + 64 * KB)
        attn = at_u + 64 * KB
        probs = at("probs", [P, 2, 512], F32, attn)
        a_t = at("a_t", [P, 2, 512], F32, attn + 4 * KB)
        q_head = at("q_head", [P, 2, 2, T], F32, attn + 8 * KB)
        o_feat = at("o_feat", [P, 2, T], F32, attn + 12 * KB)
        o_square = at("o_square", [P, T], F32, attn + 14 * KB)
        o_rows = at("o_rows", [P, 2, 2, T], F32, attn + 16 * KB)
        heads_out = at("heads_out", [P, KT, 2 * T], F32R, at_u)
        x_again = at("x_again", [P, 2, D], F32, at_x)
        y_qk = at("y_qk", [P, 2, T], F32, at_res)
        rot = at("rot", [P, 2, T], F32, at_res + 2 * KB)
        rope_cos = at("rope_cos", [P, T], F32, at_res + 4 * KB)
        rope_sin = at("rope_sin", [P, T], F32, at_res + 5 * KB)
        act = at("act", [P, FT, 2 * T], F32R, at_u)
        z = at("z", [P, KT, 2 * T], F32R, at_u)
        y = at("y", [P, 2, T], F32, at_u + 88 * KB)
        part_a = at("part_a", [P, 2, T], F32, at_u + 90 * KB)
        part_b = at("part_b", [P, 2, T], F32, at_u + 92 * KB)
        part_c = at("part_c", [P, 2, T], F32, at_u + 94 * KB)
        out_tok = at("out_tok", [P, 2, D], F32, at_x)
        ident = little("ident", [P, P])
        ones = little("ones", [P, P])
        vec = little("vec", [P, VECS])
        cond = little("cond", [P, 2, KT])
        ctx_mod = little("ctx_mod", [P, 32])
        row_sum = little("row_sum", [P, 4])
        row_var = little("row_var", [P, 4])
        row_inv = little("row_inv", [P, 4])
        row_rstd = little("row_rstd", [P, 4])
        lam_prod = little("lam_prod", [P, 2])
        lam_exp = little("lam_exp", [P, 2])
        neg_lam = little("neg_lam", [P, 1])
        gain_o = little("gain_o", [P, 2])
        s_max = little("s_max", [P, 2])
        s_neg = little("s_neg", [P, 2])
        s_sum = little("s_sum", [P, 2])
        s_inv = little("s_inv", [P, 2])
        s_lam = little("s_lam", [P, 1])
        o_sum = little("o_sum", [P, 2, HEADS])
        o_inv = little("o_inv", [P, 2, HEADS])
        o_rstd = little("o_rstd", [P, 2, HEADS])
        assert small[0] <= nc.sbuf_usable_end, (small[0], nc.sbuf_usable_end)

        ps = scope.enter_context(nc.psum_tensor("ps", [P, 8, 512], F32))

        sem = lambda name: scope.enter_context(nc.semaphore(name))
        vecs_loaded, ident_loaded, x_loaded, ctx_loaded = sem("vecs_loaded"), sem("ident_loaded"), sem("x_loaded"), sem("ctx_loaded")
        rope_loaded = sem("rope_loaded")
        start_full = [sem(f"start_full{n}") for n in range(4)]
        start_used = sem("start_used")
        sums_full = [sem(f"sums_full{n}") for n in range(4)]
        start_step, start_reduced = sem("start_step"), sem("start_reduced")
        ones_made, vecs_turned, vecs_made, plus_one = sem("ones_made"), sem("vecs_turned"), sem("vecs_made"), sem("plus_one")
        cond_made, lam_multiplied, lam_summed, lam_exped, lam_part, lam_made = (
            sem("cond_made"), sem("lam_multiplied"), sem("lam_summed"), sem("lam_exped"), sem("lam_part"), sem("lam_made"))
        rows_squared, rows_var, rows_inv, rows_rstd, rows_normed = (
            sem("rows_squared"), sem("rows_var"), sem("rows_inv"), sem("rows_rstd"), sem("rows_normed"))
        xn_turned, xn_kept, ctx_kept = sem("xn_turned"), sem("xn_kept"), sem("ctx_kept")
        mod_copied, mod_turned, mod_made, h_made, h_hi = (
            sem("mod_copied"), sem("mod_turned"), sem("mod_made"), sem("h_made"), sem("h_hi"))
        raw_full = [sem(f"raw_full{n}") for n in range(RING)]
        hi_made, lo_made, w_used = sem("hi_made"), sem("lo_made"), sem("w_used")
        ada_full = [sem(f"ada_full{n}") for n in range(ADA_SLOTS_KV)]
        ada_step, ada_reduced, ada_added = sem("ada_step"), sem("ada_reduced"), sem("ada_added")
        a_copied, acc_read = sem("a_copied"), sem("acc_read")
        ctx_copied, ctx_read = sem("ctx_copied"), sem("ctx_read")
        xs_ready = sem("xs_ready")
        rot_made, rope_part, rope_done = sem("rot_made"), sem("rope_part"), sem("rope_done")
        taps_mid, taps_first, taps_done = sem("taps_mid"), sem("taps_first"), sem("taps_done")
        silu_made, gated, act_hi_made, act_made = sem("silu_made"), sem("gated"), sem("act_hi_made"), sem("act_made")
        gx_made, z_mul, z_hi_made, z_made = sem("gx_made"), sem("z_mul"), sem("z_hi_made"), sem("z_made")
        res_made, sq_made, sq_added, sq_used = sem("res_made"), sem("sq_made"), sem("sq_added"), sem("sq_used")
        var_made, inv_made, rstd_made, xm_made, xh_made, xh_hi = (
            sem("var_made"), sem("inv_made"), sem("rstd_made"), sem("xm_made"), sem("xh_made"), sem("xh_hi"))
        scores_made, max_made, neg_made, exp_done = sem("scores_made"), sem("max_made"), sem("neg_made"), sem("exp_done")
        sum_inv, lam_scaled, p1_scaled, a_made = sem("sum_inv"), sem("lam_scaled"), sem("p1_scaled"), sem("a_made")
        at_made, at_copied, o_made, o_copied, o_squared = (
            sem("at_made"), sem("at_copied"), sem("o_made"), sem("o_copied"), sem("o_squared"))
        o_var, o_inverted, o_root, o_normed, o_turned, o_gained, o_hi = (
            sem("o_var"), sem("o_inverted"), sem("o_root"), sem("o_normed"), sem("o_turned"), sem("o_gained"), sem("o_hi"))
        xt_turned, xt_kept, xt_loaded = sem("xt_turned"), sem("xt_kept"), sem("xt_loaded")
        fin_gained, fin_turned, fin_kept, fin_stored = sem("fin_gained"), sem("fin_turned"), sem("fin_kept"), sem("fin_stored")
        fin_scaled = [sem("fin_scaled0"), sem("fin_scaled1")]

        block = scope.enter_context(nc.Block())

        def wait(eng, s, n):
            if isinstance(n, int) and n <= 0:
                return
            eng.wait_ge(s, n)

        def first(i, h):
            return isinstance(i, int) and i == 0 and h == 0

        def loop(eng, n, body):
            body(0)
            if n > 1:
                with eng.Fori(1, n) as i:
                    body(i)

        def pair_loop(eng, body):
            body(0)
            body(1)
            with eng.Fori(2, 4) as i:
                body(i)

        def o_loop(eng, body):
            body(1)
            with eng.Fori(2, 4) as i:
                body(i)

        def up_loop(eng, body):
            body(0, True)
            with eng.Fori(1, 4) as i:
                body(i, True)
            with eng.Fori(4, FT // 4) as i:
                body(i, False)

        @block.sync
        def _(sp):
            def ada_rows(q, col):
                return ada_w[0][:, 2 * q:2 * q + 2, col:col + ADA_COLS]

            def to_multiply(n, q, col):
                wait(sp, start_used, n - 3)
                sp.dma_start(start_ring[:, q % 4, :, :], ada_rows(q, col)).then_inc(start_full[q % 4], 16)

            def to_sum(n, q, col):
                wait(sp, start_step, 4 * (n - 3))
                sp.dma_start(sums_ring[:, q % 4, :, :], ada_rows(q, col)).then_inc(sums_full[q % 4], 16)

            def load(quad, slot, w, tile, n_tiles, col):
                wait(sp, lo_made, 4 * quad + slot - 3)
                sp.dma_start(raw[:, slot, 0:n_tiles, :], w[:, tile:tile + n_tiles, bass.ds(col, SLAB)]
                             ).then_inc(raw_full[slot], 16)

            def k_unit(s, k):
                load(s + UNITS["k"] // 4, k, qkv_w, 4 * k, 4, s * SLAB + QK)

            for b, col in enumerate((SC1, SH1)):
                for q in range(8):
                    if b == 1 and q == 4:
                        sp.wait_ge(xn_turned, 8)
                        for r in range(4):
                            to_sum(r, r, SC1 * P + ADA_COLS)
                    to_multiply(8 * b + q, q, col * P)
            for g in range(1, 4):
                for q in range(8):
                    if g > 1 or q > 3:
                        to_sum(8 * (g - 1) + q, q, SC1 * P + g * ADA_COLS)
                    to_multiply(8 * (g + 1) + q, q, SH1 * P + g * ADA_COLS)
                    if q == 3:
                        k_unit(0, g - 1)
            k_unit(0, 3)
            with sp.Fori(1, 8) as s:
                for k in range(4):
                    k_unit(s, k)

            def plain(phase, w, base):
                with sp.Fori(0, 8) as s:
                    for k in range(4):
                        load(s + UNITS[phase] // 4, k, w, 4 * k, 4, s * SLAB + base)

            def up(phase, w):
                with sp.Fori(0, FT // 2) as j:
                    for h in range(2):
                        for k in range(4):
                            load(2 * j + (UNITS[phase] // 4 + h), k, w, 4 * k, 4, j * SLAB + h * D_FF)

            def down(phase, w):
                with sp.Fori(0, 8) as s:
                    for k in range(12):
                        tile, n = down_tiles(k)
                        load(3 * s + (UNITS[phase] // 4 + k // 4), k % 4, w, tile, n, s * SLAB)

            plain("v", qkv_w, 2 * QK)
            plain("q", qkv_w, 0)
            for n, (s, k) in enumerate(O_FIRST):
                load(UNITS["o"] // 4 + n // 4, n % 4, o_w, 4 * k, 4, s * SLAB)
            with sp.Fori(2, 8) as s:
                for k in range(4):
                    load(s + UNITS["o"] // 4, k, o_w, 4 * k, 4, s * SLAB)
            up("up0", up_w[0])
            down("dn0", dn_w[0])
            with sp.Fori(1, 9) as n:
                for h, first in ((0, D), (1, 2 * D), (2, 0)):
                    for k in range(4):
                        load(3 * n + (UNITS["sin"] // 4 + h - 3), k, in_w, 4 * k, 4, n * SLAB + (first - SLAB))
            plain("so", out_w, 0)
            up("up1", up_w[1])
            down("dn1", dn_w[1])
            for t in range(2):
                sp.wait_ge(fin_scaled[t], 1)
                sp.dma_start(out_rows[:, t, :], out_tok[:, t, :]).then_inc(fin_stored, 16)
            sp.wait_ge(fin_stored, 32)

        @block.gpsimd
        def _(pool):
            nc.gpsimd.memset(ones[:, :], 1.0).then_inc(ones_made, 1)

            def ada_slab(j, layer, col, slots=ADA_SLOTS):
                for q in range(8):
                    if isinstance(j, int) and q == 0:
                        pool.wait_ge(xs_ready, 8)
                        pool.dma_start(rope_cos[:, :], rope_cos_in).then_inc(rope_loaded, 16)
                        pool.dma_start(rope_sin[:, :], rope_sin_in).then_inc(rope_loaded, 16)
                    wait(pool, ada_step, 16 * j + (2 * q + 2 - 2 * slots))
                    pool.dma_start(ada_slot(q % slots),
                                   ada_w[layer][:, 2 * q:2 * q + 2, bass.ds(col, ADA_COLS)]
                                   ).then_inc(ada_full[q % slots], 16)

            loop(pool, 16, lambda j: ada_slab(j, 0, j * ADA_COLS + ADA_FIRST * ADA_COLS, ADA_SLOTS_KV))
            pool.wait_ge(w_used, UNITS["o"])
            pool.dma_start(x_again[:, :, :], x_rows).then_inc(xt_loaded, 16)
            with pool.Fori(16, 40) as j:
                ada_slab(j, 1, j * ADA_COLS + (-16 * ADA_COLS))

        @block.scalar
        def _(se):
            se.dma_start(ident[:, :], ident_in).then_inc(ident_loaded, 16)
            rows = lambda v: v.rearrange("(t p) -> t p", p=P)
            r = vec_rows
            loads = [(r[0:96, 0, :], rows(b_ada[0])), (r[96:112, 0, :], rows(c[0])), (r[112:128, 0, :], rows(c_ctx)),
                     (r[0:96, 1, :], rows(b_ada[1])), (r[96:112, 1, :], rows(final_gain)),
                     (r[112:114, 1, :], rows(subln[0])), (r[114:115, 1, :], lq1), (r[115:116, 1, :], lk1),
                     (r[116:117, 1, :], lq2), (r[117:118, 1, :], lk2)]
            for n in range(3):
                loads += [(r[0:88, 2 + n, :], rows(conv_ffn[0, n])), (r[88:104, 2 + n, :], rows(conv_in[0, n])),
                          (r[0:88, 5 + n, :], rows(conv_ffn[1, n]))]
            for dst, src in loads:
                se.dma_start(dst, src).then_inc(vecs_loaded, 16)
            assert len(loads) == 19
            se.dma_start(x_tok[:, :, :], x_rows).then_inc(x_loaded, 16)
            se.dma_start(ctx_tok[:, :, :], ctx_rows).then_inc(ctx_loaded, 16)

            se.wait_ge(vecs_made, 1)
            nc.scalar.activation(cond[:, :, :], vec[:, COND:COND + 32].rearrange("p (c k) -> p c k", c=2), ACT.Silu).then_inc(cond_made, 1)
            se.wait_ge(lam_summed, 1)
            nc.scalar.activation(lam_exp[:, :], ps[:, 3, 0:2], ACT.Exp).then_inc(lam_exped, 1)
            for n, (loaded, tok) in enumerate(((x_loaded, x_tok), (ctx_loaded, ctx_tok))):
                se.wait_ge(loaded, 16)
                for t in range(2):
                    wait(se, rows_squared, 2 * n + t)
                    nc.scalar.activation(squares[:, :], tok[:, t, :], ACT.Square,
                                         accum_out=row_sum[:, 2 * n + t:2 * n + t + 1]).then_inc(rows_squared, 1)
            se.wait_ge(rows_inv, 1)
            nc.scalar.activation(row_rstd[:, :], row_inv[:, :], ACT.Sqrt).then_inc(rows_rstd, 1)

            def copy_rows(b, n, n_used):
                se.wait_ge(start_used, n_used)
                wait(se, mod_turned, n)
                nc.scalar.activation(mod_rows[:, b, :], ps[0:2, 6 + b, :], ACT.Copy).then_inc(mod_copied, 1)

            def modulate(g):
                se.wait_ge(mod_made, 2 * g + 2)
                for m, (xn, dst) in enumerate(((xn_l, xs), (xn_c, cs))):
                    table = ctx_mod if m else vec
                    for k in range(4 * g, 4 * g + 4):
                        last = nc.scalar.activation(xn[:, k, :], xn[:, k, :], ACT.Identity,
                                                    scale=table[:, SC1 + k:SC1 + k + 1], bias=table[:, SH1 + k:SH1 + k + 1])
                    last.then_inc(h_made, 1)
                    se.wait_ge(h_made, 2 * g + (m + 1))
                    nc.scalar.activation(dst[:, 4 * g:4 * g + 4, 0:T], xn[:, 4 * g:4 * g + 4, :], ACT.Copy).then_inc(h_hi, 1)

            def hi(quad, slot, n_tiles=KU):
                se.wait_ge(raw_full[slot], 16 * quad + 16)
                wait(se, w_used, 4 * quad + slot - 3)
                nc.scalar.activation(w_hi[:, slot, 0:n_tiles, :], raw[:, slot, 0:n_tiles, :], ACT.Copy).then_inc(hi_made, 1)

            copy_rows(0, 0, 8)
            copy_rows(1, 0, 16)
            for i in range(8):
                se.wait_ge(xn_turned, 8 + i + 1)
                nc.scalar.activation(xn_c[:, 2 * i:2 * i + 2, :], ps[:, i % 2, :].rearrange("p (k t) -> p k t", k=2), ACT.Copy
                                     ).then_inc(ctx_kept, 1)
            se.wait_ge(xn_kept, 8)
            se.wait_ge(ctx_kept, 8)
            modulate(0)
            for g in range(1, 4):
                hi(0, g - 1)
                copy_rows(1, g + 1, 8 * g + 16)
                modulate(g)
            hi(0, 3)

            def copy_a(phase, s, bank, dst, per_slab=4):
                if phase == "o" and isinstance(s, int) and s == 0:
                    se.wait_ge(w_used, UNITS["o"] + O_FIRST.index((0, 3)) + 1)
                else:
                    se.wait_ge(w_used, per_slab * s + (UNITS[phase] + per_slab))
                nc.scalar.activation(dst, ps[:, bank:bank + 2, 0:T], ACT.Copy).then_inc(a_copied, 1)

            def rotate(n):
                se.wait_ge(acc_read, n + 1)
                for d in range(4):
                    last = nc.scalar.activation(rot[32 * d:32 * d + 32, :, :], y_qk[32 * (d ^ 1):32 * (d ^ 1) + 32, :, :], ACT.Copy)
                last.then_inc(rot_made, 1)

            def k_point(k, s, h):
                if k == 2:
                    se.wait_ge(w_used, 4 * s + (UNITS["k"] + 4))
                    nc.scalar.activation(k_t[:, bass.ds(2 * s, 2), T:2 * T], ps[:, 2:4, 0:T], ACT.Copy).then_inc(ctx_copied, 1)
                    wait(se, rope_done, s)
                    copy_a("k", s, 4 * h, y_qk[:, :, :])
                if k == 3:
                    rotate(s + SLABS["k"])

            def v_point(k, s, h):
                if k == 2:
                    copy_a("v", s, 4 * h, v_rows[:, 0:2, bass.ds(s * SLAB, SLAB)])

            def q_point(s, h):
                se.wait_ge(rope_done, s + 8)
                copy_a("q", s, 2 * h, y_qk[:, :, :])
                rotate(s + SLABS["q"])

            def res_point(k, phase, s, h, n_res, per_slab=4):
                if k == 2:
                    wait(se, res_made, s + n_res)
                    copy_a(phase, s, 2 * h, y[:, :, :], per_slab)
                if k == 3:
                    se.wait_ge(res_made, s + (n_res + 1))
                    wait(se, sq_added, s + n_res)
                    nc.scalar.activation(part_c[:, :, :], res[:, bass.ds(2 * s, 2), :], ACT.Square).then_inc(sq_made, 1)
                    if phase == "dn1":
                        gained(s)

            def gained(s):
                wait(se, fin_turned, s)
                for m in range(2):
                    last = nc.scalar.activation(part_a[:, m, :], res[:, bass.ds(2 * s + m, 1), :], ACT.Copy,
                                                scale=vec[:, bass.ds(2 * s + (FGAIN + m), 1)])
                last.then_inc(fin_gained, 1)

            def keep_rows(s, h):
                se.wait_ge(fin_turned, s + 1)
                nc.scalar.activation(out_tok[:, :, bass.ds(2 * P * s, 2 * P)],
                                     ps[:, 4 + h, :].rearrange("p (t f) -> p t f", t=2), ACT.Copy).then_inc(fin_kept, 1)

            def norm_tail(n_norm, table):
                se.wait_ge(inv_made, n_norm + 1)
                nc.scalar.activation(part_c[:, 1, :], part_c[:, 0, :], ACT.Sqrt).then_inc(rstd_made, 1)

                def two(i):
                    for b, part in ((0, part_a), (1, part_b)):
                        n = 2 * i + b
                        se.wait_ge(xm_made, n + (8 * n_norm + 1))
                        for m in range(2):
                            last = nc.scalar.activation(part[:, m, :], part[:, m, :], ACT.Identity,
                                                        scale=vec[:, bass.ds(2 * n + (table + 16 + m), 1)],
                                                        bias=vec[:, bass.ds(2 * n + (table + m), 1)])
                        last.then_inc(xh_made, 1)
                        se.wait_ge(xh_made, n + (8 * n_norm + 1))
                        nc.scalar.activation(xs[:, bass.ds(2 * n, 2), 0:T], part[:, :, :], ACT.Copy).then_inc(xh_hi, 1)
                with se.Fori(0, 4) as i:
                    two(i)

            def up_copy(phase, j, which, h):
                wait(se, taps_done, 2 * j + (TAPS[phase] + which))
                copy_a(phase, 2 * j + which, 2 * h, y[:, :, :])

            def up_mid(phase, j, which, part):
                se.wait_ge(acc_read, 2 * j + (SLABS[phase] + which + 1))
                for m in range(2):
                    last = nc.scalar.activation(part[:, m, :], y[:, m, :], ACT.Copy,
                                                scale=vec[:, bass.ds(2 * j + tap_column(phase, which, m, 1), 1)])
                last.then_inc(taps_mid, 1)

            def up_silu(phase, j):
                se.wait_ge(taps_done, 2 * j + (TAPS[phase] + 1))
                nc.scalar.activation(part_a[:, :, :], part_a[:, :, :], ACT.Silu).then_inc(silu_made, 1)

            def up_hi(phase, j):
                se.wait_ge(gated, j + (PAIRS[phase] + 1))
                nc.scalar.activation(act[:, bass.ds(2 * j, 2), 0:T], part_a[:, :, :], ACT.Copy).then_inc(act_hi_made, 1)

            def g_point(k, phase, j, h):
                if k == 2:
                    up_copy(phase, j, 0, h)
                if k == 3:
                    wait(se, act_made, j + PAIRS[phase])
                    up_mid(phase, j, 0, part_a)

            def v_up_point(k, phase, j, h):
                if k == 0:
                    up_silu(phase, j)
                if k == 2:
                    up_copy(phase, j, 1, h)
                if k == 3:
                    up_mid(phase, j, 1, part_b)

            def k_pair(i):
                for h in range(2):
                    for k in range(4):
                        if not first(i, 0):
                            hi(2 * i + h, k)
                            k_point(k, 2 * i + (h - 1), 1 - h)
                        elif h == 0:
                            hi(1, k)
                            if k in (1, 3):
                                k_point(2 + k // 2, 0, 0)
            pair_loop(se, k_pair)

            def v_pair(i):
                for h in range(2):
                    for k in range(4):
                        hi(2 * i + (UNITS["v"] // 4 + h), k)
                        if first(i, h):
                            k_point(k, 7, 1)
                        else:
                            v_point(k, 2 * i + (h - 1), 1 - h)
            loop(se, 4, v_pair)

            def exponentials(h, t):
                n = 2 * h + t
                se.wait_ge(neg_made, n + 1)
                wait(se, at_made, n)
                for b in range(2):
                    nc.scalar.activation(probs[:, b, :], ps[:, 4 + b, :], ACT.Exp, scale=SCALE, bias=s_neg[:, b:b + 1],
                                         accum_out=s_sum[:, b:b + 1]).then_inc(exp_done, 1)

            def keep_a(h, t):
                n = 2 * h + t
                se.wait_ge(at_made, n + 1)
                wait(se, o_made, n - 1)
                nc.scalar.activation(a_t[:, t, :], ps[:, 6, :], ACT.Copy).then_inc(at_copied, 1)

            def square_o(h, parity):
                for t in range(2):
                    n = 2 * h + t
                    se.wait_ge(o_copied, n + 1)
                    wait(se, o_squared, n)
                    nc.scalar.activation(o_square[:, :], o_rows[:, parity, t, :], ACT.Square,
                                         accum_out=o_sum[:, t, bass.ds(h, 1)]).then_inc(o_squared, 1)

            def root(h):
                se.wait_ge(o_inverted, h + 1)
                nc.scalar.activation(o_rstd[:, :, bass.ds(h, 1)], o_inv[:, :, bass.ds(h, 1)], ACT.Sqrt).then_inc(o_root, 1)

            def gain(h):
                se.wait_ge(o_turned, h + 1)
                se.wait_ge(xs_ready, h + 8)
                for m in range(2):
                    last = nc.scalar.activation(o_feat[:, m, :], ps[:, 6, T * m:T * m + T], ACT.Copy, scale=gain_o[:, m:m + 1])
                last.then_inc(o_gained, 1)
                se.wait_ge(o_gained, h + 1)
                nc.scalar.activation(heads_out[:, bass.ds(2 * h, 2), 0:T], o_feat[:, :, :], ACT.Copy).then_inc(o_hi, 1)

            def attention_point(k, h, parity):
                at = lambda m: not isinstance(h, int) or 0 <= h + m < HEADS
                if k == 0:
                    if at(-1):
                        keep_a(h + (-1), 1)
                    if at(0):
                        exponentials(h, 0)
                if k == 1 and at(-2):
                    root(h + (-2))
                if k == 2 and at(0):
                    keep_a(h, 0)
                    exponentials(h, 1)
                if k == 3:
                    if at(-2):
                        gain(h + (-2))
                    if at(-1):
                        square_o(h + (-1), 1 - parity)

            def q_pair(i):
                for h in range(2):
                    for k in range(4):
                        hi(2 * i + (UNITS["q"] // 4 + h), k)
                        if first(i, h):
                            v_point(k, 7, 1)
                        elif k == 2:
                            q_point(2 * i + (h - 1), 1 - h)
                        attention_point(k, 2 * i + (h - 2), h)
            pair_loop(se, q_pair)

            def keep_x(*parts):
                for n in parts:
                    se.wait_ge(xt_turned, n + 1)
                    nc.scalar.activation(res[:, 2 * n:2 * n + 2, :], ps[:, 4 + n % 2, :].rearrange("p (k t) -> p k t", k=2), ACT.Copy).then_inc(xt_kept, 1)

            o_hi_unit = lambda n: hi(UNITS["o"] // 4 + n // 4, n % 4)
            for k in range(4):
                o_hi_unit(k)
                if k == 2:
                    q_point(7, 1)
                attention_point(k, 6, 0)
            attention_point(0, 7, 1)
            attention_point(1, 7, 1)
            o_hi_unit(4)
            attention_point(2, 7, 1)
            attention_point(3, 7, 1)
            o_hi_unit(5)
            attention_point(0, 8, 0)
            keep_x(0, 1)
            attention_point(1, 8, 0)
            o_hi_unit(6)
            attention_point(3, 8, 0)
            attention_point(1, 9, 1)
            o_hi_unit(7)
            attention_point(3, 9, 1)
            keep_x(2, 3, 4, 5, 6, 7)

            def o_pair(i):
                for h in range(2):
                    for k in range(4):
                        hi(2 * i + (UNITS["o"] // 4 + h), k)
                        if isinstance(i, int) and h == 0 and k < 2:
                            res_point(k + 2, "o", 0, 0, RES["o"])
                        res_point(k, "o", 2 * i + (h - 1), 1 - h, RES["o"])
            o_loop(se, o_pair)

            def up(phase, tail):
                def four(i, ada):
                    for p in range(2):
                        for h in range(2):
                            for k in range(4):
                                hi(4 * i + (UNITS[phase] // 4 + 2 * p + h), k)
                                if first(i, p + h):
                                    tail(k)
                                elif h == 0:
                                    v_up_point(k, phase, 2 * i + (p - 1), 1)
                                else:
                                    g_point(k, phase, 2 * i + p, 0)
                                    if k == 1 and not first(i, p):
                                        up_hi(phase, 2 * i + (p - 1))
                up_loop(se, four)

            def down(phase, up_phase):
                def pair(i):
                    for h in range(2):
                        for k in range(12):
                            hi(6 * i + (UNITS[phase] // 4 + 3 * h + k // 4), k % 4, down_tiles(k)[1])
                            if first(i, h):
                                v_up_point(k, up_phase, FT // 2 - 1, 1)
                                if k == 5:
                                    up_hi(up_phase, FT // 2 - 1)
                            else:
                                res_point(k, phase, 2 * i + (h - 1), 1 - h, RES[phase], 12)
                                if phase == "dn1" and k == 8:
                                    keep_rows(2 * i + (h - 1), 1 - h)
                loop(se, 4, pair)

            def o_tail(k):
                res_point(k, "o", 7, 1, RES["o"])
                if k == 3:
                    se.wait_ge(ada_added, 12)
                    norm_tail(0, B0 + SH2)
            up("up0", o_tail)
            down("dn0", "up0")

            def sin_point(k, j, h, which):
                if which == 0:
                    if k == 2:
                        wait(se, gx_made, j)
                        copy_a("sin", 3 * j, 2 * h, part_a[:, :, :])
                elif which == 1:
                    if k == 2:
                        wait(se, taps_done, j + TAPS["sin"])
                        copy_a("sin", 3 * j + 1, 2 * h, y[:, :, :])
                    if k == 3:
                        se.wait_ge(gx_made, j + 1)
                        wait(se, z_mul, j)
                        for m in range(2):
                            last = nc.scalar.activation(part_b[:, m, :], y[:, m, :], ACT.Copy,
                                                        scale=vec[:, bass.ds(2 * j + (SCONV + 16 + m), 1)])
                        last.then_inc(taps_mid, 1)
                else:
                    if k == 2:
                        wait(se, z_made, j)
                        copy_a("sin", 3 * j + 2, 2 * h, part_c[:, :, :])
                    if k == 3:
                        se.wait_ge(z_mul, j + 1)
                        nc.scalar.activation(z[:, bass.ds(2 * j, 2), 0:T], part_c[:, :, :], ACT.Copy).then_inc(z_hi_made, 1)

            def sin_six(i):
                for n in range(6):
                    for k in range(4):
                        hi(6 * i + (UNITS["sin"] // 4 + n), k)
                        if first(i, n):
                            res_point(k, "dn0", 7, 1, RES["dn0"], 12)
                            if k == 3:
                                se.wait_ge(ada_added, 24)
                                norm_tail(1, B1 + SH1)
                        elif n % 3 == 0:
                            sin_point(k, 2 * i + (n // 3 - 1), (n - 1) % 2, 2)
                        else:
                            sin_point(k, 2 * i + n // 3, (n - 1) % 2, n % 3 - 1)
            loop(se, 4, sin_six)

            def so_pair(i):
                for h in range(2):
                    for k in range(4):
                        hi(2 * i + (UNITS["so"] // 4 + h), k)
                        if first(i, h):
                            sin_point(k, 7, 1, 2)
                        else:
                            res_point(k, "so", 2 * i + (h - 1), 1 - h, RES["so"])
            loop(se, 4, so_pair)

            def so_tail(k):
                res_point(k, "so", 7, 1, RES["so"])
                if k == 3:
                    norm_tail(2, B1 + SH2)
            up("up1", so_tail)
            down("dn1", "up1")
            for k in range(4):
                res_point(k, "dn1", 7, 1, RES["dn1"], 12)
            keep_rows(7, 1)
            se.wait_ge(rows_inv, 2)
            nc.scalar.activation(row_rstd[:, 0:2], row_inv[:, 0:2], ACT.Sqrt).then_inc(rows_rstd, 1)
            se.wait_ge(fin_kept, 8)
            se.wait_ge(rows_rstd, 2)
            nc.scalar.activation(out_tok[:, 1, :], out_tok[:, 1, :], ACT.Copy, scale=row_rstd[:, 1:2]).then_inc(fin_scaled[1], 1)

        @block.vector
        def _(ve):
            ve.wait_ge(vecs_turned, 1)
            spans = [(0, 0, 96, B0), (0, 96, 32, COND), (1, 0, 96, B1), (1, 96, 16 + 2 + 4, FGAIN)]
            for n in range(3):
                spans += [(2 + n, 0, 88, CONV[0] + 88 * n), (2 + n, 88, 16, SCONV + 16 * n), (5 + n, 0, 88, CONV[1] + 88 * n)]
            for tile, first_col, n, dst in spans:
                last = nc.vector.tensor_copy(vec[:, dst:dst + n],
                                             ps[:, tile // 4, 128 * (tile % 4) + first_col:128 * (tile % 4) + first_col + n])
            last.then_inc(vecs_made, 1)
            ve.wait_ge(vecs_made, 1)
            for base in (B0, B1):
                for scale in (SC1, SC2):
                    v = vec[:, base + scale:base + scale + 16]
                    last = nc.vector.tensor_scalar(v, v, 1.0, None, ALU.add)
            last.then_inc(plus_one, 1)
            lam4 = vec[:, LAMB:LAMB + 4].rearrange("p (n two) -> p two n", two=2)
            nc.vector.tensor_tensor(lam_prod[:, :], lam4[:, 0, :], lam4[:, 1, :], ALU.mult).then_inc(lam_multiplied, 1)
            nc.vector.tensor_scalar(gain_o[:, :], vec[:, SUBLN:SUBLN + 2], 1.0 - LAM_INIT, None, ALU.mult)
            ve.wait_ge(plus_one, 1)
            nc.vector.tensor_copy(ctx_mod[:, :], vec[:, 0:32]).then_inc(plus_one, 1)
            ve.wait_ge(lam_exped, 1)
            nc.vector.tensor_tensor(neg_lam[:, :], lam_exp[:, 1:2], lam_exp[:, 0:1], ALU.subtract).then_inc(lam_part, 1)
            ve.wait_ge(lam_part, 1)
            nc.vector.tensor_scalar(neg_lam[:, :], neg_lam[:, :], LAM_INIT, None, ALU.subtract).then_inc(lam_made, 1)

            ve.wait_ge(rows_squared, 4)
            nc.vector.tensor_scalar(row_var[:, :], row_sum[:, :], 1.0 / D, EPS, ALU.mult, ALU.add).then_inc(rows_var, 1)
            ve.wait_ge(rows_var, 1)
            nc.vector.reciprocal(row_inv[:, :], row_var[:, :]).then_inc(rows_inv, 1)
            ve.wait_ge(rows_rstd, 1)
            for n, tok in enumerate((x_tok, ctx_tok)):
                for t in range(2):
                    nc.vector.tensor_scalar(tok[:, t, :], tok[:, t, :], row_rstd[:, 2 * n + t:2 * n + t + 1], None, ALU.mult
                                            ).then_inc(rows_normed, 1)
            for i in range(8):
                ve.wait_ge(xn_turned, i + 1)
                nc.vector.tensor_copy(xn_l[:, 2 * i:2 * i + 2, :], ps[:, i % 2, :].rearrange("p (k t) -> p k t", k=2)).then_inc(xn_kept, 1)

            ve.wait_ge(plus_one, 2)

            def add_mod(col, products):
                for m, table in enumerate((vec, ctx_mod)):
                    v = table[:, col:col + 4]
                    last = nc.vector.tensor_tensor(v, v, products[:, m, :], ALU.add)
                last.then_inc(mod_made, 1)

            def low_h(g):
                for m, (xn, dst) in enumerate(((xn_l, xs), (xn_c, cs))):
                    ve.wait_ge(h_hi, 2 * g + (m + 1))
                    nc.vector.tensor_tensor(dst[:, 4 * g:4 * g + 4, T:2 * T], xn[:, 4 * g:4 * g + 4, :],
                                            dst[:, 4 * g:4 * g + 4, 0:T], ALU.subtract).then_inc(xs_ready, 1)

            def start_chunk(g, q):
                ve.wait_ge(sums_full[q % 4], 16 * (2 * (g - 1) + q // 4 + 1))
                for t in (2 * q, 2 * q + 1):
                    for m in range(2):
                        w, scalar = sums_ring[:, q % 4, t % 2, :], cond[:, m, t:t + 1]
                        if t == 0:
                            wait(ve, start_reduced, g - 1)
                            nc.vector.tensor_scalar(start_sum[:, m, :], w, scalar, None, ALU.mult).then_inc(start_step, 1)
                        else:
                            ve.wait_ge(start_step, 32 * (g - 1) + 2 * t + m - 1)
                            nc.vector.scalar_tensor_tensor(out=start_sum[:, m, :], in0=w, scalar=scalar, in1=start_sum[:, m, :],
                                                           op0=ALU.mult, op1=ALU.add).then_inc(start_step, 1)

            def lo(quad, slot, n_tiles=KU):
                ve.wait_ge(hi_made, 4 * quad + (slot + 1))
                nc.vector.tensor_tensor(w_lo[:, slot, 0:n_tiles, :], raw[:, slot, 0:n_tiles, :],
                                        w_hi[:, slot, 0:n_tiles, :], ALU.subtract).then_inc(lo_made, 1)

            turned = lambda b: ps[:, 4 + b, 0:8].rearrange("p (k c) -> p c k", c=2)
            for g in range(1, 4):
                for q in range(4):
                    start_chunk(g, q)
                    if g == 1 and q in (1, 3):
                        b = q // 2
                        ve.wait_ge(mod_turned, b + 1)
                        add_mod((SC1, SH1)[b], turned(b))
                if g > 1:
                    low_h(g - 1)
                for q in range(4, 7):
                    start_chunk(g, q)
                if g == 1:
                    low_h(0)
                lo(0, g - 1)
                start_chunk(g, 7)
                ve.wait_ge(start_reduced, g)
                add_mod(SC1 + 4 * g, ps[:, 4, 0:8].rearrange("p (c k) -> p c k", c=2))
                ve.wait_ge(mod_turned, g + 2)
                add_mod(SH1 + 4 * g, turned(1))
            low_h(3)
            lo(0, 3)

            def ada_chunk(j, q, sums=ada_sum, buffers=1):
                if buffers == 2:
                    slot = q % ADA_SLOTS_KV
                    ve.wait_ge(ada_full[slot], 32 * j + 16 * (q // ADA_SLOTS_KV + 1))
                else:
                    slot = q % ADA_SLOTS
                    ve.wait_ge(ada_full[slot], 64 * j + 16 * (q // ADA_SLOTS + 1 - 32))
                for b in range(2):
                    t = 2 * q + b
                    w, scalar = ada_slot(slot)[:, b, :], cond[:, 0, t:t + 1]
                    if t == 0:
                        wait(ve, ada_reduced, j + (1 - buffers))
                        nc.vector.tensor_scalar(sums[:, :], w, scalar, None, ALU.mult).then_inc(ada_step, 1)
                    else:
                        ve.wait_ge(ada_step, 16 * j + t)
                        nc.vector.scalar_tensor_tensor(out=sums[:, :], in0=w, scalar=scalar, in1=sums[:, :],
                                                       op0=ALU.mult, op1=ALU.add).then_inc(ada_step, 1)

            def ada_add(j):
                ve.wait_ge(ada_reduced, j + 1)
                v = vec[:, bass.ds(4 * j + 4 * ADA_FIRST, 4)]
                nc.vector.tensor_tensor(v, v, ps[:, 6, 0:4], ALU.add).then_inc(ada_added, 1)

            def ada_in_pair(phase, i, h, k):
                j = 2 * i + ADA_AT[phase]
                sums = (ada_sum, ada_sum_b)[h]
                ada_chunk(j + h, 2 * k, sums, 2)
                ada_chunk(j + h, 2 * k + 1, sums, 2)
                if k == 3 and not (phase == "k" and first(i, 0)):
                    ada_add(j + (h - 1))

            def ada_in_24(phase, i, n):
                j = 2 * i + ADA_AT[phase]
                if n < 8:
                    ada_chunk(j, n)
                if n == 11:
                    ada_add(j)
                if 11 <= n < 19:
                    ada_chunk(j + 1, n - 11)
                if n == 23:
                    ada_add(j + 1)

            def add_b(n, bank, dst):
                ve.wait_ge(a_copied, n + 1)
                nc.vector.tensor_tensor(dst, dst, ps[:, bank:bank + 2, T:2 * T], ALU.add).then_inc(acc_read, 1)

            two = lambda t: t[:, :].unsqueeze(1).broadcast_to([P, 2, T])

            def rope(r, dst, n_slabs):
                if isinstance(r, int) and r == 0:
                    ve.wait_ge(rope_loaded, 32)
                ve.wait_ge(acc_read, n_slabs + 1)
                nc.vector.tensor_tensor(dst, y_qk[:, :, :], two(rope_cos), ALU.mult)
                ve.wait_ge(rot_made, r + 1)
                nc.vector.tensor_tensor(rot[:, :, :], rot[:, :, :], two(rope_sin), ALU.mult).then_inc(rope_part, 1)
                ve.wait_ge(rope_part, r + 1)
                nc.vector.tensor_tensor(dst, dst, rot[:, :, :], ALU.add).then_inc(rope_done, 1)

            def k_point(k, s, h):
                if k == 2:
                    kc = k_t[:, bass.ds(2 * s, 2), T:2 * T]
                    ve.wait_ge(ctx_copied, s + 1)
                    nc.vector.tensor_tensor(kc, kc, ps[:, 2:4, T:2 * T], ALU.add).then_inc(ctx_read, 1)
                    add_b(s, 4 * h, y_qk[:, :, :])
                if k == 3:
                    rope(s, k_t[:, bass.ds(2 * s, 2), 0:T], s)

            def v_point(k, s, h):
                if k == 2:
                    ve.wait_ge(a_copied, s + (SLABS["v"] + 1))
                    nc.vector.tensor_copy(v_rows[:, 2:4, bass.ds(s * SLAB, SLAB)], ps[:, 2:4, 0:SLAB]).then_inc(acc_read, 1)

            def q_point(s, h):
                add_b(s + SLABS["q"], 2 * h, y_qk[:, :, :])
                rope(s + 8, q_head[:, h, :, :], s + SLABS["q"])

            def res_point(k, phase, s, h, gate):
                if k == 2:
                    n = s + SLABS[phase]
                    add_b(n, 2 * h, y[:, :, :])
                    ve.wait_ge(acc_read, n + 1)
                    for m in range(2):
                        r_ = res[:, bass.ds(2 * s + m, 1), :]
                        last = nc.vector.scalar_tensor_tensor(out=r_, in0=y[:, m:m + 1, :], scalar=vec[:, bass.ds(2 * s + (gate + m), 1)],
                                                              in1=r_, op0=ALU.mult, op1=ALU.add)
                    last.then_inc(res_made, 1)
                if k == 3:
                    n = s + RES[phase]
                    ve.wait_ge(sq_made, n + 1)
                    if isinstance(s, int) and s == 0:
                        nc.vector.tensor_copy(part_b[:, :, :], part_c[:, :, :]).then_inc(sq_added, 1)
                    else:
                        ve.wait_ge(sq_added, n)
                        nc.vector.tensor_tensor(part_b[:, :, :], part_b[:, :, :], part_c[:, :, :], ALU.add).then_inc(sq_added, 1)

            def norm_tail(n_norm):
                ve.wait_ge(sq_used, n_norm + 1)
                nc.vector.tensor_scalar(part_c[:, 1, :], ps[:, 7, 0:T], 1.0 / D, EPS, ALU.mult, ALU.add).then_inc(var_made, 1)
                ve.wait_ge(var_made, n_norm + 1)
                nc.vector.reciprocal(part_c[:, 0, :], part_c[:, 1, :]).then_inc(inv_made, 1)
                ve.wait_ge(rstd_made, n_norm + 1)
                parts = (part_a, part_b)
                rstd = part_c[:, 1:2, :].broadcast_to([P, 2, T])

                def scaled(n, b):
                    nc.vector.tensor_tensor(parts[b][:, :, :], res[:, bass.ds(2 * n, 2), :], rstd, ALU.mult).then_inc(xm_made, 1)

                def low(n, b):
                    ve.wait_ge(xh_hi, n + (8 * n_norm + 1))
                    nc.vector.tensor_tensor(xs[:, bass.ds(2 * n, 2), T:2 * T], parts[b][:, :, :], xs[:, bass.ds(2 * n, 2), 0:T],
                                            ALU.subtract).then_inc(xs_ready, 1)
                scaled(0, 0)
                scaled(1, 1)
                with ve.Fori(0, 3) as i:
                    for b in range(2):
                        low(2 * i + b, b)
                        ve.wait_ge(xs_ready, 2 * i + (8 * n_norm + 16 + b + 1))
                        scaled(2 * i + (b + 2), b)
                low(6, 0)
                low(7, 1)

            def taps(phase, j, which, part):
                n = j + TAPS[phase] if phase == "sin" else 2 * j + (TAPS[phase] + which)
                ve.wait_ge(taps_mid, n + 1)
                for m in range(2):
                    last = nc.vector.scalar_tensor_tensor(out=part[:, m, 1:T], in0=y[:, m, 0:T - 1],
                                                          scalar=vec[:, bass.ds(2 * j + tap_column(phase, which, m, 0), 1)],
                                                          in1=part[:, m, 1:T], op0=ALU.mult, op1=ALU.add)
                last.then_inc(taps_first, 1)
                ve.wait_ge(taps_first, n + 1)
                for m in range(2):
                    last = nc.vector.scalar_tensor_tensor(out=part[:, m, 0:T - 1], in0=y[:, m, 1:T],
                                                          scalar=vec[:, bass.ds(2 * j + tap_column(phase, which, m, 2), 1)],
                                                          in1=part[:, m, 0:T - 1], op0=ALU.mult, op1=ALU.add)
                last.then_inc(taps_done, 1)

            def g_point(k, phase, j, h):
                if k == 2:
                    add_b(2 * j + SLABS[phase], 2 * h, y[:, :, :])
                if k == 3:
                    taps(phase, j, 0, part_a)

            def v_up_point(k, phase, j, h):
                if k == 2:
                    add_b(2 * j + (SLABS[phase] + 1), 2 * h, y[:, :, :])
                if k == 3:
                    taps(phase, j, 1, part_b)

            def gate_pair(phase, j):
                n = j + PAIRS[phase]
                ve.wait_ge(silu_made, n + 1)
                ve.wait_ge(taps_done, 2 * j + (TAPS[phase] + 2))
                nc.vector.tensor_tensor(part_a[:, :, :], part_a[:, :, :], part_b[:, :, :], ALU.mult).then_inc(gated, 1)

            def low_pair(phase, j):
                ve.wait_ge(act_hi_made, j + (PAIRS[phase] + 1))
                nc.vector.tensor_tensor(act[:, bass.ds(2 * j, 2), T:2 * T], part_a[:, :, :], act[:, bass.ds(2 * j, 2), 0:T],
                                        ALU.subtract).then_inc(act_made, 1)

            def k_pair(i):
                for h in range(2):
                    for k in range(4):
                        if not first(i, 0):
                            lo(2 * i + h, k)
                            k_point(k, 2 * i + (h - 1), 1 - h)
                        elif h == 0:
                            lo(1, k)
                            if k in (1, 3):
                                k_point(2 + k // 2, 0, 0)
                        if not first(i, h):
                            ada_in_pair("k", i, h, k)
            pair_loop(ve, k_pair)

            def v_pair(i):
                for h in range(2):
                    for k in range(4):
                        lo(2 * i + (UNITS["v"] // 4 + h), k)
                        if first(i, h):
                            k_point(k, 7, 1)
                        else:
                            v_point(k, 2 * i + (h - 1), 1 - h)
                        ada_in_pair("v", i, h, k)
            loop(ve, 4, v_pair)

            def row_max(h, t):
                n = 2 * h + t
                ve.wait_ge(scores_made, 2 * n + 2)
                nc.vector.reduce_max(s_max[:, :], ps[:, 4:6, :], AX_X).then_inc(max_made, 1)
                ve.wait_ge(max_made, n + 1)
                nc.vector.tensor_scalar(s_neg[:, :], s_max[:, :], -SCALE, None, ALU.mult).then_inc(neg_made, 1)

            def combine(h, t):
                n = 2 * h + t
                ve.wait_ge(exp_done, 2 * n + 2)
                nc.vector.reciprocal(s_inv[:, :], s_sum[:, :]).then_inc(sum_inv, 1)
                ve.wait_ge(sum_inv, n + 1)
                nc.vector.tensor_scalar(s_lam[:, :], s_inv[:, 1:2], neg_lam[:, 0:1], None, ALU.mult).then_inc(lam_scaled, 1)
                ve.wait_ge(lam_scaled, n + 1)
                nc.vector.tensor_scalar(probs[:, 1, :], probs[:, 1, :], s_lam[:, 0:1], None, ALU.mult).then_inc(p1_scaled, 1)
                ve.wait_ge(p1_scaled, n + 1)
                nc.vector.scalar_tensor_tensor(out=probs[:, 0, :], in0=probs[:, 0, :], scalar=s_inv[:, 0:1],
                                               in1=probs[:, 1, :], op0=ALU.mult, op1=ALU.add).then_inc(a_made, 1)

            def keep_o(h, t, parity):
                ve.wait_ge(o_made, 2 * h + (t + 1))
                if t == 0:
                    wait(ve, o_turned, h - 1)
                nc.vector.tensor_copy(o_rows[:, parity, t, :], ps[:, 7, 0:T]).then_inc(o_copied, 1)

            def invert(h):
                ve.wait_ge(o_squared, 2 * h + 2)
                v = o_sum[:, :, bass.ds(h, 1)]
                nc.vector.tensor_scalar(v, v, 1.0 / T, EPS, ALU.mult, ALU.add).then_inc(o_var, 1)
                ve.wait_ge(o_var, h + 1)
                nc.vector.reciprocal(o_inv[:, :, bass.ds(h, 1)], v).then_inc(o_inverted, 1)

            def scale_o(h, parity):
                ve.wait_ge(o_root, h + 1)
                ve.wait_ge(o_copied, 2 * h + 2)
                for t in range(2):
                    o = o_rows[:, parity, t, :]
                    last = nc.vector.tensor_scalar(o, o, o_rstd[:, t, bass.ds(h, 1)], None, ALU.mult)
                last.then_inc(o_normed, 1)

            def low_o(h):
                ve.wait_ge(o_hi, h + 1)
                nc.vector.tensor_tensor(heads_out[:, bass.ds(2 * h, 2), T:2 * T], o_feat[:, :, :], heads_out[:, bass.ds(2 * h, 2), 0:T],
                                        ALU.subtract).then_inc(xs_ready, 1)

            def attention_point(k, h, parity):
                at = lambda m: not isinstance(h, int) or 0 <= h + m < HEADS
                if k == 0:
                    if at(-2):
                        invert(h + (-2))
                    if at(0):
                        row_max(h, 0)
                        combine(h, 0)
                if k == 1 and at(-2):
                    scale_o(h + (-2), parity)
                if k == 2:
                    if at(-1):
                        keep_o(h + (-1), 1, 1 - parity)
                    if at(0):
                        row_max(h, 1)
                        combine(h, 1)
                if k == 3:
                    if at(0):
                        keep_o(h, 0, parity)
                    if at(-2):
                        low_o(h + (-2))

            def q_pair(i):
                for h in range(2):
                    for k in range(4):
                        lo(2 * i + (UNITS["q"] // 4 + h), k)
                        if first(i, h):
                            v_point(k, 7, 1)
                            ada_chunk(15, 2 * k, ada_sum, 2)
                            ada_chunk(15, 2 * k + 1, ada_sum, 2)
                            if k == 3:
                                ada_add(14)
                        elif k == 2:
                            q_point(2 * i + (h - 1), 1 - h)
                        if first(i, h - 1) and k == 3:
                            ada_add(15)
                        attention_point(k, 2 * i + (h - 2), h)
            ve.wait_ge(lam_made, 1)
            pair_loop(ve, q_pair)

            o_lo_unit = lambda n: lo(UNITS["o"] // 4 + n // 4, n % 4)
            for k in range(4):
                o_lo_unit(k)
                if k == 2:
                    q_point(7, 1)
                attention_point(k, 6, 0)
            attention_point(0, 7, 1)
            attention_point(1, 7, 1)
            o_lo_unit(4)
            attention_point(2, 7, 1)
            attention_point(3, 7, 1)
            o_lo_unit(5)
            attention_point(0, 8, 0)
            attention_point(1, 8, 0)
            attention_point(2, 8, 0)
            o_lo_unit(6)
            attention_point(3, 8, 0)
            attention_point(0, 9, 1)
            attention_point(1, 9, 1)
            o_lo_unit(7)
            attention_point(3, 9, 1)
            ve.wait_ge(xt_kept, 8)

            def o_pair(i):
                for h in range(2):
                    for k in range(4):
                        lo(2 * i + (UNITS["o"] // 4 + h), k)
                        if isinstance(i, int) and h == 0 and k < 2:
                            res_point(k + 2, "o", 0, 0, B0 + G1)
                        res_point(k, "o", 2 * i + (h - 1), 1 - h, B0 + G1)
            o_loop(ve, o_pair)

            def up(phase, tail):
                def four(i, ada):
                    for p in range(2):
                        for h in range(2):
                            for k in range(4):
                                lo(4 * i + (UNITS[phase] // 4 + 2 * p + h), k)
                                if first(i, p + h):
                                    tail(k)
                                elif h == 0:
                                    v_up_point(k, phase, 2 * i + (p - 1), 1)
                                else:
                                    if not first(i, p):
                                        if k == 0:
                                            gate_pair(phase, 2 * i + (p - 1))
                                        if k == 1:
                                            low_pair(phase, 2 * i + (p - 1))
                                    g_point(k, phase, 2 * i + p, 0)
                                n = 8 * p + 4 * h + k
                                if ada:
                                    j = i + ADA_AT[phase]
                                    if n < 8:
                                        ada_chunk(j, n)
                                    if n == 13:
                                        ada_add(j)
                up_loop(ve, four)

            def down(phase, up_phase, gate, ada):
                def pair(i):
                    for h in range(2):
                        for k in range(12):
                            lo(6 * i + (UNITS[phase] // 4 + 3 * h + k // 4), k % 4, down_tiles(k)[1])
                            if ada:
                                ada_in_24(phase, i, 12 * h + k)
                            if first(i, h):
                                v_up_point(k, up_phase, FT // 2 - 1, 1)
                                if k == 4:
                                    gate_pair(up_phase, FT // 2 - 1)
                                if k == 5:
                                    low_pair(up_phase, FT // 2 - 1)
                            else:
                                res_point(k, phase, 2 * i + (h - 1), 1 - h, gate)
                loop(ve, 4, pair)

            def o_tail(k):
                res_point(k, "o", 7, 1, B0 + G1)
                if k == 3:
                    norm_tail(0)
            up("up0", o_tail)
            down("dn0", "up0", B0 + G2, True)

            def sin_point(k, j, h, which):
                n = 3 * j + (SLABS["sin"] + which)
                if which == 0 and k == 2:
                    add_b(n, 2 * h, part_a[:, :, :])
                if which == 1:
                    if k == 2:
                        add_b(n, 2 * h, y[:, :, :])
                        ve.wait_ge(acc_read, n + 1)
                        nc.vector.tensor_tensor(y[:, :, :], y[:, :, :], part_a[:, :, :], ALU.mult).then_inc(gx_made, 1)
                    if k == 3:
                        taps("sin", j, 0, part_b)
                if which == 2:
                    if k == 2:
                        add_b(n, 2 * h, part_c[:, :, :])
                        ve.wait_ge(acc_read, n + 1)
                        ve.wait_ge(taps_done, j + (TAPS["sin"] + 1))
                        nc.vector.tensor_tensor(part_c[:, :, :], part_c[:, :, :], part_b[:, :, :], ALU.mult).then_inc(z_mul, 1)
                    if k == 3:
                        ve.wait_ge(z_hi_made, j + 1)
                        nc.vector.tensor_tensor(z[:, bass.ds(2 * j, 2), T:2 * T], part_c[:, :, :], z[:, bass.ds(2 * j, 2), 0:T],
                                                ALU.subtract).then_inc(z_made, 1)

            def sin_six(i):
                for n in range(6):
                    for k in range(4):
                        lo(6 * i + (UNITS["sin"] // 4 + n), k)
                        if first(i, n):
                            res_point(k, "dn0", 7, 1, B0 + G2)
                            if k == 3:
                                norm_tail(1)
                        elif n % 3 == 0:
                            sin_point(k, 2 * i + (n // 3 - 1), (n - 1) % 2, 2)
                        else:
                            sin_point(k, 2 * i + n // 3, (n - 1) % 2, n % 3 - 1)
                        ada_in_24("sin", i, 4 * n + k)
            loop(ve, 4, sin_six)

            def so_pair(i):
                for h in range(2):
                    for k in range(4):
                        lo(2 * i + (UNITS["so"] // 4 + h), k)
                        if first(i, h):
                            sin_point(k, 7, 1, 2)
                        else:
                            res_point(k, "so", 2 * i + (h - 1), 1 - h, B1 + G1)
            loop(ve, 4, so_pair)

            def so_tail(k):
                res_point(k, "so", 7, 1, B1 + G1)
                if k == 3:
                    norm_tail(2)
            up("up1", so_tail)
            down("dn1", "up1", B1 + G2, False)
            for k in range(4):
                res_point(k, "dn1", 7, 1, B1 + G2)
            ve.wait_ge(sq_used, 4)
            for t in range(2):
                last = nc.vector.tensor_scalar(row_var[:, t:t + 1], ps[:, 6 + t, 0:1], 1.0 / D, EPS, ALU.mult, ALU.add)
            last.then_inc(rows_var, 1)
            ve.wait_ge(rows_var, 2)
            nc.vector.reciprocal(row_inv[:, 0:2], row_var[:, 0:2]).then_inc(rows_inv, 1)
            ve.wait_ge(fin_kept, 8)
            ve.wait_ge(rows_rstd, 2)
            nc.vector.tensor_scalar(out_tok[:, 0, :], out_tok[:, 0, :], row_rstd[:, 0:1], None, ALU.mult).then_inc(fin_scaled[0], 1)

        @block.tensor
        def _(pe):
            mm = nc.tensor.matmul
            pe.wait_ge(ident_loaded, 16)
            pe.wait_ge(vecs_loaded, 16 * 19)
            for tile, n in enumerate((128, 118, 104, 104, 104, 88, 88, 88)):
                last = nc.tensor.transpose(ps[:, tile // 4, 128 * (tile % 4):128 * (tile % 4) + n], vec_rows[0:n, tile, :], ident[0:n, 0:n])
            last.then_inc(vecs_turned, 1)
            pe.wait_ge(ones_made, 1)
            pe.wait_ge(lam_multiplied, 1)
            mm(ps[:, 3, 0:2], ones[:, :], lam_prod[:, :], start=True, stop=True).then_inc(lam_summed, 1)

            pe.wait_ge(cond_made, 1)

            def mod_products(b, n):
                wait(pe, mod_copied, n // 8 - 1)
                for q in range(8):
                    pe.wait_ge(start_full[q % 4], 16 * (n // 4 + q // 4 + 1))
                    for t in range(2):
                        last = mm(ps[0:2, 6 + b, :], cond[:, :, 2 * q + t], start_ring[:, q % 4, t, :],
                                  start=(q == 0 and t == 0), stop=(q == 7 and t == 1))
                    last.then_inc(start_used, 1)

            def mod_turn(b, n):
                pe.wait_ge(mod_copied, n + 1)
                wait(pe, mod_made, 2 * n - 2)
                for t in range(4):
                    last = nc.tensor.transpose(ps[:, 4 + b, 2 * t:2 * t + 2], mod_rows[:, b, P * t:P * t + P], ident[0:2, 0:2])
                last.then_inc(mod_turned, 1)

            def turn_tokens(n, tok):
                pe.wait_ge(rows_normed, 2 * n + 2)
                for i in range(8):
                    if n == 0:
                        wait(pe, xn_kept, i - 1)
                    elif i < 2:
                        pe.wait_ge(xn_kept, 7 + i)
                    else:
                        pe.wait_ge(ctx_kept, i - 1)
                    for k in range(2):
                        for t in range(2):
                            last = nc.tensor.transpose(ps[:, i % 2, T * k + P * t:T * k + P * t + P],
                                                       tok[:, t, P * (2 * i + k):P * (2 * i + k) + P], ident[:, :])
                    last.then_inc(xn_turned, 1)

            mod_products(0, 0)
            pe.wait_ge(vecs_made, 1)
            turn_tokens(0, x_tok)
            mod_turn(0, 0)
            mod_products(1, 8)
            mod_turn(1, 1)
            turn_tokens(1, ctx_tok)

            def k_unit(i, h, k):
                if first(i, h):
                    pe.wait_ge(xs_ready, 2 * k + 1)
                pe.wait_ge(lo_made, 8 * i + (4 * h + k + 1))
                for src, bank in ((xs, 4 * h), (cs, 2)):
                    if src is cs and first(i, h):
                        pe.wait_ge(xs_ready, 2 * k + 2)
                    if src is cs and k == 0:
                        wait(pe, ctx_read, 2 * i + h)
                    for t in range(4):
                        for m in range(2):
                            cols = slice(P * m, P * m + P)
                            mm(ps[:, bank + m, :], w_hi[:, k, t, cols], src[:, 4 * k + t, :], start=(k == 0 and t == 0), stop=False)
                            last = mm(ps[:, bank + m, 0:T], w_lo[:, k, t, cols], src[:, 4 * k + t, 0:T], start=False, stop=(k == 3 and t == 3))
                last.then_inc(w_used, 1)

            for g in range(1, 4):
                mod_products(1, 8 * (g + 1))
                pe.wait_ge(start_step, 32 * g)
                pe.wait_ge(mod_made, 2 * g)
                for m in range(2):
                    for t in range(4):
                        last = mm(ps[:, 4, 4 * m + t:4 * m + t + 1], start_sum[:, m, P * t:P * t + P], ones[:, 0:1], start=True, stop=True)
                last.then_inc(start_reduced, 1)
                mod_turn(1, g + 1)
                k_unit(0, 0, g - 1)
            k_unit(0, 0, 3)

            def unit(quad, slot, bank, src, tile, n_tiles, is_first, is_last):
                pe.wait_ge(lo_made, 4 * quad + (slot + 1))
                for t in range(n_tiles):
                    for m in range(2):
                        cols = slice(P * m, P * m + P)
                        mm(ps[:, bank + m, :], w_hi[:, slot, t, cols], src[:, tile + t, :],
                           start=(is_first and t == 0), stop=False)
                        last = mm(ps[:, bank + m, 0:T], w_lo[:, slot, t, cols], src[:, tile + t, 0:T],
                                  start=False, stop=(is_last and t == n_tiles - 1))
                last.then_inc(w_used, 1)

            def ada_reduce(j, sums=ada_sum):
                pe.wait_ge(ada_step, 16 * j + 16)
                wait(pe, ada_added, j)
                for t in range(4):
                    last = mm(ps[:, 6, t:t + 1], sums[:, P * t:P * t + P], ones[:, 0:1], start=True, stop=True)
                last.then_inc(ada_reduced, 1)

            def ada_in_pair(phase, i, h, k):
                if k == 0 and not (phase == "k" and first(i, 0)):
                    ada_reduce(2 * i + (ADA_AT[phase] + h - 1), (ada_sum_b, ada_sum)[h])

            def sum_squares(n_norm):
                pe.wait_ge(sq_added, 8 * (n_norm + 1))
                for m in range(2):
                    last = mm(ps[:, 7, 0:T], ones[:, :], part_b[:, m, :], start=(m == 0), stop=(m == 1))
                last.then_inc(sq_used, 1)

            def k_pair(i):
                for h in range(2):
                    if first(i, h):
                        continue
                    if first(i, h - 1):
                        pe.wait_ge(mod_made, 8)
                    wait(pe, acc_read, 2 * i + (h - 1))
                    for k in range(4):
                        k_unit(i, h, k)
                        ada_in_pair("k", i, h, k)
            pair_loop(pe, k_pair)

            def v_pair(i):
                for h in range(2):
                    if first(i, h):
                        pe.wait_ge(acc_read, SLABS["v"] - 1)
                        pe.wait_ge(ctx_read, SLABS["v"])
                    for k in range(4):
                        pe.wait_ge(lo_made, 8 * i + (UNITS["v"] + 4 * h + k + 1))
                        for src, bank in ((xs, 4 * h), (cs, 2)):
                            if src is cs and k == 0 and not first(i, h):
                                pe.wait_ge(acc_read, 2 * i + (SLABS["v"] + h))
                            for t in range(4):
                                for n in range(2):
                                    x_hi = src[:, 4 * k + t, P * n:P * n + P]
                                    x_lo = src[:, 4 * k + t, T + P * n:T + P * n + P]
                                    mm(ps[:, bank + n, 0:SLAB], x_hi, w_hi[:, k, t, :], start=(k == 0 and t == 0), stop=False)
                                    mm(ps[:, bank + n, 0:SLAB], x_hi, w_lo[:, k, t, :], start=False, stop=False)
                                    last = mm(ps[:, bank + n, 0:SLAB], x_lo, w_hi[:, k, t, :], start=False, stop=(k == 3 and t == 3))
                        last.then_inc(w_used, 1)
                        ada_in_pair("v", i, h, k)
            loop(pe, 4, v_pair)

            def scores(h, t, parity):
                n = 2 * h + t
                if t == 0:
                    pe.wait_ge(rope_done, h + 9)
                wait(pe, exp_done, 2 * n)
                for b in range(2):
                    mm(ps[:, 4 + b, :], q_head[:, parity, b, P * t:P * t + P], k_t[:, bass.ds(2 * h + b, 1), :],
                       start=True, stop=True).then_inc(scores_made, 1)

            def turn_a(h, t):
                n = 2 * h + t
                pe.wait_ge(a_made, n + 1)
                wait(pe, at_copied, n)
                for k in range(4):
                    last = nc.tensor.transpose(ps[:, 6, P * k:P * k + P], probs[:, 0, P * k:P * k + P], ident[:, :])
                last.then_inc(at_made, 1)

            def weigh(h, t):
                n = 2 * h + t
                pe.wait_ge(at_copied, n + 1)
                wait(pe, o_copied, n)
                for k in range(4):
                    last = mm(ps[:, 7, 0:T], a_t[:, t, P * k:P * k + P], v_rows[:, k, bass.ds(T * h, T)],
                              start=(k == 0), stop=(k == 3))
                last.then_inc(o_made, 1)

            def turn_o(h, parity):
                pe.wait_ge(o_normed, h + 1)
                for m in range(2):
                    for t in range(2):
                        last = nc.tensor.transpose(ps[:, 6, T * m + P * t:T * m + P * t + P],
                                                   o_rows[:, parity, t, P * m:P * m + P], ident[:, :])
                last.then_inc(o_turned, 1)

            def attention_point(k, h, parity):
                at = lambda m: not isinstance(h, int) or 0 <= h + m < HEADS
                if k == 0 and at(0):
                    if isinstance(h, int) and h == 0:
                        pe.wait_ge(ada_added, 16)
                    turn_a(h, 0)
                    scores(h, 1, parity)
                if k == 1:
                    if at(0):
                        weigh(h, 0)
                    if at(-2):
                        turn_o(h + (-2), parity)
                if k == 2:
                    if at(0):
                        wait(pe, o_gained, h - 1)
                        turn_a(h, 1)
                    if at(1):
                        scores(h + 1, 0, 1 - parity)
                if k == 3 and at(0):
                    weigh(h, 1)

            def q_pair(i):
                for h in range(2):
                    if first(i, h):
                        pe.wait_ge(acc_read, SLABS["q"] - 1)
                    elif first(i, h - 1):
                        pe.wait_ge(acc_read, SLABS["q"])
                    else:
                        pe.wait_ge(acc_read, 2 * i + (SLABS["q"] + h - 1))
                    for k in range(4):
                        unit(2 * i + (UNITS["q"] // 4 + h), k, 2 * h, xs, 4 * k, 4, k == 0, k == 3)
                        if first(i, 0) and k == 0:
                            ada_reduce(14 + h, (ada_sum_b, ada_sum)[h])
                        attention_point(k, 2 * i + (h - 2), h)
            pair_loop(pe, q_pair)

            def turn_x(*parts):
                pe.wait_ge(xt_loaded, 16)
                for n in parts:
                    wait(pe, xt_kept, n - 1)
                    for k in range(2):
                        for t in range(2):
                            last = nc.tensor.transpose(ps[:, 4 + n % 2, T * k + P * t:T * k + P * t + P],
                                                       x_again[:, t, P * (2 * n + k):P * (2 * n + k) + P], ident[:, :])
                    last.then_inc(xt_turned, 1)

            def o_unit(n):
                slab, k = O_FIRST[n]
                pe.wait_ge(xs_ready, 8 + 2 * (k + 1))
                if k == 0:
                    pe.wait_ge(acc_read, SLABS["o"] - 1 + slab)
                unit(UNITS["o"] // 4 + n // 4, n % 4, 2 * slab, heads_out, 4 * k, 4, k == 0, k == 3)

            attention_point(0, 6, 0)
            o_unit(0)
            attention_point(1, 6, 0)
            attention_point(2, 6, 0)
            o_unit(1)
            attention_point(3, 6, 0)
            attention_point(0, 7, 1)
            o_unit(2)
            attention_point(1, 7, 1)
            o_unit(3)
            attention_point(2, 7, 1)
            turn_x(0, 1)
            attention_point(3, 7, 1)
            attention_point(1, 8, 0)
            o_unit(4)
            pe.wait_ge(o_gained, 7)
            attention_point(1, 9, 1)
            turn_x(2, 3)
            o_unit(5)
            turn_x(4, 5)
            o_unit(6)
            turn_x(6, 7)
            o_unit(7)

            def narrow(phase, i, src, ready):
                for h in range(2):
                    if first(i, h - 1):
                        pe.wait_ge(acc_read, SLABS[phase])
                    elif not first(i, h):
                        pe.wait_ge(acc_read, 2 * i + (SLABS[phase] + h - 1))
                    for k in range(4):
                        if first(i, h):
                            ready(k)
                        unit(2 * i + (UNITS[phase] // 4 + h), k, 2 * h, src, 4 * k, 4, k == 0, k == 3)
            o_loop(pe, lambda i: narrow("o", i, heads_out, None))

            def up(phase, n_ready, n_norm):
                sum_squares(n_norm)

                def four(i, ada):
                    for p in range(2):
                        for h in range(2):
                            g = 2 * p + h
                            if first(i, g) or first(i, g - 1):
                                pe.wait_ge(acc_read, SLABS[phase])
                            else:
                                pe.wait_ge(acc_read, 4 * i + (SLABS[phase] + g - 1))
                            for k in range(4):
                                if first(i, g):
                                    pe.wait_ge(xs_ready, n_ready + 2 * (k + 1))
                                unit(4 * i + (UNITS[phase] // 4 + g), k, 2 * h, xs, 4 * k, 4, k == 0, k == 3)
                                if ada and 4 * g + k == 9:
                                    ada_reduce(i + ADA_AT[phase])
                up_loop(pe, four)

            def turn_rows(s, h):
                pe.wait_ge(fin_gained, s + 1)
                wait(pe, fin_kept, s - 1)
                for t in range(2):
                    for m in range(2):
                        last = nc.tensor.transpose(ps[:, 4 + h, T * t + P * m:T * t + P * m + P], part_a[:, m, P * t:P * t + P], ident[:, :])
                last.then_inc(fin_turned, 1)

            def down(phase, ada):
                def pair(i):
                    for h in range(2):
                        if first(i, h) or first(i, h - 1):
                            pe.wait_ge(acc_read, SLABS[phase] + h - 1)
                        else:
                            pe.wait_ge(acc_read, 2 * i + (SLABS[phase] + h - 1))
                        for k in range(12):
                            tile, n = down_tiles(k)
                            if first(i, h) and k in (0, 11):
                                pe.wait_ge(act_made, PAIRS_END[phase] - (1 if k == 0 else 0))
                            unit(6 * i + (UNITS[phase] // 4 + 3 * h + k // 4), k % 4, 2 * h, act, tile, n, k == 0, k == 11)
                            if phase == "dn1" and k == 4 and not first(i, h):
                                turn_rows(2 * i + (h - 1), 1 - h)
                            if ada and 12 * h + k == 8:
                                ada_reduce(2 * i + ADA_AT[phase])
                            if ada and 12 * h + k == 20:
                                ada_reduce(2 * i + (ADA_AT[phase] + 1))
                loop(pe, 4, pair)

            up("up0", 16, 0)
            down("dn0", True)
            sum_squares(1)

            def sin_six(i):
                for n in range(6):
                    if first(i, n) or first(i, n - 1):
                        pe.wait_ge(acc_read, SLABS["sin"])
                    else:
                        pe.wait_ge(acc_read, 6 * i + (SLABS["sin"] + n - 1))
                    for k in range(4):
                        if first(i, n):
                            pe.wait_ge(xs_ready, 24 + 2 * (k + 1))
                        unit(6 * i + (UNITS["sin"] // 4 + n), k, 2 * (n % 2), xs, 4 * k, 4, k == 0, k == 3)
                        if 4 * n + k == 8:
                            ada_reduce(2 * i + ADA_AT["sin"])
                        if 4 * n + k == 20:
                            ada_reduce(2 * i + (ADA_AT["sin"] + 1))
            loop(pe, 4, sin_six)

            def z_ready(k):
                pe.wait_ge(z_made, 8 if k == 3 else 7)
                if k == 0:
                    pe.wait_ge(acc_read, SLABS["so"] - 1)
            loop(pe, 4, lambda i: narrow("so", i, z, z_ready))

            up("up1", 32, 2)
            down("dn1", False)
            pe.wait_ge(sq_added, 32)
            for t in range(2):
                for m in range(2):
                    last = mm(ps[:, 6 + t, 0:1], part_b[:, m, P * t:P * t + P], ones[:, 0:1], start=(m == 0), stop=(m == 1))
            last.then_inc(sq_used, 1)
            turn_rows(7, 1)


RES = {"o": 0, "dn0": 8, "so": 16, "dn1": 24}
TAPS = {"up0": 0, "sin": 44, "up1": 52}
PAIRS = {"up0": 0, "up1": 22}
PAIRS_END = {"dn0": 22, "dn1": 44}


def tap_column(phase, which, m, tap):
    if phase == "sin":
        return SCONV + KT * tap + m
    return CONV[0 if phase == "up0" else 1] + 2 * FT * tap + FT * which + m


_INS = ["x", "c", "ctx", "c_ctx", "w_ada", "b_ada", "attn_w_qkv", "attn_w_o", "attn_lambda_q1", "attn_lambda_k1",
        "attn_lambda_q2", "attn_lambda_k2", "attn_subln_gain", "sconv_w_in", "sconv_conv", "sconv_w_out",
        "ffn_w_up", "ffn_conv", "ffn_w_down", "final_gain"]


def _rope_tables(np):
    half = HEAD_DIM // 2
    inv = (1.0 / (np.float32(10000.0) ** (np.arange(0, half, 2, dtype=np.float32) / np.float32(half)))).astype(np.float32)
    row = np.repeat(np.arange(T // GRID_W, dtype=np.float32), GRID_W)
    col = np.tile(np.arange(GRID_W, dtype=np.float32), T // GRID_W)
    ang_r, ang_c = inv[:, None] * row[None, :], inv[:, None] * col[None, :]
    ang = np.concatenate([ang_r, ang_r, ang_c, ang_c], axis=0)
    sign = np.repeat(np.array([-1, 1, -1, 1], np.float32), 32)[:, None]
    return np.cos(ang).astype(np.float32), (sign * np.sin(ang)).astype(np.float32)


def kernel(**inputs):
    import numpy as _np
    import concourse.bacc as _bacc
    from concourse import mybir as _mybir
    from concourse.bass_utils import run_bass_kernel_spmd as _run

    nc = _bacc.Bacc("TRN2", target_bir_lowering=False, num_devices=1)
    arrays, args = {}, []

    def give(name, a):
        arrays[f"in_{name}_dram"] = a
        args.append(nc.dram_tensor(f"in_{name}_dram", a.shape, _mybir.dt.from_np(a.dtype), kind="ExternalInput").ap())

    for name in _INS:
        give(name, _np.ascontiguousarray(inputs[name]))
    cos, sin = _rope_tables(_np)
    give("ident", _np.eye(P, dtype=_np.float32))
    give("rope_cos", cos)
    give("rope_sin", sin)
    o = nc.dram_tensor("out_0_dram", (1, T, D), _mybir.dt.float32, kind="ExternalOutput").ap()
    program(nc, *args, o)
    r = _run(nc, [arrays], core_ids=[0])
    return r.results[0]["out_0_dram"]
```
